# Optimizing a Trainium2 kernel written in Bass

```python
import jax, jax.numpy as jnp
from jax import lax
import numpy as np
import math

D_MODEL = 1024
BATCH = 1
SEQ = 256
DEPTH = 2

N_A = DEPTH // 2
N_B = DEPTH - N_A
N_META = 16
A_EXPAND = 128
A_HEADS = D_MODEL // A_EXPAND
A_DV = D_MODEL // A_HEADS
A_CHUNK = 64
B_HEADS = 16
B_HDIM = D_MODEL // B_HEADS
Q_BLOCK = 128
FG_BIAS_INIT = 2.0
D_FF = ((8 * D_MODEL // 3 + 63) // 64) * 64
CONV_W = 3
EPS = 1e-6


def rmsnorm(x, g):
    xf = x.astype(jnp.float32)
    y = xf * lax.rsqrt(jnp.mean(xf * xf, axis=-1, keepdims=True) + EPS)
    return (y * g.astype(jnp.float32)).astype(x.dtype)

def causal_dwconv(u, w):
    C = u.shape[-1]
    return lax.conv_general_dilated(
        u, w[:, None, :].astype(u.dtype), window_strides=(1,),
        padding=[(CONV_W - 1, 0)], dimension_numbers=("NWC", "WIO", "NWC"),
        feature_group_count=C)

def conv_ffn(x, w_up, conv_w, w_down):
    u = causal_dwconv(x @ w_up, conv_w)
    gate, val = jnp.split(u, 2, axis=-1)
    return (jax.nn.silu(gate) * val) @ w_down

def gla_chunks(q, k, v, logf, s0):
    b = jnp.cumsum(logf, axis=3)
    b_last = b[..., -1:, :]
    q_in = q * jnp.exp(b)
    k_in = k * jnp.exp(-b)
    k_out = k * jnp.exp(b_last - b)
    C = q.shape[3]
    causal = jnp.tril(jnp.ones((C, C), dtype=bool))
    attn = jnp.where(causal, jnp.einsum("bhnck,bhnsk->bhncs", q_in, k_in), 0.0)
    o_intra = jnp.einsum("bhncs,bhnsv->bhncv", attn, v)
    dS = jnp.einsum("bhnck,bhncv->bhnkv", k_out, v)
    decay = jnp.exp(b_last[..., 0, :])

    def step(S, inp):
        d, ds = inp
        return d[..., :, None] * S + ds, S

    S_fin, S_in = lax.scan(step, s0, (jnp.moveaxis(decay, 2, 0), jnp.moveaxis(dS, 2, 0)))
    S_in = jnp.moveaxis(S_in, 0, 2)
    o_inter = jnp.einsum("bhnck,bhnkv->bhncv", q_in, S_in)
    return o_intra + o_inter, S_fin

def hgrn2_mixer(x, w_in, lb, head_gain, w_out):
    Bsz, T, _ = x.shape
    q, f_pre, i, g = jnp.split(x @ w_in, 4, axis=-1)
    f = lb + (1.0 - lb) * jax.nn.sigmoid(f_pre.astype(jnp.float32))
    logf = jnp.log(f)
    k = 1.0 - f

    def heads(t):
        return t.astype(jnp.float32).reshape(Bsz, T, A_HEADS, -1).transpose(0, 2, 1, 3)

    qh, kh, vh, lh = heads(q), heads(k), heads(i), heads(logf)

    def meta_part(t):
        return t[:, :, :N_META][:, :, None]

    def real_part(t):
        return t[:, :, N_META:].reshape(Bsz, A_HEADS, -1, A_CHUNK, t.shape[-1])

    s0 = jnp.zeros((Bsz, A_HEADS, A_EXPAND, A_DV), jnp.float32)
    o_meta, s_meta = gla_chunks(meta_part(qh), meta_part(kh), meta_part(vh), meta_part(lh), s0)
    o_real, _ = gla_chunks(real_part(qh), real_part(kh), real_part(vh), real_part(lh), s_meta)
    o = jnp.concatenate([o_meta.reshape(Bsz, A_HEADS, N_META, A_DV),
                         o_real.reshape(Bsz, A_HEADS, T - N_META, A_DV)], axis=2)
    o = o.transpose(0, 2, 1, 3)
    o = o * lax.rsqrt(jnp.mean(o * o, axis=-1, keepdims=True) + EPS)
    o = o * head_gain.astype(jnp.float32).reshape(A_HEADS, A_DV)
    o = o.reshape(Bsz, T, D_MODEL).astype(x.dtype) * jax.nn.silu(g)
    return o @ w_out

def shared_kv(h, kv_norm, kv_w, fg_b):
    Bsz, T, _ = h.shape
    proj = rmsnorm(h, kv_norm) @ kv_w
    k = proj[..., :D_MODEL].reshape(Bsz, T, B_HEADS, B_HDIM).transpose(0, 2, 1, 3)
    v = proj[..., D_MODEL:2 * D_MODEL].reshape(Bsz, T, B_HEADS, B_HDIM).transpose(0, 2, 1, 3)
    zf = proj[..., 2 * D_MODEL:].astype(jnp.float32) + fg_b.astype(jnp.float32)
    c = jnp.cumsum(jax.nn.log_sigmoid(zf), axis=1).transpose(0, 2, 1)
    return k, v, c

def fox_mixer(x, w_q, w_out, k, v, c):
    Bsz, T, _ = x.shape
    q = (x @ w_q).reshape(Bsz, T, B_HEADS, B_HDIM).transpose(0, 2, 1, 3)
    scale = 1.0 / np.sqrt(B_HDIM).astype(np.float32)
    bounds = [(0, N_META)] + [(N_META + n * Q_BLOCK, N_META + (n + 1) * Q_BLOCK)
                              for n in range((T - N_META) // Q_BLOCK)]
    outs = []
    for s, e in bounds:
        logits = jnp.einsum("bhqd,bhkd->bhqk", q[:, :, s:e], k[:, :, :e]).astype(jnp.float32) * scale
        logits = logits + (c[:, :, s:e, None] - c[:, :, None, :e])
        mask = jnp.arange(s, e)[:, None] >= jnp.arange(e)[None, :]
        p = jax.nn.softmax(jnp.where(mask, logits, -1e30), axis=-1)
        outs.append(jnp.einsum("bhqk,bhkd->bhqd", p.astype(v.dtype), v[:, :, :e]))
    o = jnp.concatenate(outs, axis=2).transpose(0, 2, 1, 3).reshape(Bsz, T, D_MODEL)
    return o @ w_out

def first_inputs(seed: int = 0) -> dict:
    key = jax.random.key(seed)
    ks = jax.random.split(key, 16)
    D = D_MODEL

    def nrm(k, shape, scale):
        return jax.random.normal(k, shape, jnp.float32) * scale

    return {
        "x": nrm(ks[0], (BATCH, SEQ, D), 1.0),
        "meta_tokens": nrm(ks[1], (N_META, D), 1.0),
        "norm_gains": 1.0 + nrm(ks[2], (DEPTH, 4, D), 0.05),
        "a_w_in": nrm(ks[3], (N_A, D, 4 * D), D ** -0.5),
        "a_lb_logits": nrm(ks[4], (N_A + 1, D), 0.1),
        "a_head_norm": 1.0 + nrm(ks[5], (N_A, D), 0.05),
        "a_w_out": nrm(ks[6], (N_A, D, D), D ** -0.5),
        "kv_norm": 1.0 + nrm(ks[7], (D,), 0.05),
        "kv_w": nrm(ks[8], (D, 2 * D + B_HEADS), D ** -0.5),
        "fg_b": FG_BIAS_INIT + nrm(ks[9], (B_HEADS,), 0.1),
        "b_w_q": nrm(ks[10], (N_B, D, D), D ** -0.5),
        "b_w_out": nrm(ks[11], (N_B, D, D), D ** -0.5),
        "ffn_w_up": nrm(ks[12], (DEPTH, D, 2 * D_FF), D ** -0.5),
        "ffn_conv": nrm(ks[13], (DEPTH, CONV_W, 2 * D_FF), CONV_W ** -0.5),
        "ffn_w_down": nrm(ks[14], (DEPTH, D_FF, D), D_FF ** -0.5),
    }

def first_block(x, meta_tokens, norm_gains, a_w_in, a_lb_logits, a_head_norm, a_w_out,
              kv_norm, kv_w, fg_b, b_w_q, b_w_out, ffn_w_up, ffn_conv, ffn_w_down):
    Bsz = x.shape[0]
    meta = jnp.broadcast_to(meta_tokens[None].astype(x.dtype), (Bsz, N_META, D_MODEL))
    h = jnp.concatenate([meta, x], axis=1)
    lb_all = jnp.cumsum(jax.nn.softmax(a_lb_logits.astype(jnp.float32), axis=0), axis=0)
    k_sh = v_sh = c_sh = None
    for l in range(DEPTH):
        g = norm_gains[l]
        hn = rmsnorm(h, g[0])
        if l < N_A:
            mix = hgrn2_mixer(hn, a_w_in[l], lb_all[l], a_head_norm[l], a_w_out[l])
        else:
            if l == N_A:
                k_sh, v_sh, c_sh = shared_kv(h, kv_norm, kv_w, fg_b)
            j = l - N_A
            mix = fox_mixer(hn, b_w_q[j], b_w_out[j], k_sh, v_sh, c_sh)
        h = h + rmsnorm(mix, g[1])
        ff = conv_ffn(rmsnorm(h, g[2]), ffn_w_up[l], ffn_conv[l], ffn_w_down[l])
        h = h + rmsnorm(ff, g[3])
    return h[:, N_META:]


N_MIXERS = 2
N_GDN_LAYERS = (DEPTH + N_MIXERS - 1) // N_MIXERS
N_MLA_LAYERS = DEPTH // N_MIXERS

GDN_HEADS = 8
GDN_HEAD_DIM = 128
GDN_KEY_DIM = GDN_HEADS * GDN_HEAD_DIM
GDN_VALUE_DIM = GDN_HEADS * GDN_HEAD_DIM
GDN_CONV = 4
GDN_CHUNK = 64
GDN_IN = 2 * GDN_KEY_DIM + 2 * GDN_VALUE_DIM + 2 * GDN_HEADS

MLA_HEADS = 8
MLA_NOPE = 128
MLA_ROPE = 64
MLA_V = 128
MLA_Q_RANK = 384
MLA_KV_RANK = 256
MLA_IN = MLA_Q_RANK + MLA_KV_RANK + MLA_ROPE
ROPE_THETA = 10000.0

D_FF_2 = ((8 * D_MODEL + 3 * 256 - 1) // (3 * 256)) * 256
N_MOD = 6


def rmsnorm_2(x, g):
    xf = x.astype(jnp.float32)
    y = xf * lax.rsqrt(jnp.mean(xf * xf, axis=-1, keepdims=True) + EPS)
    return (y * g.astype(jnp.float32)).astype(x.dtype)

def l2norm(x):
    return x * lax.rsqrt(jnp.sum(x * x, axis=-1, keepdims=True) + EPS)

def causal_depthwise_conv(x, w):
    K = w.shape[-1]
    kern = jnp.transpose(w)[:, None, :].astype(x.dtype)
    return lax.conv_general_dilated(
        x, kern, window_strides=(1,), padding=[(K - 1, 0)],
        dimension_numbers=("NWC", "WIO", "NWC"), feature_group_count=x.shape[-1])

def chunk_gated_delta_rule(q, k, v, g, beta):
    B, H, T, Dk = q.shape
    Dv = v.shape[-1]
    C = GDN_CHUNK
    N = T // C
    q = q.reshape(B, H, N, C, Dk)
    k = k.reshape(B, H, N, C, Dk)
    v = v.reshape(B, H, N, C, Dv)
    g_cum = jnp.cumsum(g.reshape(B, H, N, C), axis=-1)
    beta = beta.reshape(B, H, N, C)

    tril = jnp.tril(jnp.ones((C, C), dtype=bool))
    strict = jnp.tril(jnp.ones((C, C), dtype=bool), k=-1)
    diff = g_cum[..., :, None] - g_cum[..., None, :]
    decay = jnp.exp(jnp.where(tril, diff, -jnp.inf))

    kb = k * beta[..., None]
    L = jnp.where(strict, jnp.einsum("bhnid,bhnjd->bhnij", kb, k) * decay, 0.0)
    A = L + jnp.eye(C, dtype=L.dtype)
    u = lax.linalg.triangular_solve(A, v * beta[..., None], left_side=True, lower=True,
                                    unit_diagonal=True)
    w = lax.linalg.triangular_solve(A, kb * jnp.exp(g_cum)[..., None], left_side=True,
                                    lower=True, unit_diagonal=True)
    attn = jnp.einsum("bhnid,bhnjd->bhnij", q, k) * decay
    q_dec = q * jnp.exp(g_cum)[..., None]
    k_dec = k * jnp.exp(g_cum[..., -1:] - g_cum)[..., None]
    g_last = jnp.exp(g_cum[..., -1])

    def step(S, xs):
        q_i, k_i, w_i, u_i, a_i, gl_i = xs
        v_new = u_i - jnp.einsum("bhck,bhkv->bhcv", w_i, S)
        o_i = jnp.einsum("bhck,bhkv->bhcv", q_i, S) + jnp.einsum("bhij,bhjv->bhiv", a_i, v_new)
        S = S * gl_i[..., None, None] + jnp.einsum("bhck,bhcv->bhkv", k_i, v_new)
        return S, o_i

    xs = tuple(jnp.moveaxis(t, 2, 0) for t in (q_dec, k_dec, w, u, attn, g_last))
    S0 = jnp.zeros((B, H, Dk, Dv), dtype=jnp.float32)
    _, o = lax.scan(step, S0, xs)
    return jnp.moveaxis(o, 0, 2).reshape(B, H, T, Dv)

def gdn_mixer(h, w_in, conv_w, a_log, dt_bias, norm_g, w_out):
    B, T, _ = h.shape
    proj = h @ w_in
    qkv = proj[..., :2 * GDN_KEY_DIM + GDN_VALUE_DIM]
    o0 = 2 * GDN_KEY_DIM + GDN_VALUE_DIM
    gate = proj[..., o0:o0 + GDN_VALUE_DIM]
    a_in = proj[..., o0 + GDN_VALUE_DIM:o0 + GDN_VALUE_DIM + GDN_HEADS]
    b_in = proj[..., o0 + GDN_VALUE_DIM + GDN_HEADS:]

    qkv = jax.nn.silu(causal_depthwise_conv(qkv, conv_w)).astype(jnp.float32)
    q = qkv[..., :GDN_KEY_DIM].reshape(B, T, GDN_HEADS, GDN_HEAD_DIM)
    k = qkv[..., GDN_KEY_DIM:2 * GDN_KEY_DIM].reshape(B, T, GDN_HEADS, GDN_HEAD_DIM)
    v = qkv[..., 2 * GDN_KEY_DIM:].reshape(B, T, GDN_HEADS, GDN_HEAD_DIM)
    q = l2norm(q) * (GDN_HEAD_DIM ** -0.5)
    k = l2norm(k)
    beta = jax.nn.sigmoid(b_in.astype(jnp.float32))
    g = -jnp.exp(a_log.astype(jnp.float32)) * jax.nn.softplus(
        a_in.astype(jnp.float32) + dt_bias.astype(jnp.float32))

    to_bhtd = lambda t: jnp.transpose(t, (0, 2, 1, 3))
    o = chunk_gated_delta_rule(to_bhtd(q), to_bhtd(k), to_bhtd(v),
                               jnp.transpose(g, (0, 2, 1)), jnp.transpose(beta, (0, 2, 1)))
    o = jnp.transpose(o, (0, 2, 1, 3)).astype(h.dtype)
    o = rmsnorm_2(o, norm_g) * jax.nn.silu(gate.reshape(B, T, GDN_HEADS, GDN_HEAD_DIM))
    return o.reshape(B, T, GDN_VALUE_DIM) @ w_out

def apply_rope(x, cos, sin):
    half = x.shape[-1] // 2
    x1, x2 = x[..., :half], x[..., half:]
    return jnp.concatenate([x1 * cos - x2 * sin, x2 * cos + x1 * sin], axis=-1)

def causal_mla_attention(q_nope, q_rope, k_nope, k_rope, v):
    B, T, H, _ = q_nope.shape
    nb = T // Q_BLOCK
    scale = (MLA_NOPE + MLA_ROPE) ** -0.5
    qn = jnp.moveaxis(q_nope.reshape(B, nb, Q_BLOCK, H, MLA_NOPE), 1, 0)
    qr = jnp.moveaxis(q_rope.reshape(B, nb, Q_BLOCK, H, MLA_ROPE), 1, 0)
    kpos = jnp.arange(T)

    def block(args):
        qn_b, qr_b, start = args
        s = (jnp.einsum("bqhd,bkhd->bhqk", qn_b, k_nope)
             + jnp.einsum("bqhd,bkd->bhqk", qr_b, k_rope)).astype(jnp.float32) * scale
        qpos = start + jnp.arange(Q_BLOCK)
        s = jnp.where(kpos[None, :] <= qpos[:, None], s, -jnp.inf)
        p = jax.nn.softmax(s, axis=-1).astype(v.dtype)
        return jnp.einsum("bhqk,bkhd->bqhd", p, v)

    o = lax.map(block, (qn, qr, jnp.arange(nb) * Q_BLOCK))
    return jnp.moveaxis(o, 0, 1).reshape(B, T, H, MLA_V)

def mla_mixer(h, cos, sin, w_in, q_norm_g, kv_norm_g, w_uq, w_ukv, w_out):
    B, T, _ = h.shape
    proj = h @ w_in
    c_q = proj[..., :MLA_Q_RANK]
    c_kv = proj[..., MLA_Q_RANK:MLA_Q_RANK + MLA_KV_RANK]
    k_rope = proj[..., MLA_Q_RANK + MLA_KV_RANK:]
    q = (rmsnorm_2(c_q, q_norm_g) @ w_uq).reshape(B, T, MLA_HEADS, MLA_NOPE + MLA_ROPE)
    kv = (rmsnorm_2(c_kv, kv_norm_g) @ w_ukv).reshape(B, T, MLA_HEADS, MLA_NOPE + MLA_V)
    q_nope, q_rope = q[..., :MLA_NOPE], q[..., MLA_NOPE:]
    k_nope, v = kv[..., :MLA_NOPE], kv[..., MLA_NOPE:]
    q_rope = apply_rope(q_rope, cos[:, :, None, :], sin[:, :, None, :])
    k_rope = apply_rope(k_rope, cos, sin)
    o = causal_mla_attention(q_nope, q_rope, k_nope, k_rope, v)
    return o.reshape(B, T, MLA_HEADS * MLA_V) @ w_out

def swiglu(h, w_gate, w_up, w_down):
    return (jax.nn.silu(h @ w_gate) * (h @ w_up)) @ w_down

def second_inputs(seed: int = 0) -> dict:
    key = jax.random.key(seed)
    ks = jax.random.split(key, 24)
    f32 = jnp.float32
    nrm = lambda k, shape, s: jax.random.normal(k, shape, f32) * s
    x = jax.random.normal(ks[0], (BATCH, SEQ, D_MODEL), f32)
    c = jax.random.normal(ks[1], (BATCH, D_MODEL), f32)
    positions = (jnp.arange(SEQ, dtype=jnp.int32)[None, :]
                 + jax.random.randint(ks[2], (BATCH, 1), 0, 1024, dtype=jnp.int32))
    ada_w = nrm(ks[3], (DEPTH, D_MODEL, N_MOD * D_MODEL), 0.5 * D_MODEL ** -0.5)
    ada_b = nrm(ks[4], (DEPTH, N_MOD * D_MODEL), 0.02)
    norm_mix_g = 1.0 + nrm(ks[5], (DEPTH, D_MODEL), 0.05)
    norm_ffn_g = 1.0 + nrm(ks[6], (DEPTH, D_MODEL), 0.05)

    gdn_w_in = nrm(ks[7], (N_GDN_LAYERS, D_MODEL, GDN_IN), D_MODEL ** -0.5)
    gdn_conv_w = nrm(ks[8], (N_GDN_LAYERS, 2 * GDN_KEY_DIM + GDN_VALUE_DIM, GDN_CONV),
                     GDN_CONV ** -0.5)
    gdn_a_log = jnp.log(jax.random.uniform(ks[9], (N_GDN_LAYERS, GDN_HEADS), f32, 1.0, 16.0))
    dt = jnp.exp(jax.random.uniform(ks[10], (N_GDN_LAYERS, GDN_HEADS), f32,
                                    math.log(1e-3), math.log(1e-1)))
    gdn_dt_bias = dt + jnp.log(-jnp.expm1(-dt))
    gdn_norm_g = 1.0 + nrm(ks[11], (N_GDN_LAYERS, GDN_HEAD_DIM), 0.05)
    gdn_w_out = nrm(ks[12], (N_GDN_LAYERS, GDN_VALUE_DIM, D_MODEL), GDN_VALUE_DIM ** -0.5)

    mla_w_in = nrm(ks[13], (N_MLA_LAYERS, D_MODEL, MLA_IN), D_MODEL ** -0.5)
    mla_q_norm_g = 1.0 + nrm(ks[14], (N_MLA_LAYERS, MLA_Q_RANK), 0.05)
    mla_kv_norm_g = 1.0 + nrm(ks[15], (N_MLA_LAYERS, MLA_KV_RANK), 0.05)
    mla_w_uq = nrm(ks[16], (N_MLA_LAYERS, MLA_Q_RANK, MLA_HEADS * (MLA_NOPE + MLA_ROPE)),
                   MLA_Q_RANK ** -0.5)
    mla_w_ukv = nrm(ks[17], (N_MLA_LAYERS, MLA_KV_RANK, MLA_HEADS * (MLA_NOPE + MLA_V)),
                    MLA_KV_RANK ** -0.5)
    mla_w_out = nrm(ks[18], (N_MLA_LAYERS, MLA_HEADS * MLA_V, D_MODEL),
                    (MLA_HEADS * MLA_V) ** -0.5)

    ffn_w_gate = nrm(ks[19], (DEPTH, D_MODEL, D_FF_2), D_MODEL ** -0.5)
    ffn_w_up = nrm(ks[20], (DEPTH, D_MODEL, D_FF_2), D_MODEL ** -0.5)
    ffn_w_down = nrm(ks[21], (DEPTH, D_FF_2, D_MODEL), D_FF_2 ** -0.5)
    final_norm_g = 1.0 + nrm(ks[22], (D_MODEL,), 0.05)
    return {
        "x": x, "c": c, "positions": positions,
        "ada_w": ada_w, "ada_b": ada_b, "norm_mix_g": norm_mix_g, "norm_ffn_g": norm_ffn_g,
        "gdn_w_in": gdn_w_in, "gdn_conv_w": gdn_conv_w, "gdn_a_log": gdn_a_log,
        "gdn_dt_bias": gdn_dt_bias, "gdn_norm_g": gdn_norm_g, "gdn_w_out": gdn_w_out,
        "mla_w_in": mla_w_in, "mla_q_norm_g": mla_q_norm_g, "mla_kv_norm_g": mla_kv_norm_g,
        "mla_w_uq": mla_w_uq, "mla_w_ukv": mla_w_ukv, "mla_w_out": mla_w_out,
        "ffn_w_gate": ffn_w_gate, "ffn_w_up": ffn_w_up, "ffn_w_down": ffn_w_down,
        "final_norm_g": final_norm_g,
    }

def second_block(x, c, positions, ada_w, ada_b, norm_mix_g, norm_ffn_g,
              gdn_w_in, gdn_conv_w, gdn_a_log, gdn_dt_bias, gdn_norm_g, gdn_w_out,
              mla_w_in, mla_q_norm_g, mla_kv_norm_g, mla_w_uq, mla_w_ukv, mla_w_out,
              ffn_w_gate, ffn_w_up, ffn_w_down, final_norm_g):
    inv_freq = ROPE_THETA ** (-jnp.arange(0, MLA_ROPE, 2, dtype=jnp.float32) / MLA_ROPE)
    ang = positions.astype(jnp.float32)[..., None] * inv_freq
    cos = jnp.cos(ang).astype(x.dtype)
    sin = jnp.sin(ang).astype(x.dtype)
    c_act = jax.nn.silu(c)

    for layer in range(DEPTH):
        mod = c_act @ ada_w[layer] + ada_b[layer]
        shift_m, scale_m, gate_m, shift_f, scale_f, gate_f = [
            m[:, None, :] for m in jnp.split(mod, N_MOD, axis=-1)]

        h = rmsnorm_2(x, norm_mix_g[layer]) * (1.0 + scale_m) + shift_m
        j = layer // N_MIXERS
        if layer % N_MIXERS == 0:
            y = gdn_mixer(h, gdn_w_in[j], gdn_conv_w[j], gdn_a_log[j], gdn_dt_bias[j],
                          gdn_norm_g[j], gdn_w_out[j])
        else:
            y = mla_mixer(h, cos, sin, mla_w_in[j], mla_q_norm_g[j], mla_kv_norm_g[j],
                          mla_w_uq[j], mla_w_ukv[j], mla_w_out[j])
        x = x + gate_m * y

        h = rmsnorm_2(x, norm_ffn_g[layer]) * (1.0 + scale_f) + shift_f
        x = x + gate_f * swiglu(h, ffn_w_gate[layer], ffn_w_up[layer], ffn_w_down[layer])

    return rmsnorm_2(x, final_norm_g)


def setup_inputs(seed=0):
    out = dict(first_inputs(seed))
    for name, value in second_inputs(seed + 1).items():
        if name != "x":
            out[name + "_2"] = value
    return out


def reference(
    x, meta_tokens, norm_gains, a_w_in, a_lb_logits, a_head_norm, a_w_out, kv_norm, kv_w, fg_b,
    b_w_q, b_w_out, ffn_w_up, ffn_conv, ffn_w_down, c_2, positions_2, ada_w_2, ada_b_2,
    norm_mix_g_2, norm_ffn_g_2, gdn_w_in_2, gdn_conv_w_2, gdn_a_log_2, gdn_dt_bias_2,
    gdn_norm_g_2, gdn_w_out_2, mla_w_in_2, mla_q_norm_g_2, mla_kv_norm_g_2, mla_w_uq_2,
    mla_w_ukv_2, mla_w_out_2, ffn_w_gate_2, ffn_w_up_2, ffn_w_down_2, final_norm_g_2,
):
    x = first_block(
        x, meta_tokens, norm_gains, a_w_in, a_lb_logits, a_head_norm, a_w_out, kv_norm, kv_w,
        fg_b, b_w_q, b_w_out, ffn_w_up, ffn_conv, ffn_w_down,
    )
    return second_block(
        x, c_2, positions_2, ada_w_2, ada_b_2, norm_mix_g_2, norm_ffn_g_2, gdn_w_in_2,
        gdn_conv_w_2, gdn_a_log_2, gdn_dt_bias_2, gdn_norm_g_2, gdn_w_out_2, mla_w_in_2,
        mla_q_norm_g_2, mla_kv_norm_g_2, mla_w_uq_2, mla_w_ukv_2, mla_w_out_2, ffn_w_gate_2,
        ffn_w_up_2, ffn_w_down_2, final_norm_g_2,
    )


_drawn_inputs = setup_inputs


def setup_inputs(seed=0):
    import zlib

    import numpy as np

    out = dict(_drawn_inputs(seed))
    spreads = {}
    factors = {'ada_b_2': 4.253,
     'norm_mix_g_2': 7.288,
     'norm_ffn_g_2': 5.751,
     'gdn_norm_g_2': 8.0,
     'mla_q_norm_g_2': 8.0,
     'mla_kv_norm_g_2': 8.0,
     'mla_w_uq_2': 2.704}
    for name, (base, spread) in spreads.items():
        noise = np.random.default_rng([zlib.crc32(name.encode()), seed]).standard_normal(out[name].shape)
        drawn = base * np.exp(spread * noise) if base else spread * noise
        out[name] = __import__('jax').numpy.asarray(drawn.astype(out[name].dtype))
    for name, factor in factors.items():
        out[name] = (out[name] * factor).astype(out[name].dtype)
    return out
```

```python
from contextlib import ExitStack

import concourse.bass as bass
from concourse import mybir

F32 = mybir.dt.float32
F32R = mybir.dt.float32r
ALU = mybir.AluOpType
ACT = mybir.ActivationFunctionType
AX = mybir.AxisListType

P = 128
D = 1024
KD = D // P
META = 16
SEQ = 256
T1 = META + SEQ
HEADS = 8
FOX_HEADS = 16
FF_TILES = 22
HALF_FF = FF_TILES // 2
CONV_LEAD = 2
EPS = 1e-6
NEG = -1e30
SLOTS = 4
LEAD = 3
ITEM = 16 * P

PARAMS = [("gains", 8 * KD), ("kv_norm", KD), ("head_norm", KD), ("lb", 2 * KD), ("conv", 2 * 3 * 2 * FF_TILES),
          ("fg_b", 1), ("norm_mix", 2 * KD), ("norm_ffn", 2 * KD), ("final", KD), ("ada_b", 2 * 6 * KD),
          ("gdn_conv", 4 * 3 * HEADS), ("gdn_norm", 1), ("q_norm", 3), ("kv_norm2", 2), ("a_log", 1), ("dt_bias", 1)]
PCOL, _at = {}, 0
for _name, _n in PARAMS:
    PCOL[_name] = _at
    _at += _n
NPARAM = _at

CONSTS = [("ident", P), ("ones", P), ("causal_qk", P), ("causal_kq", P), ("chunk_kq", P), ("levels", 7 * P),
          ("rotate", P), ("reset_hgrn", T1), ("reset_gdn", SEQ), ("ones_row", T1), ("inv_freq", 1)]
CCOL, _at = {}, 0
for _name, _n in CONSTS:
    CCOL[_name] = _at
    _at += _n
NCONST = _at

STREAM = ([("a_in", 16, 16), ("a_out", 4, 16), ("up0", 22, 16), ("down0", 16, 11)]
          + [("kv", 8, 16), ("fg", 1, 8), ("b_q", 4, 16), ("b_out", 4, 16), ("up1", 22, 16), ("down1", 16, 11)]
          + [("gdn_qkv", 12, 16), ("gdn_gate", 4, 16), ("gdn_ab", 1, 8), ("gdn_out", 4, 16), ("gu0", 22, 16), ("dn0", 16, 11)]
          + [("mla_in", 3, 16), ("uq", 3, 12), ("ukv", 4, 8), ("mla_out", 4, 16), ("gu1", 22, 16), ("dn1", 16, 11)])
MOD_HOSTS, _at = {}, 0
for _name, _n, _every in (("a_in", 16, 1), ("a_out", 4, 1), ("down0", 16, 2), ("kv", 8, 1), ("b_q", 4, 1),
                          ("down1", 16, 2)):
    MOD_HOSTS[_name] = (_at, _every)
    _at += _n // _every
MOD_ITEMS = 48
assert _at == MOD_ITEMS


class Signal:

    def __init__(self, ctx, nc, name):
        self.sem = ctx.enter_context(nc.semaphore(name))
        self.base = 0

    def at(self, n):
        return self.base + n

    def passed(self, n):
        self.base += n


def fused_model(nc, w, params_d, consts_d, hT_d, c_d, pos_d, out_d):
    with ExitStack() as ctx:
        def sbuf(c, name, shape, dt=F32):
            return c.enter_context(nc.sbuf_tensor(name, shape, dt))

        params = sbuf(ctx, "feature_params", [P, NPARAM])
        consts = sbuf(ctx, "constants", [P, NCONST])
        h = sbuf(ctx, "h", [P, KD, T1])
        rstd = sbuf(ctx, "rstd", [P, T1])
        log_var = sbuf(ctx, "log_var", [P, T1])
        mod = sbuf(ctx, "mod", [P, 2, 6, KD])
        modf = mod[:, :, :, :].rearrange("p l s k -> p (l s k)")
        mod_sum = sbuf(ctx, "mod_sum", [P, 2, 2])
        c_row = sbuf(ctx, "c_row", [P, D])
        raw = sbuf(ctx, "raw", [P, SLOTS, ITEM])
        w_hi = sbuf(ctx, "w_hi", [P, SLOTS, ITEM], F32R)
        w_lo = sbuf(ctx, "w_lo", [P, SLOTS, ITEM], F32R)
        bank = [ctx.enter_context(nc.psum_tensor(f"bank{i}", [P, 512], F32)) for i in range(8)]

        sigs = {}

        def sig(name):
            if name not in sigs:
                sigs[name] = Signal(ctx, nc, name)
            return sigs[name]

        def par(name, i=0, n=1, p0=0, p1=P):
            if isinstance(i, int):
                return params[p0:p1, PCOL[name] + i:PCOL[name] + i + n]
            return params[p0:p1, bass.ds(i + PCOL[name], n)]

        def con(name, c0=0, n=None, p0=0, p1=P):
            n = dict(CONSTS)[name] - c0 if n is None else n
            return consts[p0:p1, CCOL[name] + c0:CCOL[name] + c0 + n]

        ident, ones = con("ident"), con("ones")

        raw_loaded = [ctx.enter_context(nc.semaphore(f"raw_loaded{s}")) for s in range(SLOTS)]
        hi_split = sig("hi_split")
        lo_split = sig("lo_split")
        plain_used = sig("plain_used")
        item_done = sig("item_done")
        item_out = sig("item_out")
        starts, at = {}, 0
        for name, n, blocks in STREAM:
            starts[name] = (at, n, blocks)
            at += n
        ring_end = at

        mod_turns = [0, 0]

        def item_of(r):
            for name, (first, n, blocks) in starts.items():
                if first <= r < first + n:
                    return name, first, n, blocks

        def each(eng, lo, hi, body):
            i = lo
            while i < hi and (i % SLOTS or i - lo < 2):
                body(i, i % SLOTS, i // SLOTS)
                i += 1
            turns = (hi - i) // SLOTS
            if turns >= 2:
                with eng.Fori(0, turns) as t:
                    for s in range(SLOTS):
                        body(t * SLOTS + (i + s), s, t + i // SLOTS)
                i += turns * SLOTS
            while i < hi:
                body(i, i % SLOTS, i // SLOTS)
                i += 1

        def load(sp, name, r, s):
            first, n, blocks = starts[name]
            if not isinstance(r, int) or r >= SLOTS:
                sp.wait_ge(lo_split.sem, r - (SLOTS - 1))
            sp.dma_start(raw[:, s, 0:blocks * P], w[name][r - first, :, :]).then_inc(raw_loaded[s], 16)

        mod_w = w["ada"]
        mod_loaded = [ctx.enter_context(nc.semaphore(f"mod_loaded{s}")) for s in range(2)]
        mod_used = sig("mod_used")
        mod_made = sig("mod_made")

        def mod_load(sp, room, a, s):
            sp.dma_start(room[:, s, :, :], mod_w[a, :, :].rearrange("p (t k) -> p t k", t=2)).then_inc(mod_loaded[s], 16)

        def mod_column(dve, room, a, s, turn):
            dve.wait_ge(mod_loaded[s], (turn + 1) * 16)
            for t in range(2):
                last = dve.tensor_tensor_reduce(out=room[:, s, t, :], in0=room[:, s, t, :], in1=c_row[:, :], scale=1.0,
                                                scalar=0.0, op0=ALU.mult, op1=ALU.add,
                                                accum_out=mod_sum[:, s, t:t + 1])
            last.then_inc(mod_used.sem, 1)
            dve.wait_ge(mod_used.sem, a + 1)
            at = a * 2
            d = modf[:, at:at + 2] if isinstance(at, int) else modf[:, bass.ds(at, 2)]
            dve.tensor_tensor(d, mod_sum[:, s, :], par("ada_b", at, 2), ALU.add)

        def split_hi(act, r, s, turn, blocks):
            act.wait_ge(raw_loaded[s], (turn + 1) * 16)
            if not isinstance(r, int) or r >= SLOTS:
                act.wait_ge(item_done.sem, r - (SLOTS - 1))
            act.activation(w_hi[:, s, 0:blocks * P], raw[:, s, 0:blocks * P], ACT.Copy).then_inc(hi_split.sem, 1)

        def split_lo(dve, r, s, turn, blocks):
            dve.wait_ge(hi_split.sem, r + 1)
            dve.tensor_tensor(w_lo[:, s, 0:blocks * P], raw[:, s, 0:blocks * P],
                              w_hi[:, s, 0:blocks * P].bitcast(F32), ALU.subtract).then_inc(lo_split.sem, 1)

        def split_ahead(eng, split, r, s, turn, last, blocks):
            if not isinstance(r, int):
                split(eng, r + LEAD, (s + LEAD) % SLOTS, turn + (s + LEAD) // SLOTS, blocks)
            elif r + LEAD < ring_end:
                split(eng, r + LEAD, (s + LEAD) % SLOTS, turn + (s + LEAD) // SLOTS, item_of(r + LEAD)[3])

        def steps(eng, name, step):
            first, n, blocks = starts[name]
            cut = max(first, first + n - LEAD)
            each(eng, first, cut, step)
            for r in range(cut, first + n):
                step(r, r % SLOTS, r // SLOTS)

        def product(name, tiles, k_tiles, x_hi, x_lo, cols, act_out=None, dve_out=None, pool_out=None, halves=False,
                    signals=(), dve_late=None, act_late=None):
            first, n, blocks = starts[name]
            width = cols[1] - cols[0]

            def where(r, s, t):
                if halves:
                    return bank[((s - first) % SLOTS) // 2]
                return bank[4 * (s % 2) + t]

            mod_first, every = MOD_HOSTS.get(name, (0, 0))
            hosts = n // every if every else 0
            ahead = LEAD + SLOTS
            with ExitStack() as inner, nc.Block() as block:
                if hosts:
                    room = sbuf(inner, f"mod_w_{name}", [P, 2, 2, D])

                def mod_at(s, turn):
                    slot = (s - first) % SLOTS // every % 2
                    i = turn * (SLOTS // every) + (s - first) // every
                    turns = turn * (SLOTS // every // 2) + (s - first - every * slot) // (2 * every)
                    return i + mod_first, slot, turns + mod_turns[slot]

                @block.sync
                def _(sp):
                    def step(r, s, turn):
                        if not isinstance(r, int):
                            load(sp, name, r + ahead, (s + ahead) % SLOTS)
                        elif r + ahead < ring_end:
                            load(sp, item_of(r + ahead)[0], r + ahead, (s + ahead) % SLOTS)
                        local = (s - first) % SLOTS
                        if hosts and local % every == 0:
                            a, slot, _ = mod_at(s, turn)
                            if not isinstance(a, int) or a + 2 < mod_first + hosts:
                                sp.wait_ge(mod_used.sem, a + 1)
                                mod_load(sp, room, a + 2, slot)
                    for i in range(min(2, hosts)):
                        mod_load(sp, room, mod_first + i, i)
                    cut = max(first, first + n - ahead)
                    each(sp, first, cut, step)
                    for r in range(cut, first + n):
                        step(r, r % SLOTS, r // SLOTS)

                @block.scalar
                def _(act):
                    def step(r, s, turn):
                        if act_out:
                            act_out(act, r - first, (s - first) % SLOTS, lambda t: where(r, s, t))
                        split_ahead(act, split_hi, r, s, turn, first + n, blocks)
                        if act_late:
                            act_late(act, r - first, (s - first) % SLOTS, lambda t: where(r, s, t))
                    steps(act, name, step)

                @block.vector
                def _(dve):
                    def step(r, s, turn):
                        if dve_out:
                            dve_out(dve, r - first, (s - first) % SLOTS, lambda t: where(r, s, t))
                        split_ahead(dve, split_lo, r, s, turn, first + n, blocks)
                        local = (s - first) % SLOTS
                        if hosts and local % every == 0:
                            mod_column(dve, room, *mod_at(s, turn))
                        if dve_late:
                            dve_late(dve, r - first, (s - first) % SLOTS, lambda t: where(r, s, t))
                    steps(dve, name, step)

                @block.gpsimd
                def _(pool):
                    if pool_out:
                        each(pool, first, first + n,
                             lambda r, s, turn: pool_out(pool, r - first, (s - first) % SLOTS))

                @block.tensor
                def _(pe):
                    def step(r, s, turn):
                        i = r
                        pe.wait_ge(lo_split.sem, i + 1)
                        if not halves:
                            if not isinstance(i, int) or i >= 2:
                                pe.wait_ge(item_out.sem, i - 1)
                        elif (s - first) % 2 == 0:
                            pe.wait_ge(item_out.sem, i - 2)
                        k0 = HALF_FF * ((s - first) % 2) if halves else 0
                        for t in range(tiles):
                            o = where(r, s, t)[:, 0:width]
                            for k in range(k_tiles):
                                b = slice((t * k_tiles + k) * P, (t * k_tiles + k + 1) * P)
                                xk = k0 + k
                                begin = xk == 0
                                end = xk == (FF_TILES if halves else k_tiles) - 1
                                pe.matmul(o, w_hi[:, s, b], x_hi[:, xk, cols[0]:cols[1]], start=begin, stop=False)
                                pe.matmul(o, w_hi[:, s, b], x_lo[:, xk, cols[0]:cols[1]], start=False, stop=False)
                                last = pe.matmul(o, w_lo[:, s, b], x_hi[:, xk, cols[0]:cols[1]], start=False,
                                                 stop=end)
                        last.then_inc(item_done.sem, 1)
                    each(pe, first, first + n, step)
            for i in range(2):
                mod_turns[i] += (hosts + 1 - i) // 2
            for name_, count in signals:
                sig(name_).passed(count)

        def item_ready(eng, name, j):
            eng.wait_ge(item_done.sem, j + (starts[name][0] + 1))

        def copy_out(name, tiles, dst, tile0, width, func=ACT.Copy, scale=1.0):
            def out(act, j, s, where):
                item_ready(act, name, j)
                for t in range(tiles):
                    at = j * tiles + (tile0 + t)
                    d = dst[:, at, 0:width] if isinstance(at, int) else dst[:, bass.ds(at, 1), 0:width]
                    last = act.activation(d, where(t)[:, 0:width], func, scale=scale)
                last.then_inc(item_out.sem, 1)
            return out

        def statistics(src, n, cols, count, squares):
            squared, summed, logged, ready = sig("squared"), sig("summed"), sig("logged"), sig("rstd_ready")
            c0, c1 = cols
            with nc.Block() as block:
                @block.scalar
                def _(act):
                    for k in range(n):
                        act.activation(squares[:, k, c0:c1], src(k), ACT.Square).then_inc(squared.sem, 1)
                    act.wait_ge(summed.sem, summed.at(1))
                    act.activation(log_var[:, c0:c1], bank[0][:, 0:c1 - c0], ACT.Ln, scale=1.0 / count,
                                   bias=eps_col[:, 0:1]).then_inc(logged.sem, 1)
                    act.wait_ge(logged.sem, logged.at(1))
                    act.activation(rstd[:, c0:c1], log_var[:, c0:c1], ACT.Exp, scale=-0.5).then_inc(ready.sem, 1)

                @block.tensor
                def _(pe):
                    for k in range(n):
                        pe.wait_ge(squared.sem, squared.at(k + 1))
                        last = pe.matmul(bank[0][:, 0:c1 - c0], ones, squares[:, k, c0:c1], start=k == 0,
                                         stop=k == n - 1)
                    last.then_inc(summed.sem, 1)
            squared.passed(n)
            summed.passed(1)
            logged.passed(1)
            ready.passed(1)

        def scaled_split(src, n, cols, gain, x_hi, x_lo, scaled, shift=None, use_rstd=True, out=None):
            made, shifted, high = sig("x_made"), sig("x_shifted"), sig("x_high")
            c0, c1 = cols
            with nc.Block() as block:
                @block.vector
                def _(dve):
                    def low(k):
                        dve.wait_ge(high.sem, high.at(k + 1))
                        dve.tensor_tensor(x_lo[:, k, c0:c1], scaled[:, k, c0:c1], x_hi[:, k, c0:c1].bitcast(F32),
                                          ALU.subtract)
                    for k in range(n):
                        if use_rstd:
                            dve.scalar_tensor_tensor(scaled[:, k, c0:c1], src(k), gain(k), rstd[:, c0:c1],
                                                     ALU.mult, ALU.mult).then_inc(made.sem, 1)
                        else:
                            dve.tensor_copy(scaled[:, k, c0:c1], src(k)).then_inc(made.sem, 1)
                        if shift is not None:
                            dve.wait_ge(made.sem, made.at(k + 1))
                            dve.tensor_scalar(scaled[:, k, c0:c1], scaled[:, k, c0:c1], shift(k), None,
                                              ALU.add).then_inc(shifted.sem, 1)
                        if k >= 1 and x_hi is not None:
                            low(k - 1)
                    if x_hi is not None:
                        low(n - 1)

                @block.scalar
                def _(act):
                    if x_hi is None:
                        return
                    for k in range(n):
                        s = shifted if shift is not None else made
                        act.wait_ge(s.sem, s.at(k + 1))
                        act.activation(x_hi[:, k, c0:c1], scaled[:, k, c0:c1], ACT.Copy).then_inc(high.sem, 1)
            made.passed(n)
            if shift is not None:
                shifted.passed(n)
            if x_hi is not None:
                high.passed(n)

        def add_residual(branch, cols, gain, use_rstd=True):
            weighed = sig("weighed")
            c0, c1 = cols
            with nc.Block() as block:
                @block.vector
                def _(dve):
                    for k in range(KD):
                        if use_rstd:
                            dve.scalar_tensor_tensor(branch(k), branch(k), gain(k), rstd[:, c0:c1], ALU.mult,
                                                     ALU.mult).then_inc(weighed.sem, 1)
                            dve.wait_ge(weighed.sem, weighed.at(k + 1))
                            dve.tensor_tensor(h[:, k, c0:c1], h[:, k, c0:c1], branch(k), ALU.add)
                        else:
                            dve.scalar_tensor_tensor(h[:, k, c0:c1], branch(k), gain(k), h[:, k, c0:c1], ALU.mult,
                                                     ALU.add)
            if use_rstd:
                weighed.passed(KD)

        def head_norm(o, n, width, gain, gate, x_hi, x_lo, head_sq):
            squared, summed, logged, ready = (sig("head_squared"), sig("head_summed"), sig("head_logged"),
                                              sig("head_rstd"))
            normed, gated, high = sig("head_normed"), sig("head_gated"), sig("head_high")
            with nc.Block() as block:
                @block.scalar
                def _(act):
                    for k in range(n):
                        act.activation(head_sq[:, k, :], o[:, k, :], ACT.Square).then_inc(squared.sem, 1)
                    for k in range(n):
                        act.wait_ge(summed.sem, summed.at(k + 1))
                        act.activation(head_sq[:, k, :], bank[k][:, 0:width], ACT.Ln, scale=1.0 / P,
                                       bias=eps_col[:, 0:1]).then_inc(logged.sem, 1)
                    for k in range(n):
                        act.wait_ge(logged.sem, logged.at(k + 1))
                        act.activation(head_sq[:, k, :], head_sq[:, k, :], ACT.Exp, scale=-0.5).then_inc(ready.sem, 1)
                    for k in range(n):
                        act.wait_ge(gated.sem, gated.at(k + 1))
                        act.activation(x_hi[:, k, 0:width], o[:, k, :], ACT.Copy).then_inc(high.sem, 1)

                @block.tensor
                def _(pe):
                    for k in range(n):
                        pe.wait_ge(squared.sem, squared.at(k + 1))
                        pe.matmul(bank[k][:, 0:width], ones, head_sq[:, k, :], start=True,
                                  stop=True).then_inc(summed.sem, 1)

                @block.vector
                def _(dve):
                    def low(k):
                        dve.wait_ge(high.sem, high.at(k + 1))
                        dve.tensor_tensor(x_lo[:, k, 0:width], o[:, k, :], x_hi[:, k, 0:width].bitcast(F32),
                                          ALU.subtract)
                    for k in range(n):
                        dve.wait_ge(ready.sem, ready.at(k + 1))
                        dve.scalar_tensor_tensor(o[:, k, :], o[:, k, :], gain(k), head_sq[:, k, :], ALU.mult,
                                                 ALU.mult).then_inc(normed.sem, 1)
                        dve.wait_ge(normed.sem, normed.at(k + 1))
                        dve.tensor_tensor(o[:, k, :], o[:, k, :], gate(k), ALU.mult).then_inc(gated.sem, 1)
                        if k >= 1:
                            low(k - 1)
                    low(n - 1)
            for s in (squared, summed, logged, ready, normed, gated, high):
                s.passed(n)

        eps_col = sbuf(ctx, "eps_col", [P, 1])

        inputs_in = sig("inputs_in")
        c_ready = sig("c_ready")
        with nc.Block() as block:
            @block.sync
            def _(sp):
                sp.dma_start(h[:, :, :], hT_d).then_inc(inputs_in.sem, 16)
                sp.dma_start(params[:, :], params_d).then_inc(inputs_in.sem, 16)
                for r in range(LEAD):
                    load(sp, "a_in", r, r % SLOTS)
                sp.dma_start(consts[:, :], consts_d).then_inc(inputs_in.sem, 16)
                sp.dma_start(c_row[:, :], c_d).then_inc(inputs_in.sem, 16)
                for r in range(LEAD, LEAD + SLOTS):
                    load(sp, "a_in", r, r % SLOTS)

            @block.vector
            def _(dve):
                dve.memset(eps_col[:, :], EPS)
                for r in range(LEAD):
                    split_lo(dve, r, r % SLOTS, 0, starts["a_in"][2])

            @block.scalar
            def _(act):
                for r in range(LEAD):
                    split_hi(act, r, r % SLOTS, 0, starts["a_in"][2])
                act.wait_ge(inputs_in.sem, 64)
                act.activation(c_row[:, :], c_row[:, :], ACT.Silu).then_inc(c_ready.sem, 1)

        def modulation_scales():
            with nc.Block() as block:
                @block.vector
                def _(dve):
                    for layer in range(2):
                        for part, gains in ((1, "norm_mix"), (4, "norm_ffn")):
                            dve.scalar_tensor_tensor(mod[:, layer, part, :], mod[:, layer, part, :], 1.0,
                                                     par(gains, layer * KD, KD), ALU.add, ALU.mult)

        gain1 = lambda layer, i: (lambda k: par("gains", (4 * layer + i) * KD + k))

        def up_product(layer, x_hi, x_lo, a_hi, a_lo, cols, up, conv, phase):
            lead = 0 if cols[0] == 0 else CONV_LEAD * conv
            width_in = cols[1] - cols[0]
            width = width_in - lead
            gate = sbuf(phase, f"gate_{up}", [P, 2, width])
            value = sbuf(phase, f"value_{up}", [P, 2, width])
            act_s = sbuf(phase, f"act_{up}", [P, 2, width])
            tapped, conved, silued, multiplied, high, halved = (sig("tapped"), sig("conved"), sig("silued"),
                                                                sig("multiplied"), sig("a_high"), sig("a_split"))
            first, n, _ = starts[up]
            taps = 4 if conv else 0

            def act_out(act, j, s, where):
                item_ready(act, up, j)
                if not conv:
                    return
                if not isinstance(j, int) or j >= 2:
                    act.wait_ge(multiplied.sem, multiplied.at(j - 1))
                for t, dst in ((0, gate), (1, value)):
                    act.activation(dst[:, s % 2, :], where(t)[:, lead:width_in], ACT.Copy,
                                   scale=par("conv", j + ((layer * 3 + 2) * 2 + t) * FF_TILES)).then_inc(tapped.sem, 1)

            def dve_out(dve, j, s, where):
                if not conv:
                    return
                for tap in (1, 0):
                    back = 2 - tap
                    skip = max(0, back - lead)
                    for t, dst in ((0, gate), (1, value)):
                        if tap == 1:
                            dve.wait_ge(tapped.sem, tapped.at(j * 2 + (t + 1)))
                        else:
                            dve.wait_ge(conved.sem, conved.at(j * 4 + (t + 1)))
                        d = dst[:, s % 2, skip:width]
                        last = dve.scalar_tensor_tensor(
                            d, where(t)[:, lead + skip - back:width_in - back],
                            par("conv", j + ((layer * 3 + tap) * 2 + t) * FF_TILES), d, ALU.mult, ALU.add)
                        last.then_inc(conved.sem, 1)

            def act_late(act, j, s, where):
                if conv:
                    act.wait_ge(conved.sem, conved.at(j * 4 + 3))
                if not isinstance(j, int) or j >= 2:
                    act.wait_ge(multiplied.sem, multiplied.at(j - 1))
                src = gate[:, s % 2, :] if conv else where(0)[:, 0:width]
                act.activation(act_s[:, s % 2, :], src, ACT.Silu).then_inc(silued.sem, 1)

            def dve_late(dve, j, s, where):
                dve.wait_ge(silued.sem, silued.at(j + 1))
                if conv:
                    dve.wait_ge(conved.sem, conved.at(j * 4 + 4))
                if not isinstance(j, int) or j >= 2:
                    dve.wait_ge(halved.sem, halved.at(j - 1))
                src = value[:, s % 2, :] if conv else where(1)[:, 0:width]
                dve.tensor_tensor(prod[:, s % 2, :], act_s[:, s % 2, :], src, ALU.mult).then_inc(multiplied.sem, 1)

            def pool_out(pool, j, s):
                pool.wait_ge(multiplied.sem, multiplied.at(j + 1))
                hi = a_hi[:, j, :] if isinstance(j, int) else a_hi[:, bass.ds(j, 1), :]
                lo = a_lo[:, j, :] if isinstance(j, int) else a_lo[:, bass.ds(j, 1), :]
                pool.tensor_copy(hi, prod[:, s % 2, :]).then_inc(high.sem, 1)
                pool.wait_ge(high.sem, high.at(j + 1))
                pool.tensor_tensor(lo, prod[:, s % 2, :], hi.bitcast(F32), ALU.subtract).then_inc(halved.sem, 1)

            prod = sbuf(phase, f"prod_{up}", [P, 2, width])

            if conv:
                def dve_conv(dve, j, s, where):
                    dve_out(dve, j, s, where)
                    dve.wait_ge(conved.sem, conved.at(j * 4 + 4))
                    dve.sem_inc(item_out.sem, 1)
                product(up, 2, KD, x_hi, x_lo, cols, act_out=act_out, dve_out=dve_conv, pool_out=pool_out,
                        act_late=act_late, dve_late=dve_late,
                        signals=(("tapped", 2 * n), ("conved", 4 * n), ("silued", n), ("multiplied", n),
                                 ("a_high", n), ("a_split", n)))
            else:
                def dve_plain(dve, j, s, where):
                    dve_late(dve, j, s, where)
                    dve.wait_ge(multiplied.sem, multiplied.at(j + 1))
                    dve.sem_inc(item_out.sem, 1)
                product(up, 2, KD, x_hi, x_lo, cols, act_out=lambda a, j, s, wh: (act_out(a, j, s, wh),
                                                                                act_late(a, j, s, wh)),
                        dve_out=dve_plain, pool_out=pool_out,
                        signals=(("silued", n), ("multiplied", n), ("a_high", n), ("a_split", n)))

        def down_product(down, a_hi, a_lo, width, dst):
            first, n, _ = starts[down]

            def act_out(act, j, s, where):
                if s % 2 == 1:
                    item_ready(act, down, j)
                    d = dst[:, j // 2, :] if isinstance(j, int) else dst[:, bass.ds((j - 1) // 2, 1), :]
                    act.activation(d, where(0)[:, 0:width], ACT.Copy).then_inc(item_out.sem, 2)
            product(down, 1, HALF_FF, a_hi, a_lo, (0, width), act_out=act_out, halves=True)

        with ExitStack() as outer:
            qfig = sbuf(outer, "qfig", [P, 4 * KD, T1])
            with ExitStack() as phase:
                x_hi, x_lo = sbuf(phase, "x_hi_a", [P, KD, T1], F32R), sbuf(phase, "x_lo_a", [P, KD, T1], F32R)
                room = sbuf(phase, "room_a", [P, KD, T1])
                statistics(lambda k: h[:, k, :], KD, (0, T1), D, room)
                scaled_split(lambda k: h[:, k, :], KD, (0, T1), gain1(0, 0), x_hi, x_lo, room)

                def a_in_out(act, j, s, where):
                    item_ready(act, "a_in", j)
                    for t in range(2):
                        at = j * 2 + t
                        d = qfig[:, at, :] if isinstance(at, int) else qfig[:, bass.ds(at, 1), :]
                        last = act.activation(d, where(t)[:, 0:T1], ACT.Copy)
                    last.then_inc(item_out.sem, 1)
                product("a_in", 2, KD, x_hi, x_lo, (0, T1), act_out=a_in_out)

            q, f, v, g = (qfig[:, i * KD:(i + 1) * KD, :] for i in range(4))
            hgrn2(nc, sbuf, sig, bank, q, f, v, g, par, con, ident)
            with ExitStack() as phase:
                x_hi, x_lo = sbuf(phase, "x_hi_b", [P, KD, T1], F32R), sbuf(phase, "x_lo_b", [P, KD, T1], F32R)
                head_sq = sbuf(phase, "head_sq_b", [P, KD, T1])
                head_norm(v, HEADS, T1, lambda k: par("head_norm", k), lambda k: g[:, k, :], x_hi, x_lo, head_sq)
                product("a_out", 2, KD, x_hi, x_lo, (0, T1), act_out=copy_out("a_out", 2, q, 0, T1))
            statistics(lambda k: q[:, k, :], KD, (0, T1), D, f)
            add_residual(lambda k: q[:, k, :], (0, T1), gain1(0, 1))

        def ffn_layer(layer, cols, gain, up, down, gain_out, conv, shift=None, gate_out=None):
            width = cols[1] - cols[0] - (CONV_LEAD if conv and cols[0] else 0)
            out = (cols[1] - width, cols[1])
            with ExitStack() as phase:
                branch = sbuf(phase, f"branch_{up}", [P, KD, T1])
                a_hi = sbuf(phase, f"a_hi_{up}", [P, FF_TILES, width], F32R)
                a_lo = sbuf(phase, f"a_lo_{up}", [P, FF_TILES, width], F32R)
                with ExitStack() as inner:
                    x_hi = sbuf(inner, f"x_hi_{up}", [P, KD, T1], F32R)
                    x_lo = sbuf(inner, f"x_lo_{up}", [P, KD, T1], F32R)
                    statistics(lambda k: h[:, k, cols[0]:cols[1]], KD, cols, D, branch)
                    scaled_split(lambda k: h[:, k, cols[0]:cols[1]], KD, cols, gain, x_hi, x_lo, branch, shift=shift)
                    up_product(layer, x_hi, x_lo, a_hi, a_lo, cols, up, conv, inner)
                down_product(down, a_hi, a_lo, width, branch[:, :, out[0]:out[1]])
                part = lambda k: branch[:, k, out[0]:out[1]]
                if gate_out is None:
                    squares = sbuf(phase, f"squares_{up}", [P, KD, T1])
                    statistics(part, KD, out, D, squares)
                    add_residual(part, out, gain_out)
                else:
                    add_residual(part, out, gate_out, use_rstd=False)

        ffn_layer(0, (0, T1), gain1(0, 2), "up0", "down0", gain1(0, 3), 1)

        late = (META - CONV_LEAD, T1)
        real = (META, T1)
        with ExitStack() as outer:
            kv = sbuf(outer, "kv", [P, 2 * KD, T1])
            qf = sbuf(outer, "q_fox", [P, KD, T1])
            zf = sbuf(outer, "zf", [P, T1])
            with ExitStack() as phase:
                x_hi, x_lo = sbuf(phase, "x_hi_c", [P, KD, T1], F32R), sbuf(phase, "x_lo_c", [P, KD, T1], F32R)
                room = sbuf(phase, "room_c", [P, KD, T1])
                statistics(lambda k: h[:, k, :], KD, (0, T1), D, room)
                scaled_split(lambda k: h[:, k, :], KD, (0, T1), lambda k: par("kv_norm", k), x_hi, x_lo, room)
                product("kv", 2, KD, x_hi, x_lo, (0, T1), act_out=copy_out("kv", 2, kv, 0, T1))

                def fg_out(act, j, s, where):
                    item_ready(act, "fg", j)
                    act.activation(zf[0:FOX_HEADS, :], where(0)[0:FOX_HEADS, 0:T1], ACT.Identity,
                                   bias=par("fg_b", p1=FOX_HEADS)).then_inc(item_out.sem, 1)
                product("fg", 1, KD, x_hi, x_lo, (0, T1), act_out=fg_out)
                scaled_split(lambda k: h[:, k, :], KD, (0, T1), gain1(1, 0), x_hi, x_lo, room)
                product("b_q", 2, KD, x_hi, x_lo, (0, T1), act_out=copy_out("b_q", 2, qf, 0, T1, scale=0.125))
            with ExitStack() as phase:
                v_tok = sbuf(phase, "v_tok", [P, 3, D])
                c_tok = sbuf(phase, "c_tok", [P, 3, FOX_HEADS])
                neg_c = sbuf(phase, "neg_c", [FOX_HEADS, T1])
                fox_gates(nc, sbuf, sig, bank, zf, neg_c, c_tok, con, ident)
                chunks = [(0, META), (META, P), (META + P, P)]
                to_token_major(nc, sig, bank, lambda t: kv[:, KD + t, :], KD, chunks, v_tok, ident)

                def logits(pe, h_, out, q0, qn, kn):
                    p0 = 64 * (h_ % 2)
                    pe.matmul(out, qf[p0:p0 + 64, h_ // 2, q0:q0 + qn], kv[p0:p0 + 64, h_ // 2, 0:kn],
                              start=True, stop=False)
                    return pe.matmul(out, con("ident", h_, 1, 0, FOX_HEADS).broadcast_to([FOX_HEADS, qn]),
                                     neg_c[:, 0:kn], start=False, stop=True)
                attention(nc, sbuf, sig, bank, "fox", FOX_HEADS, 64, chunks, logits, v_tok, qf, con, ident,
                          row_add=lambda c, h_, n: c_tok[0:n, c, h_:h_ + 1])
            with ExitStack() as phase:
                x_hi, x_lo = sbuf(phase, "x_hi_d", [P, KD, T1], F32R), sbuf(phase, "x_lo_d", [P, KD, T1], F32R)
                room = sbuf(phase, "room_d", [P, KD, T1])
                scaled_split(lambda k: qf[:, k, late[0]:late[1]], KD, late, None, x_hi, x_lo, room, use_rstd=False)
                product("b_out", 2, KD, x_hi, x_lo, late,
                        act_out=copy_out("b_out", 2, kv, 0, late[1] - late[0]))
                part = lambda k: kv[:, k, 0:late[1] - late[0]]
                statistics(part, KD, late, D, room)
                add_residual(part, late, gain1(1, 1))
        ffn_layer(1, late, gain1(1, 2), "up1", "down1", gain1(1, 3), 1)
        modulation_scales()

        modcol = lambda layer, part: (lambda k: mod[:, layer, part, k:k + 1])
        with ExitStack() as outer:
            qkvg = sbuf(outer, "qkvg", [P, 4 * HEADS, SEQ])
            ab = sbuf(outer, "ab", [P, SEQ])
            with ExitStack() as phase:
                x_hi, x_lo = sbuf(phase, "x_hi_e", [P, KD, T1], F32R), sbuf(phase, "x_lo_e", [P, KD, T1], F32R)
                room = sbuf(phase, "room_e", [P, KD, T1])
                u = sbuf(phase, "u_gdn", [P, 4, SEQ])
                statistics(lambda k: h[:, k, META:T1], KD, real, D, room)
                scaled_split(lambda k: h[:, k, META:T1], KD, real, modcol(0, 1), x_hi, x_lo, room,
                             shift=modcol(0, 0))
                gdn_in_product(sig, starts, product, item_ready, item_out, x_hi, x_lo, real, qkvg, u, par)

                def ab_out(act, j, s, where):
                    item_ready(act, "gdn_ab", j)
                    act.activation(ab[:, :], where(0)[:, 0:SEQ], ACT.Copy).then_inc(item_out.sem, 1)
                product("gdn_ab", 1, KD, x_hi, x_lo, real, act_out=ab_out)
            delta_rule(nc, sbuf, sig, bank, qkvg, ab, par, con, ident, ones, eps_col)
            o = qkvg[:, 0:HEADS, :]
            with ExitStack() as phase:
                x_hi, x_lo = sbuf(phase, "x_hi_f", [P, KD, T1], F32R), sbuf(phase, "x_lo_f", [P, KD, T1], F32R)
                head_sq = sbuf(phase, "head_sq_f", [P, HEADS, SEQ])
                head_norm(o, HEADS, SEQ, lambda k: par("gdn_norm"), lambda k: qkvg[:, 3 * HEADS + k, :], x_hi, x_lo,
                          head_sq)
                product("gdn_out", 2, KD, x_hi, x_lo, (0, SEQ), act_out=copy_out("gdn_out", 2, o, 0, SEQ))
            add_residual(lambda k: o[:, k, :], real, modcol(0, 2), use_rstd=False)
        ffn_layer(0, real, modcol(0, 4), "gu0", "dn0", None, 0, shift=modcol(0, 3), gate_out=modcol(0, 5))

        with ExitStack() as outer:
            k_nope = sbuf(outer, "k_nope", [P, 2 * HEADS, SEQ])
            q_mla = sbuf(outer, "q_mla", [P, HEADS + HEADS // 2, SEQ])
            latent = sbuf(outer, "latent", [P, 6, SEQ])
            sin_cos = sbuf(outer, "sin_cos", [P, 2, SEQ])
            rope_angles(nc, sbuf, sig, sin_cos, pos_d, con)
            with ExitStack() as phase:
                x_hi, x_lo = sbuf(phase, "x_hi_g", [P, KD, T1], F32R), sbuf(phase, "x_lo_g", [P, KD, T1], F32R)
                room = sbuf(phase, "room_g", [P, KD, T1])
                statistics(lambda k: h[:, k, META:T1], KD, real, D, room)
                scaled_split(lambda k: h[:, k, META:T1], KD, real, modcol(1, 1), x_hi, x_lo, room,
                             shift=modcol(1, 0))
                product("mla_in", 2, KD, x_hi, x_lo, real, act_out=copy_out("mla_in", 2, latent, 0, SEQ))
                whole = (0, SEQ)
                statistics(lambda k: latent[:, k, :], 3, whole, 3 * P, room)
                scaled_split(lambda k: latent[:, k, :], 3, whole, lambda k: par("q_norm", k), x_hi, x_lo, room)
                product("uq", 4, 3, x_hi, x_lo, whole, act_out=copy_out("uq", 4, q_mla, 0, SEQ,
                                                                        scale=float(192 ** -0.5)))
                statistics(lambda k: latent[:, 3 + k, :], 2, whole, 2 * P, room)
                scaled_split(lambda k: latent[:, 3 + k, :], 2, whole, lambda k: par("kv_norm2", k), x_hi, x_lo, room)
                product("ukv", 4, 2, x_hi, x_lo, whole, act_out=copy_out("ukv", 4, k_nope, 0, SEQ))
            q_rope = q_mla[:, HEADS:HEADS + HEADS // 2, :]
            k_rope = latent[:, 5:6, :]
            rotate(nc, sbuf, sig, bank, [(q_rope, 4), (k_rope, 1)], sin_cos, con)
            o = q_mla[:, 0:HEADS, :]
            with ExitStack() as phase:
                v_tok = sbuf(phase, "v_tok2", [P, 2, D])
                chunks = [(0, P), (P, P)]
                to_token_major(nc, sig, bank, lambda t: k_nope[:, HEADS + t, :], HEADS, chunks, v_tok, ident)

                def logits(pe, h_, out, q0, qn, kn):
                    p0 = 64 * (h_ % 2)
                    pe.matmul(out, q_mla[:, h_, q0:q0 + qn], k_nope[:, h_, 0:kn], start=True, stop=False)
                    return pe.matmul(out, q_rope[p0:p0 + 64, h_ // 2, q0:q0 + qn], k_rope[p0:p0 + 64, 0, 0:kn],
                                     start=False, stop=True)
                attention(nc, sbuf, sig, bank, "mla", HEADS, P, chunks, logits, v_tok, o, con, ident)
            with ExitStack() as phase:
                x_hi, x_lo = sbuf(phase, "x_hi_i", [P, KD, T1], F32R), sbuf(phase, "x_lo_i", [P, KD, T1], F32R)
                room = sbuf(phase, "room_i", [P, KD, T1])
                scaled_split(lambda k: o[:, k, :], KD, (0, SEQ), None, x_hi, x_lo, room, use_rstd=False)
                product("mla_out", 2, KD, x_hi, x_lo, (0, SEQ), act_out=copy_out("mla_out", 2, o, 0, SEQ))
            add_residual(lambda k: o[:, k, :], real, modcol(1, 2), use_rstd=False)
        ffn_layer(1, real, modcol(1, 4), "gu1", "dn1", None, 0, shift=modcol(1, 3), gate_out=modcol(1, 5))

        with ExitStack() as phase:
            room = sbuf(phase, "room_z", [P, KD, T1])
            statistics(lambda k: h[:, k, META:T1], KD, real, D, room)
            scaled_split(lambda k: h[:, k, META:T1], KD, real, lambda k: par("final", k), None, None, room)
            stored = sig("stored")
            with nc.Block() as block:
                @block.sync
                def _(sp):
                    sp.dma_start(out_d, room[:, :, META:T1]).then_inc(stored.sem, 16)
                    sp.wait_ge(stored.sem, 16)


def hgrn2(nc, sbuf, sig, bank, q, f, v, g, par, con, ident):
    real = (META, T1)
    tiles = [(0, META), (META, P), (META + P, P)]
    n_chunks = SEQ // 64
    with ExitStack() as scope:
        b = sbuf(scope, "log_decay", [P, HEADS, T1])
        e = sbuf(scope, "decay", [P, HEADS, T1])
        k_in = sbuf(scope, "k_in", [P, HEADS, T1])
        k = sbuf(scope, "k_gate", [P, HEADS, T1])
        lb = sbuf(scope, "lower_bound", [P, 6, KD])
        lb_max, lb_exp, lb_done = sig("lb_max"), sig("lb_exp"), sig("lb_done")
        sigmoided, silued = sig("f_sigmoided"), sig("g_silued")
        f_made, k_made, logged, summed = sig("f_made"), sig("k_made"), sig("f_logged"), sig("b_summed")
        exped, q_in, k_in_made, diffed = sig("b_exped"), sig("q_in"), sig("k_in_made"), sig("b_diffed")
        diff_exped = sig("diff_exped")
        reset = con("reset_hgrn")
        with nc.Block() as block:
            @block.scalar
            def _(act):
                act.activation(f, f, ACT.Sigmoid).then_inc(sigmoided.sem, 1)
                act.activation(g, g, ACT.Silu).then_inc(silued.sem, 1)
                act.wait_ge(lb_max.sem, lb_max.at(3))
                act.activation(lb[:, 1:3, :], lb[:, 1:3, :], ACT.Exp).then_inc(lb_exp.sem, 1)
                for i in range(HEADS):
                    act.wait_ge(k_made.sem, k_made.at(i + 1))
                    act.activation(f[:, i, :], f[:, i, :], ACT.Ln).then_inc(logged.sem, 1)
                for i in range(HEADS + 2):
                    if i < HEADS:
                        act.wait_ge(summed.sem, summed.at(i + 1))
                        act.activation(e[:, i, :], b[:, i, :], ACT.Exp).then_inc(exped.sem, 1)
                        act.activation(k_in[:, i, :], b[:, i, :], ACT.Exp, scale=-1.0).then_inc(exped.sem, 1)
                    if i >= 2:
                        h = i - 2
                        act.wait_ge(diffed.sem, diffed.at(2 * h + 2))
                        act.activation(f[:, h, :], f[:, h, :], ACT.Exp).then_inc(diff_exped.sem, 1)

            @block.vector
            def _(dve):
                l0, l1 = par("lb", 0, KD), par("lb", KD, KD)
                dve.tensor_tensor(lb[:, 0, :], l0, l1, ALU.max).then_inc(lb_max.sem, 1)
                dve.wait_ge(lb_max.sem, lb_max.at(1))
                dve.tensor_tensor(lb[:, 1, :], l0, lb[:, 0, :], ALU.subtract).then_inc(lb_max.sem, 1)
                dve.tensor_tensor(lb[:, 2, :], l1, lb[:, 0, :], ALU.subtract).then_inc(lb_max.sem, 1)
                dve.wait_ge(lb_exp.sem, lb_exp.at(1))
                dve.tensor_tensor(lb[:, 3, :], lb[:, 1, :], lb[:, 2, :], ALU.add).then_inc(lb_done.sem, 1)
                dve.wait_ge(lb_done.sem, lb_done.at(1))
                dve.reciprocal(lb[:, 3, :], lb[:, 3, :]).then_inc(lb_done.sem, 1)
                dve.wait_ge(lb_done.sem, lb_done.at(2))
                dve.tensor_tensor(lb[:, 4, :], lb[:, 1, :], lb[:, 3, :], ALU.mult).then_inc(lb_done.sem, 1)
                dve.wait_ge(lb_done.sem, lb_done.at(3))
                dve.tensor_scalar(lb[:, 5, :], lb[:, 4, :], -1.0, 1.0, ALU.mult, ALU.add).then_inc(lb_done.sem, 1)
                dve.wait_ge(lb_done.sem, lb_done.at(4))
                dve.wait_ge(sigmoided.sem, sigmoided.at(1))
                for i in range(HEADS):
                    dve.tensor_scalar(f[:, i, :], f[:, i, :], lb[:, 5, i:i + 1], lb[:, 4, i:i + 1], ALU.mult,
                                      ALU.add).then_inc(f_made.sem, 1)
                    dve.wait_ge(f_made.sem, f_made.at(i + 1))
                    dve.tensor_scalar(k[:, i, :], f[:, i, :], -1.0, 1.0, ALU.mult, ALU.add).then_inc(k_made.sem, 1)
                for i in range(1, HEADS + 4):
                    if 0 <= i - 1 < HEADS:
                        h = i - 1
                        dve.wait_ge(logged.sem, logged.at(h + 1))
                        dve.tensor_tensor_scan(b[:, h, :], reset, f[:, h, :], 0.0, ALU.mult,
                                               ALU.add).then_inc(summed.sem, 1)
                    if 0 <= i - 2 < HEADS:
                        h = i - 2
                        dve.wait_ge(summed.sem, summed.at(h + 1))
                        dve.wait_ge(exped.sem, exped.at(2 * h + 2))
                        dve.tensor_tensor(q[:, h, :], q[:, h, :], e[:, h, :], ALU.mult).then_inc(q_in.sem, 1)
                        dve.tensor_tensor(k_in[:, h, :], k_in[:, h, :], k[:, h, :], ALU.mult).then_inc(k_in_made.sem, 1)
                        dve.tensor_tensor(f[:, h, 0:META], b[:, h, META - 1:META].broadcast_to([P, META]),
                                          b[:, h, 0:META], ALU.subtract).then_inc(diffed.sem, 1)
                        chunked = b[:, h, META:T1].rearrange("p (c t) -> p c t", t=64)
                        dve.tensor_tensor(f[:, h, META:T1].rearrange("p (c t) -> p c t", t=64),
                                          chunked[:, :, 63:64].broadcast_to([P, n_chunks, 64]), chunked,
                                          ALU.subtract).then_inc(diffed.sem, 1)
                    if 0 <= i - 4 < HEADS:
                        h = i - 4
                        dve.wait_ge(diff_exped.sem, diff_exped.at(h + 1))
                        dve.tensor_tensor(f[:, h, :], f[:, h, :], k[:, h, :], ALU.mult)
        for s, n in ((lb_max, 3), (lb_exp, 1), (lb_done, 4), (sigmoided, 1), (silued, 1), (f_made, HEADS),
                     (k_made, HEADS), (logged, HEADS), (summed, HEADS), (exped, 2 * HEADS), (q_in, HEADS),
                     (k_in_made, HEADS), (diffed, 2 * HEADS), (diff_exped, HEADS)):
            s.passed(n)
        v_tok = sbuf(scope, "v_tok_a", [P, 2, 3, P])
        k_tok = sbuf(scope, "k_tok_a", [P, 2, 3, P])
        attn = sbuf(scope, "attn_a", [P, 2, 3, P])
        state = sbuf(scope, "state_a", [P, 2, n_chunks, P])
        turned, copied, masked = sig("turned"), sig("tok_copied"), sig("attn_masked")
        ds_done, stated, o_done, o_out = sig("ds_done"), sig("stated"), sig("o_done"), sig("o_out")

        def added_to(y, c):
            return bank[y][:, 3 * P:4 * P] if c == 2 else bank[6][:, c * P:(c + 1) * P]

        with nc.Block() as block:
            @block.tensor
            def _(pe):
                for i in range(HEADS + 2):
                    if i >= 2:
                        h, y = i - 2, i % 2
                        pe.wait_ge(masked.sem, masked.at(h + 1))
                        pe.wait_ge(stated.sem, stated.at(n_chunks * (h + 1)))
                        if h >= 1:
                            pe.wait_ge(o_out.sem, o_out.at(h))
                        for x, (t0, n) in enumerate(tiles):
                            pe.matmul(bank[7][:, t0:t0 + n], v_tok[0:n, y, x, :], attn[0:n, y, x, 0:n],
                                      start=x == 0, stop=False, skip_group_check=True)
                        for c in range(n_chunks):
                            t = slice(META + 64 * c, META + 64 * c + 64)
                            last = pe.matmul(bank[7][:, t], state[:, y, c, :], q[:, h, t], start=False,
                                             stop=c == n_chunks - 1, skip_group_check=True)
                        last.then_inc(o_done.sem, 1)
                    if i < HEADS:
                        y = i % 2
                        if i >= 2:
                            pe.wait_ge(copied.sem, copied.at(i - 1))
                            pe.wait_ge(masked.sem, masked.at(i - 1))
                            pe.wait_ge(stated.sem, stated.at(n_chunks * (i - 1)))
                        for x, (t0, n) in enumerate(tiles):
                            pe.transpose(bank[2 + y][0:n, x * P:(x + 1) * P], v[:, i, t0:t0 + n], ident)
                            pe.transpose(bank[4 + y][0:n, x * P:(x + 1) * P], f[:, i, t0:t0 + n], ident)
                        for x, (t0, n) in enumerate(tiles):
                            last = pe.matmul(bank[y][0:n, x * P:x * P + n], k_in[:, i, t0:t0 + n], q[:, i, t0:t0 + n],
                                             start=True, stop=True)
                        last.then_inc(turned.sem, 1)
                    if 1 <= i <= HEADS:
                        h, y = i - 1, (i - 1) % 2
                        pe.wait_ge(copied.sem, copied.at(h + 1))
                        if h >= 1:
                            pe.wait_ge(stated.sem, stated.at(n_chunks * h))
                        pe.wait_ge(masked.sem, masked.at(h + 1))
                        pe.matmul(added_to(y, 0), k_tok[0:META, y, 0, :], v_tok[0:META, y, 0, :], start=True, stop=True)
                        for c in range(n_chunks - 1):
                            r = slice(64 * (c % 2), 64 * (c % 2) + 64)
                            last = pe.matmul(added_to(y, c + 1), k_tok[r, y, 1 + c // 2, :],
                                             v_tok[r, y, 1 + c // 2, :], start=True, stop=True)
                        last.then_inc(ds_done.sem, 1)

            @block.scalar
            def _(act):
                for i in range(HEADS + 2):
                    if i >= 2:
                        act.wait_ge(o_done.sem, o_done.at(i - 1))
                        act.activation(v[:, i - 2, :], bank[7][:, 0:T1], ACT.Copy).then_inc(o_out.sem, 1)
                    if i < HEADS:
                        y = i % 2
                        act.wait_ge(turned.sem, turned.at(i + 1))
                        for src, dst in ((bank[2 + y], v_tok), (bank[4 + y], k_tok)):
                            act.activation(dst[0:META, y, 0, :], src[0:META, 0:P], ACT.Copy)
                            last = act.activation(dst[:, y, 1:3, :],
                                                  src[:, P:3 * P].rearrange("p (x c) -> p x c", x=2), ACT.Copy)
                        last.then_inc(copied.sem, 1)

            @block.vector
            def _(dve):
                for i in range(HEADS + 1):
                    if i < HEADS:
                        y = i % 2
                        dve.wait_ge(turned.sem, turned.at(i + 1))
                        if i >= 2:
                            dve.wait_ge(o_done.sem, o_done.at(i - 1))
                        dve.tensor_tensor(attn[0:META, y, 0, 0:META], bank[y][0:META, 0:META],
                                          con("chunk_kq", 0, META, 0, META), ALU.mult)
                        dve.tensor_tensor(attn[:, y, 1:3, :], bank[y][:, P:3 * P].rearrange("p (x c) -> p x c", x=2),
                                          con("chunk_kq").unsqueeze(1).broadcast_to([P, 2, P]),
                                          ALU.mult).then_inc(masked.sem, 1)
                    if i >= 1:
                        h, y = i - 1, (i - 1) % 2
                        dve.wait_ge(ds_done.sem, ds_done.at(h + 1))
                        dve.tensor_copy(state[:, y, 0, :], added_to(y, 0)).then_inc(stated.sem, 1)
                        for c in range(n_chunks - 1):
                            t = META + 64 * c + 63
                            dve.wait_ge(stated.sem, stated.at(n_chunks * h + c + 1))
                            dve.scalar_tensor_tensor(state[:, y, c + 1, :], state[:, y, c, :], e[:, h, t:t + 1],
                                                     added_to(y, c + 1), ALU.mult,
                                                     ALU.add).then_inc(stated.sem, 1)
        for s, n in ((turned, HEADS), (copied, HEADS), (masked, HEADS), (ds_done, HEADS),
                     (stated, n_chunks * HEADS), (o_done, HEADS), (o_out, HEADS)):
            s.passed(n)


def fox_gates(nc, sbuf, sig, bank, zf, neg_c, c_tok, con, ident):
    n = FOX_HEADS
    a_step, c_step, c_turned = sig("fg_act"), sig("fg_dve"), sig("c_turned")
    with ExitStack() as scope:
        t = sbuf(scope, "fg_room", [n, 3, T1])
        z = zf[0:n, :]
        with nc.Block() as block:
            @block.scalar
            def _(act):
                act.activation(t[:, 0, :], z, ACT.Abs).then_inc(a_step.sem, 1)
                act.wait_ge(a_step.sem, a_step.at(1))
                act.activation(t[:, 0, :], t[:, 0, :], ACT.Exp, scale=-1.0).then_inc(a_step.sem, 1)
                act.wait_ge(a_step.sem, a_step.at(2))
                act.activation(t[:, 0, :], t[:, 0, :], ACT.Ln, bias=1.0).then_inc(a_step.sem, 1)

            @block.vector
            def _(dve):
                dve.wait_ge(a_step.sem, a_step.at(3))
                dve.scalar_tensor_tensor(t[:, 1, :], z, 0.0, t[:, 0, :], ALU.min, ALU.subtract).then_inc(c_step.sem, 1)
                dve.wait_ge(c_step.sem, c_step.at(1))
                dve.tensor_tensor_scan(t[:, 2, :], con("ones_row", p1=n), t[:, 1, :], 0.0, ALU.mult,
                                       ALU.add).then_inc(c_step.sem, 1)
                dve.wait_ge(c_step.sem, c_step.at(2))
                dve.tensor_scalar(neg_c[:, :], t[:, 2, :], -1.0, None, ALU.mult)
                dve.wait_ge(c_turned.sem, c_turned.at(1))
                dve.tensor_copy(c_tok[0:META, 0, :], bank[0][0:META, 0:n])
                dve.tensor_copy(c_tok[:, 1:3, :], bank[0][:, n:3 * n].rearrange("p (x c) -> p x c", x=2))

            @block.tensor
            def _(pe):
                pe.wait_ge(c_step.sem, c_step.at(2))
                for x, (t0, m) in enumerate(((0, META), (META, P), (META + P, P))):
                    last = pe.transpose(bank[0][0:m, x * n:(x + 1) * n], t[:, 2, t0:t0 + m], ident[0:n, 0:n])
                last.then_inc(c_turned.sem, 1)
        a_step.passed(3)
        c_step.passed(2)
        c_turned.passed(1)


def to_token_major(nc, sig, bank, src, n_tiles, chunks, dst, ident):
    turned, copied = sig("tile_turned"), sig("tile_copied")
    with nc.Block() as block:
        @block.tensor
        def _(pe):
            for t in range(n_tiles):
                if t >= 4:
                    pe.wait_ge(copied.sem, copied.at(t - 3))
                for x, (t0, n) in enumerate(chunks):
                    last = pe.transpose(bank[t % 4][0:n, x * P:(x + 1) * P], src(t)[:, t0:t0 + n], ident)
                last.then_inc(turned.sem, 1)

        @block.scalar
        def _(act):
            for t in range(n_tiles):
                act.wait_ge(turned.sem, turned.at(t + 1))
                x = 0
                if chunks[0][1] < P:
                    n = chunks[0][1]
                    act.activation(dst[0:n, 0, t * P:(t + 1) * P], bank[t % 4][0:n, 0:P], ACT.Copy)
                    x = 1
                act.activation(dst[:, x:len(chunks), t * P:(t + 1) * P],
                               bank[t % 4][:, x * P:len(chunks) * P].rearrange("p (x c) -> p x c", c=P),
                               ACT.Copy).then_inc(copied.sem, 1)
    turned.passed(n_tiles)
    copied.passed(n_tiles)


def attention(nc, sbuf, sig, bank, name, n_heads, dv, chunks, logits, v_tok, out, con, ident, row_add=None):
    width = chunks[-1][0] + chunks[-1][1]
    nt = len(chunks)
    offs = [sum(q0 + qn for q0, qn in chunks[:x]) for x in range(nt)]
    cols = offs[-1] + width
    full = [y for y in range(nt) if chunks[y][1] == P]
    per = P // dv
    pt_off, at = {}, 0
    for y in full:
        pt_off[y] = at
        at += width - chunks[y][0]
    pt_cols = at
    small = [y for y in range(nt) if y not in full]
    for y in small:
        pt_off[y] = 0
    scored, maxed, exped, scaled = sig("scored"), sig("maxed"), sig("p_exped"), sig("p_scaled")
    added, inverted = sig("mask_added"), sig("sum_inverted")
    p_turned, pt_copied, pv_done, pv_out = sig("p_turned"), sig("pt_copied"), sig("pv_done"), sig("pv_out")
    with ExitStack() as scope:
        p = sbuf(scope, f"probs_{name}", [P, 3, cols])
        pt = sbuf(scope, f"probs_turned_{name}", [P, 2, pt_cols])
        pt_small = sbuf(scope, f"probs_turned_meta_{name}", [META, 2, width])
        neg_max = sbuf(scope, f"neg_max_{name}", [P, 3, nt])
        row_sum = sbuf(scope, f"row_sum_{name}", [P, 3, nt])
        n_add = nt + (sum(q0 > 0 for q0, _ in chunks) if row_add else 0)

        def pt_of(y, b):
            q0, n = chunks[y]
            if y in small:
                return pt_small[0:n, b, 0:width - q0]
            return pt[:, b, pt_off[y]:pt_off[y] + width - q0]

        with nc.Block() as block:
            @block.tensor
            def _(pe):
                for i in range(n_heads + 3):
                    if i < n_heads:
                        if i >= 2:
                            pe.wait_ge(exped.sem, exped.at(nt * (i - 1)))
                        for x, (q0, qn) in enumerate(chunks):
                            last = logits(pe, i, bank[i % 2][0:qn, offs[x]:offs[x] + q0 + qn], q0, qn, q0 + qn)
                        last.then_inc(scored.sem, 1)
                    if 2 <= i <= n_heads + 1:
                        h, b = i - 2, i % 2
                        pe.wait_ge(scaled.sem, scaled.at(nt * (h + 1)))
                        if h >= 2:
                            pe.wait_ge(pt_copied.sem, pt_copied.at(h - 1))
                        for x, (q0, qn) in enumerate(chunks):
                            for y in range(x + 1):
                                k0, kn = chunks[y]
                                at = pt_off[y] + q0 - k0
                                last = pe.transpose(bank[(4 if y in small else 2) + b][0:kn, at:at + qn],
                                                    p[0:qn, h % 3, offs[x] + k0:offs[x] + k0 + kn], ident[0:qn, 0:qn])
                        last.then_inc(p_turned.sem, 1)
                    if i >= 3:
                        h, b = i - 3, (i - 3) % 2
                        pe.wait_ge(pt_copied.sem, pt_copied.at(h + 1))
                        t, p0 = h // per, dv * (h % per)
                        if t >= 2 and h % per == 0:
                            pe.wait_ge(pv_out.sem, pv_out.at(t - 1))
                        for y, (k0, kn) in enumerate(chunks):
                            last = pe.matmul(bank[6 + t % 2][p0:p0 + dv, k0:width], v_tok[0:kn, y, h * dv:(h + 1) * dv],
                                             pt_of(y, b), start=y == 0, stop=y == nt - 1)
                        last.then_inc(pv_done.sem, 1)

            @block.vector
            def _(dve):
                for i in range(n_heads + 1):
                    if i < n_heads:
                        b = i % 2
                        dve.wait_ge(scored.sem, scored.at(i + 1))
                        n = n_add * i
                        for x, (q0, qn) in enumerate(chunks):
                            s = bank[b][0:qn, offs[x]:offs[x] + q0 + qn]
                            add = row_add(x, i, qn) if row_add else 0.0
                            dve.scalar_tensor_tensor(s[:, q0:q0 + qn], s[:, q0:q0 + qn], add,
                                                     con("causal_qk", 0, qn, 0, qn), ALU.add,
                                                     ALU.add).then_inc(added.sem, 1)
                            n += 1
                            if row_add and q0:
                                dve.tensor_scalar(s[:, 0:q0], s[:, 0:q0], add, None, ALU.add).then_inc(added.sem, 1)
                                n += 1
                        dve.wait_ge(added.sem, added.at(n))
                        for x, (q0, qn) in enumerate(chunks):
                            dve.tensor_reduce(neg_max[0:qn, i % 3, x:x + 1], bank[b][0:qn, offs[x]:offs[x] + q0 + qn],
                                              AX.X, ALU.max, negate=True).then_inc(maxed.sem, 1)
                    if i >= 1:
                        h, b = i - 1, (i - 1) % 2
                        dve.wait_ge(exped.sem, exped.at(nt * (h + 1)))
                        for x, (q0, qn) in enumerate(chunks):
                            dve.reciprocal(row_sum[0:qn, h % 3, x:x + 1],
                                           row_sum[0:qn, h % 3, x:x + 1]).then_inc(inverted.sem, 1)
                        for x, (q0, qn) in enumerate(chunks):
                            dve.wait_ge(inverted.sem, inverted.at(nt * h + x + 1))
                            s = p[0:qn, h % 3, offs[x]:offs[x] + q0 + qn]
                            dve.tensor_scalar(s, s, row_sum[0:qn, h % 3, x:x + 1], None,
                                              ALU.mult).then_inc(scaled.sem, 1)

            @block.scalar
            def _(act):
                for i in range(n_heads + 3):
                    if i < n_heads:
                        b = i % 2
                        if i >= 3:
                            act.wait_ge(p_turned.sem, p_turned.at(i - 2))
                        act.wait_ge(maxed.sem, maxed.at(nt * (i + 1)))
                        for x, (q0, qn) in enumerate(chunks):
                            act.activation(p[0:qn, i % 3, offs[x]:offs[x] + q0 + qn],
                                           bank[b][0:qn, offs[x]:offs[x] + q0 + qn], ACT.Exp,
                                           bias=neg_max[0:qn, i % 3, x:x + 1],
                                           accum_out=row_sum[0:qn, i % 3, x:x + 1]).then_inc(exped.sem, 1)
                    if 2 <= i <= n_heads + 1:
                        h, b = i - 2, i % 2
                        act.wait_ge(p_turned.sem, p_turned.at(h + 1))
                        if h >= 2:
                            act.wait_ge(pv_done.sem, pv_done.at(h - 1))
                        if small:
                            act.activation(pt_of(0, b), bank[4 + b][0:META, 0:width], ACT.Copy)
                        act.activation(pt[:, b, :], bank[2 + b][:, 0:pt_cols], ACT.Copy).then_inc(pt_copied.sem, 1)
                    if i >= 3 and (i - 3) % per == per - 1:
                        t = (i - 3) // per
                        act.wait_ge(pv_done.sem, pv_done.at(i - 2))
                        act.activation(out[:, t, 0:width], bank[6 + t % 2][:, 0:width], ACT.Copy).then_inc(pv_out.sem, 1)
        for s, n in ((scored, n_heads), (maxed, nt * n_heads), (exped, nt * n_heads), (scaled, nt * n_heads),
                     (added, n_add * n_heads), (inverted, nt * n_heads), (p_turned, n_heads),
                     (pt_copied, n_heads), (pv_done, n_heads), (pv_out, n_heads // per)):
            s.passed(n)


def gdn_in_product(sig, starts, product, item_ready, item_out, x_hi, x_lo, real, qkvg, u, par):
    tapped, conved, silued = sig("tapped"), sig("conved"), sig("silued")
    n = starts["gdn_qkv"][1]

    def act_out(act, j, s, where):
        item_ready(act, "gdn_qkv", j)
        if not isinstance(j, int) or j >= 2:
            act.wait_ge(silued.sem, silued.at(j * 2 - 2))
        for t in range(2):
            act.activation(u[:, 2 * (s % 2) + t, :], where(t)[:, 0:SEQ], ACT.Copy,
                           scale=par("gdn_conv", j * 8 + (t * 4 + 3))).then_inc(tapped.sem, 1)

    def dve_out(dve, j, s, where):
        for tap in (2, 1, 0):
            back = 3 - tap
            for t in range(2):
                if tap == 2:
                    dve.wait_ge(tapped.sem, tapped.at(j * 2 + (t + 1)))
                else:
                    dve.wait_ge(conved.sem, conved.at(j * 6 + (2 * (1 - tap) + t + 1)))
                d = u[:, 2 * (s % 2) + t, back:SEQ]
                dve.scalar_tensor_tensor(d, where(t)[:, 0:SEQ - back], par("gdn_conv", j * 8 + (t * 4 + tap)), d,
                                         ALU.mult, ALU.add).then_inc(conved.sem, 1)
        dve.wait_ge(conved.sem, conved.at(j * 6 + 6))
        dve.sem_inc(item_out.sem, 1)

    def act_late(act, j, s, where):
        for t in range(2):
            act.wait_ge(conved.sem, conved.at(j * 6 + (5 + t)))
            at = j * 2 + t
            d = qkvg[:, at, :] if isinstance(at, int) else qkvg[:, bass.ds(at, 1), :]
            act.activation(d, u[:, 2 * (s % 2) + t, :], ACT.Silu).then_inc(silued.sem, 1)
    product("gdn_qkv", 2, KD, x_hi, x_lo, real, act_out=act_out, dve_out=dve_out, act_late=act_late,
            signals=(("tapped", 2 * n), ("conved", 6 * n), ("silued", 2 * n)))

    def gate_out(act, j, s, where):
        item_ready(act, "gdn_gate", j)
        for t in range(2):
            at = j * 2 + (t + 3 * HEADS)
            d = qkvg[:, at, :] if isinstance(at, int) else qkvg[:, bass.ds(at, 1), :]
            last = act.activation(d, where(t)[:, 0:SEQ], ACT.Silu)
        last.then_inc(item_out.sem, 1)
    product("gdn_gate", 2, KD, x_hi, x_lo, real, act_out=gate_out)


def delta_rule(nc, sbuf, sig, bank, qkvg, ab, par, con, ident, ones, eps_col):
    H, C = HEADS, P
    q, k, v = qkvg[:, 0:H, :], qkvg[:, H:2 * H, :], qkvg[:, 2 * H:3 * H, :]
    with ExitStack() as scope:
        rows = sbuf(scope, "gate_rows", [P, SEQ])
        tok = sbuf(scope, "gate_tok", [P, 2, P])
        both = sbuf(scope, "coupling_inverse", [P, 2, 2 * H, C])
        LT, TT = both[:, 0, :, :], both[:, 1, :, :]
        kbe = sbuf(scope, "k_beta_decay", [P, H, P])
        kdec = sbuf(scope, "k_to_end", [P, H, P])
        G, B, BE, DE = 0, 32, 64, 96
        with ExitStack() as inner:
            t = sbuf(inner, "gate_room", [H, 6, SEQ])
            neg_a = sbuf(inner, "neg_a", [H, 1])
            sq = both[:, :, :, :].rearrange("p a (h x) c -> p a h (x c)", x=2)
            a_step, d_step, z_step = sig("gdn_act"), sig("gdn_dve"), sig("gdn_zero")
            rows_ready, rows_turned = sig("rows_ready"), sig("rows_turned")
            squared, summed, logged, ready = sig("qk_squared"), sig("qk_summed"), sig("qk_logged"), sig("qk_rstd")
            with nc.Block() as block:
                @block.gpsimd
                def _(pool):
                    pool.memset(rows[:, :], 0.0).then_inc(z_step.sem, 1)

                @block.scalar
                def _(act):
                    for a, x in enumerate((q, k)):
                        act.activation(sq[:, a, :, :], x, ACT.Square).then_inc(squared.sem, 1)
                    act.wait_ge(z_step.sem, z_step.at(1))
                    act.activation(rows[B:B + H, :], ab[32:32 + H, :], ACT.Sigmoid).then_inc(a_step.sem, 1)
                    act.activation(t[:, 5, :], ab[32:32 + H, :], ACT.Sigmoid).then_inc(a_step.sem, 1)
                    act.activation(neg_a[:, :], par("a_log", p1=H), ACT.Exp).then_inc(a_step.sem, 1)
                    act.wait_ge(d_step.sem, d_step.at(1))
                    act.activation(t[:, 1, :], t[:, 0, :], ACT.Abs).then_inc(a_step.sem, 1)
                    act.wait_ge(a_step.sem, a_step.at(4))
                    act.activation(t[:, 1, :], t[:, 1, :], ACT.Exp, scale=-1.0).then_inc(a_step.sem, 1)
                    act.wait_ge(a_step.sem, a_step.at(5))
                    act.activation(t[:, 1, :], t[:, 1, :], ACT.Ln, bias=1.0).then_inc(a_step.sem, 1)
                    for h in range(H):
                        act.wait_ge(summed.sem, summed.at(h + 1))
                        o = bank[h][:, 0:2 * SEQ].rearrange("p (a t) -> p a t", a=2)
                        act.activation(sq[:, :, h, :], o, ACT.Ln, bias=eps_col[:, 0:1]).then_inc(logged.sem, 1)
                    for h in range(H):
                        act.wait_ge(logged.sem, logged.at(h + 1))
                        act.activation(sq[:, :, h, :], sq[:, :, h, :], ACT.Exp, scale=-0.5).then_inc(ready.sem, 1)
                    act.wait_ge(d_step.sem, d_step.at(5))
                    act.activation(t[:, 3, :], rows[G:G + H, :], ACT.Exp).then_inc(a_step.sem, 1)
                    act.wait_ge(d_step.sem, d_step.at(6))
                    act.activation(rows[DE:DE + H, :], t[:, 4, :], ACT.Exp).then_inc(a_step.sem, 1)

                @block.vector
                def _(dve):
                    dve.tensor_scalar(t[:, 0, :], ab[0:H, :], par("dt_bias", p1=H), None, ALU.add).then_inc(d_step.sem, 1)
                    dve.wait_ge(a_step.sem, a_step.at(6))
                    dve.wait_ge(d_step.sem, d_step.at(1))
                    dve.scalar_tensor_tensor(t[:, 2, :], t[:, 0, :], 0.0, t[:, 1, :], ALU.max,
                                             ALU.add).then_inc(d_step.sem, 1)
                    dve.tensor_scalar(neg_a[:, :], neg_a[:, :], -1.0, None, ALU.mult).then_inc(d_step.sem, 1)
                    dve.wait_ge(d_step.sem, d_step.at(3))
                    dve.tensor_scalar(t[:, 2, :], t[:, 2, :], neg_a[:, 0:1], None, ALU.mult).then_inc(d_step.sem, 1)
                    dve.wait_ge(d_step.sem, d_step.at(4))
                    dve.wait_ge(z_step.sem, z_step.at(1))
                    dve.tensor_tensor_scan(rows[G:G + H, :], con("reset_gdn", p1=H), t[:, 2, :], 0.0, ALU.mult,
                                           ALU.add).then_inc(d_step.sem, 1)
                    dve.wait_ge(d_step.sem, d_step.at(5))
                    g2 = rows[G:G + H, :].rearrange("p (c t) -> p c t", c=2)
                    dve.tensor_tensor(t[:, 4, :].rearrange("p (c t) -> p c t", c=2),
                                      g2[:, :, C - 1:C].broadcast_to([H, 2, C]), g2,
                                      ALU.subtract).then_inc(d_step.sem, 1)
                    for h in range(H):
                        dve.wait_ge(ready.sem, ready.at(h + 1))
                        dve.scalar_tensor_tensor(q[:, h, :], q[:, h, :], float(P ** -0.5), sq[:, 0, h, :], ALU.mult,
                                                 ALU.mult)
                        dve.tensor_tensor(k[:, h, :], k[:, h, :], sq[:, 1, h, :], ALU.mult)
                    dve.wait_ge(a_step.sem, a_step.at(8))
                    dve.tensor_tensor(rows[BE:BE + H, :], t[:, 3, :], t[:, 5, :], ALU.mult).then_inc(rows_ready.sem, 1)
                    dve.wait_ge(rows_turned.sem, rows_turned.at(1))
                    dve.tensor_copy(tok[:, :, :], bank[6][:, 0:2 * P].rearrange("p (x c) -> p x c", x=2))

                @block.tensor
                def _(pe):
                    pe.wait_ge(squared.sem, squared.at(2))
                    for h in range(H):
                        for a in range(2):
                            last = pe.matmul(bank[h][:, a * SEQ:(a + 1) * SEQ], ones, sq[:, a, h, :], start=True,
                                             stop=True)
                        last.then_inc(summed.sem, 1)
                    pe.wait_ge(logged.sem, logged.at(H))
                    pe.wait_ge(rows_ready.sem, rows_ready.at(1))
                    for x in range(2):
                        last = pe.transpose(bank[6][:, x * P:(x + 1) * P], rows[:, x * C:(x + 1) * C], ident)
                    last.then_inc(rows_turned.sem, 1)
            for s, n in ((a_step, 8), (d_step, 6), (z_step, 1), (rows_ready, 1), (rows_turned, 1), (squared, 2),
                         (summed, H), (logged, H), (ready, H)):
                s.passed(n)

        with ExitStack() as inner:
            kb = sbuf(inner, "k_beta", [P, 2, SEQ])
            decay = sbuf(inner, "pair_decay", [P, 2, 2, C])
            eg = sbuf(inner, "q_decay", [P, 2, C])
            spread, turned = sig("spread"), sig("turned")
            kb_made, arg_made, decayed = sig("kb_made"), sig("decay_arg"), sig("pair_decayed")
            paired, kdec_made, coupled = sig("paired"), sig("kdec_made"), sig("coupled")
            taken = sig("tok_taken")
            with nc.Block() as block:
                @block.tensor
                def _(pe):
                    for i in range(H + 1):
                        if i < H:
                            y = i % 2
                            if i >= 2:
                                pe.wait_ge(arg_made.sem, arg_made.at(2 * (i - 1)))
                                pe.wait_ge(decayed.sem, decayed.at(2 * (i - 1)))
                                pe.wait_ge(taken.sem, taken.at(3 * (i - 1)))
                                pe.wait_ge(kdec_made.sem, kdec_made.at(i - 1))
                            pe.matmul(bank[y][:, 0:SEQ], con("ident", G + i, 1).broadcast_to([P, P]),
                                      rows[:, :], start=True, stop=True)
                            pe.matmul(bank[y][:, SEQ:2 * SEQ], con("ident", B + i, 1).broadcast_to([P, P]),
                                      rows[:, :], start=True, stop=True).then_inc(spread.sem, 1)
                            for n, src in enumerate((k, v)):
                                for x in range(2):
                                    last = pe.transpose(bank[2 + y][:, (2 * n + x) * P:(2 * n + x + 1) * P],
                                                        src[:, i, x * C:(x + 1) * C], ident)
                            last.then_inc(turned.sem, 1)
                        if i >= 1:
                            h, y = i - 1, (i - 1) % 2
                            pe.wait_ge(kb_made.sem, kb_made.at(h + 1))
                            if h >= 2:
                                pe.wait_ge(coupled.sem, coupled.at(3 * (h - 1)))
                            for n, src in enumerate((kb[:, y, :], q[:, h, :])):
                                for x in range(2):
                                    last = pe.matmul(bank[4 + y][:, (2 * n + x) * P:(2 * n + x + 1) * P],
                                                     k[:, h, x * C:(x + 1) * C], src[:, x * C:(x + 1) * C],
                                                     start=True, stop=True)
                            last.then_inc(paired.sem, 1)

                @block.vector
                def _(dve):
                    for i in range(H + 1):
                        if i < H:
                            y = i % 2
                            dve.wait_ge(spread.sem, spread.at(i + 1))
                            if i >= 2:
                                dve.wait_ge(paired.sem, paired.at(i - 1))
                                dve.wait_ge(coupled.sem, coupled.at(3 * (i - 1)))
                            dve.tensor_tensor(kb[:, y, :], k[:, i, :], bank[y][:, SEQ:2 * SEQ],
                                              ALU.mult).then_inc(kb_made.sem, 1)
                            for x in range(2):
                                dve.scalar_tensor_tensor(decay[:, y, x, :], bank[y][:, x * C:(x + 1) * C],
                                                         tok[:, x, G + i:G + i + 1], con("causal_kq"),
                                                         ALU.subtract, ALU.add).then_inc(arg_made.sem, 1)
                            dve.wait_ge(turned.sem, turned.at(i + 1))
                            dve.tensor_scalar(kdec[:, i, :], bank[2 + y][:, 0:P], tok[:, 0, DE + i:DE + i + 1], None,
                                              ALU.mult).then_inc(kdec_made.sem, 1)
                        if i >= 1:
                            h, y = i - 1, (i - 1) % 2
                            dve.wait_ge(paired.sem, paired.at(h + 1))
                            dve.wait_ge(decayed.sem, decayed.at(2 * h + 2))
                            pair = bank[4 + y][:, 0:4 * P].rearrange("p (a x c) -> p a x c", a=2, x=2)
                            dve.tensor_tensor(LT[:, 2 * h:2 * h + 2, :], pair[:, 0, :, :], decay[:, y, :, :],
                                              ALU.mult).then_inc(coupled.sem, 1)
                            dve.tensor_tensor(k[:, h, :].rearrange("p (x c) -> p x c", x=2), pair[:, 1, :, :],
                                              decay[:, y, :, :], ALU.mult).then_inc(coupled.sem, 1)
                            dve.tensor_tensor(q[:, h, C:2 * C], q[:, h, C:2 * C], eg[:, y, :],
                                              ALU.mult).then_inc(coupled.sem, 1)

                @block.scalar
                def _(act):
                    for i in range(H):
                        y = i % 2
                        act.wait_ge(arg_made.sem, arg_made.at(2 * i + 2))
                        if i >= 2:
                            act.wait_ge(coupled.sem, coupled.at(3 * (i - 1)))
                        act.activation(decay[:, y, :, :], decay[:, y, :, :], ACT.Exp).then_inc(decayed.sem, 1)
                        act.activation(eg[:, y, :], bank[y][:, C:2 * C], ACT.Exp).then_inc(decayed.sem, 1)
                        act.wait_ge(kdec_made.sem, kdec_made.at(i + 1))
                        act.activation(kbe[:, i, :], bank[2 + y][:, P:2 * P], ACT.Copy,
                                       scale=tok[:, 1, BE + i:BE + i + 1]).then_inc(taken.sem, 1)
                        for x in range(2):
                            act.activation(v[:, i, x * C:(x + 1) * C], bank[2 + y][:, (2 + x) * P:(3 + x) * P], ACT.Copy,
                                           scale=tok[:, x, B + i:B + i + 1]).then_inc(taken.sem, 1)
            for s, n in ((spread, H), (turned, H), (kb_made, H), (arg_made, 2 * H), (decayed, 2 * H), (paired, H),
                         (kdec_made, H), (coupled, 3 * H), (taken, 3 * H)):
                s.passed(n)

        with ExitStack() as inner:
            T = sbuf(inner, "inverse", [P, 2 * H, C])
            Lo = sbuf(inner, "coupling_level", [P, 2 * H, C])
            LoT = sbuf(inner, "lo_t", [P, 2 * H, C // 2])
            masked, lo_t, lo_t_out = sig("level_masked"), sig("lo_t_done"), sig("lo_t_out")
            delta, updated, t_turned, tt_out = sig("delta_done"), sig("t_updated"), sig("t_turned"), sig("tt_out")
            begun = sig("inverse_begun")
            groups, levels = 4, 7
            with nc.Block() as block:
                @block.gpsimd
                def _(pool):
                    for l in range(levels):
                        for g in range(groups):
                            if l:
                                pool.wait_ge(lo_t.sem, lo_t.at((l - 1) * groups + g + 1))
                            u = slice(4 * g, 4 * g + 4)
                            pool.tensor_tensor(Lo[:, u, :], LT[:, u, :],
                                               con("levels", l * P, P).unsqueeze(1).broadcast_to([P, 4, P]),
                                               ALU.mult).then_inc(masked.sem, 1)

                @block.vector
                def _(dve):
                    for m in (T, TT):
                        dve.tensor_copy(m[:, :, :], ident.unsqueeze(1).broadcast_to([P, 2 * H, P])).then_inc(begun.sem, 1)
                    dve.wait_ge(begun.sem, begun.at(2))
                    for l in range(levels):
                        s = 1 << l
                        for g in range(groups):
                            dve.wait_ge(delta.sem, delta.at(l * groups + g + 1))
                            left = T[:, 4 * g:4 * g + 4, :].rearrange("p u (b two s) -> p (u b) two s", two=2, s=s)
                            dve.tensor_tensor(left[:, :, 0, :], left[:, :, 0, :],
                                              bank[4 + g][:, 0:2 * P].rearrange("p (b s) -> p b s", s=s),
                                              ALU.subtract).then_inc(updated.sem, 1)

                @block.tensor
                def _(pe):
                    pe.wait_ge(begun.sem, begun.at(2))
                    for l in range(levels):
                        s = 1 << l
                        for g in range(groups):
                            pe.wait_ge(masked.sem, masked.at(l * groups + g + 1))
                            if l:
                                pe.wait_ge(tt_out.sem, tt_out.at((l - 1) * groups + g + 1))
                            for u in range(4):
                                left = T[:, 4 * g + u, :].rearrange("p (b two s) -> p b two s", two=2, s=s)[:, :, 0, :]
                                last = pe.matmul(bank[g][:, u * 64:(u + 1) * 64], Lo[:, 4 * g + u, :], left,
                                                 start=True, stop=True)
                            last.then_inc(lo_t.sem, 1)
                        for g in range(groups):
                            pe.wait_ge(lo_t_out.sem, lo_t_out.at(l * groups + g + 1))
                            if l:
                                pe.wait_ge(updated.sem, updated.at((l - 1) * groups + g + 1))
                            for u in range(4):
                                last = pe.matmul(bank[4 + g][:, u * 64:(u + 1) * 64], TT[:, 4 * g + u, :],
                                                 LoT[:, 4 * g + u, :], start=True, stop=True)
                            last.then_inc(delta.sem, 1)
                        for g in range(groups):
                            pe.wait_ge(updated.sem, updated.at(l * groups + g + 1))
                            for u in range(4):
                                last = pe.transpose(bank[g][:, u * P:(u + 1) * P], T[:, 4 * g + u, :], ident)
                            last.then_inc(t_turned.sem, 1)

                @block.scalar
                def _(act):
                    for l in range(levels):
                        for g in range(groups):
                            act.wait_ge(lo_t.sem, lo_t.at(l * groups + g + 1))
                            act.activation(LoT[:, 4 * g:4 * g + 4, :],
                                           bank[g][:, 0:2 * P].rearrange("p (u c) -> p u c", u=4),
                                           ACT.Copy).then_inc(lo_t_out.sem, 1)
                        for g in range(groups):
                            act.wait_ge(t_turned.sem, t_turned.at(l * groups + g + 1))
                            act.activation(TT[:, 4 * g:4 * g + 4, :],
                                           bank[g][:, 0:4 * P].rearrange("p (u c) -> p u c", u=4),
                                           ACT.Copy).then_inc(tt_out.sem, 1)
            for s in (masked, lo_t, lo_t_out, delta, updated, t_turned, tt_out):
                s.passed(levels * groups)
            begun.passed(2)

        with ExitStack() as inner:
            vn0, vn1, S1, wT = (sbuf(inner, n, [P, H, P]) for n in ("v_new0", "v_new1", "state1", "neg_w_T"))
            r1, r1_out, r2, r2_out, r3, r3_out, r4, r4_out = (
                sig(n) for n in ("u0_w1", "u0_w1_out", "state_done", "state_out", "v1_done", "v1_out", "o_done", "o_out"))
            with nc.Block() as block:
                @block.tensor
                def _(pe):
                    for i in range(H + 3):
                        if i < H:
                            y = i % 2
                            if i >= 2:
                                pe.wait_ge(r1_out.sem, r1_out.at(2 * (i - 1)))
                            pe.matmul(bank[y][:, 0:P], TT[:, 2 * i, :], v[:, i, 0:C], start=True, stop=True)
                            pe.matmul(bank[y][:, P:2 * P], kbe[:, i, :], TT[:, 2 * i + 1, :], start=True,
                                      stop=True).then_inc(r1.sem, 1)
                        if 1 <= i <= H:
                            h, y = i - 1, (i - 1) % 2
                            pe.wait_ge(r1_out.sem, r1_out.at(2 * h + 2))
                            if h >= 2:
                                pe.wait_ge(r2_out.sem, r2_out.at(h - 1))
                            pe.matmul(bank[2 + y][:, 0:P], kdec[:, h, :], vn0[:, h, :], start=True,
                                      stop=True).then_inc(r2.sem, 1)
                        if 2 <= i <= H + 1:
                            h, y = i - 2, i % 2
                            pe.wait_ge(r2_out.sem, r2_out.at(h + 1))
                            if h >= 2:
                                pe.wait_ge(r3_out.sem, r3_out.at(h - 1))
                            pe.matmul(bank[4 + y][:, 0:P], TT[:, 2 * h + 1, :], v[:, h, C:2 * C], start=True, stop=False)
                            pe.matmul(bank[4 + y][:, 0:P], wT[:, h, :], S1[:, h, :], start=False,
                                      stop=True).then_inc(r3.sem, 1)
                        if i >= 3:
                            h, y = i - 3, (i - 3) % 2
                            pe.wait_ge(r3_out.sem, r3_out.at(h + 1))
                            if h >= 2:
                                pe.wait_ge(r4_out.sem, r4_out.at(h - 1))
                            pe.matmul(bank[6 + y][:, 0:C], vn0[:, h, :], k[:, h, 0:C], start=True, stop=True)
                            pe.matmul(bank[6 + y][:, C:2 * C], S1[:, h, :], q[:, h, C:2 * C], start=True, stop=False)
                            pe.matmul(bank[6 + y][:, C:2 * C], vn1[:, h, :], k[:, h, C:2 * C], start=False,
                                      stop=True).then_inc(r4.sem, 1)

                @block.scalar
                def _(act):
                    for i in range(H + 3):
                        if i < H:
                            act.wait_ge(r1.sem, r1.at(i + 1))
                            act.activation(vn0[:, i, :], bank[i % 2][:, 0:P], ACT.Copy).then_inc(r1_out.sem, 1)
                            act.activation(wT[:, i, :], bank[i % 2][:, P:2 * P], ACT.Copy,
                                           scale=-1.0).then_inc(r1_out.sem, 1)
                        if 1 <= i <= H:
                            act.wait_ge(r2.sem, r2.at(i))
                            act.activation(S1[:, i - 1, :], bank[2 + (i - 1) % 2][:, 0:P],
                                           ACT.Copy).then_inc(r2_out.sem, 1)

                @block.vector
                def _(dve):
                    for i in range(2, H + 3):
                        if i <= H + 1:
                            h = i - 2
                            dve.wait_ge(r3.sem, r3.at(h + 1))
                            dve.tensor_copy(vn1[:, h, :], bank[4 + h % 2][:, 0:P]).then_inc(r3_out.sem, 1)
                        if i >= 3:
                            h = i - 3
                            dve.wait_ge(r4.sem, r4.at(h + 1))
                            dve.tensor_copy(q[:, h, :], bank[6 + h % 2][:, 0:2 * C]).then_inc(r4_out.sem, 1)
            for s, n in ((r1, H), (r1_out, 2 * H), (r2, H), (r2_out, H), (r3, H), (r3_out, H), (r4, H), (r4_out, H)):
                s.passed(n)


def rope_angles(nc, sbuf, sig, sin_cos, pos_d, con):
    import math
    pos_in, step = sig("pos_in"), sig("angle_step")
    two_pi_hi = 6.28125
    two_pi_lo = 2 * math.pi - two_pi_hi
    rounder = 1.5 * 2.0 ** 23
    top = 3.1415925
    with ExitStack() as scope:
        pos = sbuf(scope, "positions", [P, SEQ], mybir.dt.int32)
        a = sbuf(scope, "angles", [P, 4, SEQ])
        with nc.Block() as block:
            @block.sync
            def _(sp):
                sp.dma_start(pos[:, :], pos_d).then_inc(pos_in.sem, 16)

            @block.vector
            def _(dve):
                count = [0]

                def then(ins):
                    count[0] += 1
                    ins.then_inc(step.sem, 1)
                    dve.wait_ge(step.sem, step.at(count[0]))
                dve.wait_ge(pos_in.sem, pos_in.at(16))
                ang, turns, s, c = (a[:, i, :] for i in range(4))
                then(dve.tensor_copy(ang, pos[:, :]))
                then(dve.tensor_scalar(ang, ang, con("inv_freq"), None, ALU.mult))
                then(dve.tensor_scalar(turns, ang, 1 / (2 * math.pi), rounder, ALU.mult, ALU.add))
                then(dve.tensor_scalar(turns, turns, rounder, None, ALU.subtract))
                then(dve.scalar_tensor_tensor(ang, turns, -two_pi_hi, ang, ALU.mult, ALU.add))
                then(dve.scalar_tensor_tensor(ang, turns, -two_pi_lo, ang, ALU.mult, ALU.add))
                then(dve.tensor_scalar(s, ang, top, -top, ALU.min, ALU.max))
                then(dve.tensor_scalar(c, ang, math.pi / 2, None, ALU.add))
                then(dve.tensor_scalar(turns, c, top, -2 * math.pi, ALU.is_gt, ALU.mult))
                then(dve.tensor_tensor(c, c, turns, ALU.add))
                then(dve.tensor_scalar(c, c, top, -top, ALU.min, ALU.max))

            @block.scalar
            def _(act):
                act.wait_ge(step.sem, step.at(11))
                act.activation(sin_cos[:, 0, :], a[:, 2, :], ACT.Sin)
                act.activation(sin_cos[:, 1, :], a[:, 3, :], ACT.Sin)
        pos_in.passed(16)
        step.passed(11)


def rotate(nc, sbuf, sig, bank, parts, sin_cos, con):
    rotated, sined, cosined, summed = sig("rotated"), sig("sined"), sig("cosined"), sig("rope_summed")
    tiles = [(part, t) for part, n in parts for t in range(n)]
    with ExitStack() as scope:
        other = sbuf(scope, "rope_other", [P, len(tiles), SEQ])
        with nc.Block() as block:
            @block.tensor
            def _(pe):
                for i, (x, t) in enumerate(tiles):
                    pe.matmul(bank[i][:, 0:SEQ], con("rotate"), x[:, t, :], start=True, stop=True).then_inc(rotated.sem, 1)

            @block.vector
            def _(dve):
                for i, (x, t) in enumerate(tiles):
                    dve.wait_ge(rotated.sem, rotated.at(i + 1))
                    dve.tensor_tensor(other[:, i, :], bank[i][:, 0:SEQ], sin_cos[:, 0, :], ALU.mult).then_inc(sined.sem, 1)
                    dve.tensor_tensor(x[:, t, :], x[:, t, :], sin_cos[:, 1, :], ALU.mult).then_inc(cosined.sem, 1)
                    dve.wait_ge(sined.sem, sined.at(i + 1))
                    dve.wait_ge(cosined.sem, cosined.at(i + 1))
                    dve.tensor_tensor(x[:, t, :], x[:, t, :], other[:, i, :], ALU.add).then_inc(summed.sem, 1)
    for s in (rotated, sined, cosined, summed):
        s.passed(len(tiles))


def _blocks(w, k_tiles, tiles):
    import numpy as np
    k, n = w.shape
    full = np.zeros((k_tiles * P, -(-n // P) * P), np.float32)
    full[:k, :n] = w
    b = full.reshape(k_tiles, P, -1, P).transpose(2, 0, 1, 3)
    items = b.reshape(-1, tiles, k_tiles, P, P).transpose(0, 3, 1, 2, 4)
    return np.ascontiguousarray(items).reshape(items.shape[0], P, tiles * k_tiles * P)


def _halves(w):
    import numpy as np
    k, n = w.shape
    full = np.zeros((FF_TILES * P, n), np.float32)
    full[:k] = w
    b = full.reshape(2, HALF_FF, P, n // P, P).transpose(3, 0, 2, 1, 4)
    return np.ascontiguousarray(b).reshape(-1, P, HALF_FF * P)


def _pairs(a, b):
    import numpy as np
    n = FF_TILES * P
    fa, fb = np.zeros((D, n), np.float32), np.zeros((D, n), np.float32)
    fa[:, :a.shape[1]], fb[:, :b.shape[1]] = a, b
    both = np.stack([fa.reshape(D, FF_TILES, P), fb.reshape(D, FF_TILES, P)], axis=2)
    return _blocks(both.reshape(D, 2 * n), KD, 2)


def _cols(v):
    return v.reshape(-1, P).T


def _layout(x):
    import numpy as np
    d_ff = x["ffn_w_down"].shape[1]
    w = {}
    ada = np.concatenate([x["ada_w_2"][0], x["ada_w_2"][1]], axis=1)
    w["ada"] = np.ascontiguousarray(ada.T.reshape(MOD_ITEMS, 2, P, D).transpose(0, 2, 1, 3)).reshape(MOD_ITEMS, P, 2 * D)
    w["a_in"] = _blocks(x["a_w_in"][0], KD, 2)
    w["a_out"] = _blocks(x["a_w_out"][0], KD, 2)
    for l in range(2):
        w[f"up{l}"] = _pairs(x["ffn_w_up"][l][:, :d_ff], x["ffn_w_up"][l][:, d_ff:])
        w[f"down{l}"] = _halves(x["ffn_w_down"][l])
        w[f"gu{l}"] = _pairs(x["ffn_w_gate_2"][l], x["ffn_w_up_2"][l])
        w[f"dn{l}"] = _halves(x["ffn_w_down_2"][l])
    w["kv"] = _blocks(x["kv_w"][:, :2 * D], KD, 2)
    w["fg"] = _blocks(x["kv_w"][:, 2 * D:], KD, 1)
    w["b_q"] = _blocks(x["b_w_q"][0], KD, 2)
    w["b_out"] = _blocks(x["b_w_out"][0], KD, 2)
    gw = x["gdn_w_in_2"][0]
    w["gdn_qkv"] = _blocks(gw[:, :3 * D], KD, 2)
    w["gdn_gate"] = _blocks(gw[:, 3 * D:4 * D], KD, 2)
    ab = np.zeros((D, P), np.float32)
    ab[:, 0:HEADS], ab[:, 32:32 + HEADS] = gw[:, 4 * D:4 * D + HEADS], gw[:, 4 * D + HEADS:]
    w["gdn_ab"] = _blocks(ab, KD, 1)
    w["gdn_out"] = _blocks(x["gdn_w_out_2"][0], KD, 2)
    mi = x["mla_w_in_2"][0]
    w["mla_in"] = _blocks(np.concatenate([mi, mi[:, 640:704]], axis=1), KD, 2)
    uq = x["mla_w_uq_2"][0].reshape(384, HEADS, 192)
    w["uq"] = _blocks(np.concatenate([uq[:, :, :128].reshape(384, -1), uq[:, :, 128:].reshape(384, -1)], axis=1), 3, 4)
    ukv = x["mla_w_ukv_2"][0].reshape(256, HEADS, 256)
    w["ukv"] = _blocks(np.concatenate([ukv[:, :, :128].reshape(256, -1), ukv[:, :, 128:].reshape(256, -1)], axis=1), 2, 4)
    w["mla_out"] = _blocks(x["mla_w_out_2"][0], KD, 2)

    params = np.zeros((P, NPARAM), np.float32)

    def put(name, v, at=0):
        params[:v.shape[0], PCOL[name] + at:PCOL[name] + at + v.shape[1]] = v
    for l in range(2):
        for i in range(4):
            put("gains", _cols(x["norm_gains"][l, i]), (4 * l + i) * KD)
        for t in range(3):
            for half in range(2):
                v = np.zeros(FF_TILES * P, np.float32)
                v[:d_ff] = x["ffn_conv"][l, t, half * d_ff:(half + 1) * d_ff]
                put("conv", _cols(v), ((l * 3 + t) * 2 + half) * FF_TILES)
        put("norm_mix", _cols(x["norm_mix_g_2"][l]), l * KD)
        put("norm_ffn", _cols(x["norm_ffn_g_2"][l]), l * KD)
        put("ada_b", _cols(x["ada_b_2"][l]), l * 6 * KD)
        put("lb", _cols(x["a_lb_logits"][l]), l * KD)
    put("kv_norm", _cols(x["kv_norm"]))
    put("head_norm", _cols(x["a_head_norm"][0]))
    put("fg_b", x["fg_b"].reshape(-1, 1))
    put("final", _cols(x["final_norm_g_2"]))
    put("gdn_conv", x["gdn_conv_w_2"][0].reshape(3 * HEADS, P, 4).transpose(1, 0, 2).reshape(P, -1))
    put("gdn_norm", _cols(x["gdn_norm_g_2"][0]))
    put("q_norm", _cols(x["mla_q_norm_g_2"][0]))
    put("kv_norm2", _cols(x["mla_kv_norm_g_2"][0]))
    put("a_log", x["gdn_a_log_2"][0].reshape(-1, 1))
    put("dt_bias", x["gdn_dt_bias_2"][0].reshape(-1, 1))

    tokens = np.concatenate([x["meta_tokens"], x["x"][0]], axis=0)
    hT = np.ascontiguousarray(tokens.T.reshape(KD, P, T1).transpose(1, 0, 2))
    pos = np.ascontiguousarray(np.broadcast_to(x["positions_2"].astype(np.int32), (P, SEQ)))
    c = np.ascontiguousarray(np.broadcast_to(x["c_2"], (P, D)))
    return w, params, hT, c, pos


def _constants():
    import numpy as np
    c = np.zeros((P, NCONST), np.float32)

    def put(name, v):
        c[:, CCOL[name]:CCOL[name] + dict(CONSTS)[name]] = v
    row, col = np.arange(P)[:, None], np.arange(P)[None, :]
    put("ident", np.eye(P))
    put("ones", 1.0)
    put("causal_qk", np.where(col <= row, 0.0, NEG))
    put("causal_kq", np.where(row <= col, 0.0, NEG))
    put("chunk_kq", (row <= col) & (row // 64 == col // 64))
    levels = [(row // (2 * s) == col // (2 * s)) & (row % (2 * s) < s) & (col % (2 * s) >= s)
              for s in (1, 2, 4, 8, 16, 32, 64)]
    put("levels", np.concatenate(levels, axis=1))
    put("rotate", np.where((col % 64 < 32) & (row == col + 32), -1.0, np.where((col % 64 >= 32) & (row == col - 32), 1.0, 0.0)))
    t = np.arange(T1)
    put("reset_hgrn", np.broadcast_to((t != 0) & ((t < META) | ((t - META) % 64 != 0)), (P, T1)))
    t = np.arange(SEQ)
    put("reset_gdn", np.broadcast_to(t % P != 0, (P, SEQ)))
    put("ones_row", 1.0)
    exponent = (np.arange(P) % 32 * 2).astype(np.float64) / 64
    put("inv_freq", (10000.0 ** -exponent)[:, None])
    return c


def kernel(**inputs):
    import numpy as _np
    import concourse.bacc as _bacc
    from concourse.bass_utils import run_bass_kernel_spmd as _run

    nc = _bacc.Bacc("TRN2", target_bir_lowering=False, num_devices=1)
    w, params, hT, c, pos = _layout({k: _np.asarray(v) for k, v in inputs.items()})
    arrays = {f"w_{name}": a for name, a in w.items()}
    arrays |= {"params": params, "consts": _constants(), "hT": hT, "c": c, "pos": pos}
    aps = {n: nc.dram_tensor(n, a.shape, mybir.dt.from_np(a.dtype), kind="ExternalInput").ap()
           for n, a in arrays.items()}
    out = nc.dram_tensor("out", (P, KD, SEQ), F32, kind="ExternalOutput").ap()
    fused_model(nc, {name: aps[f"w_{name}"] for name in w}, aps["params"], aps["consts"], aps["hT"], aps["c"], aps["pos"], out)
    r = _run(nc, [arrays], core_ids=[0])
    got = r.results[0]["out"]
    return _np.ascontiguousarray(got.transpose(2, 1, 0).reshape(1, SEQ, D))
```

```python
from contextlib import ExitStack

import concourse.bass as bass
from concourse import mybir

F32 = mybir.dt.float32
F32R = mybir.dt.float32r
ALU = mybir.AluOpType
ACT = mybir.ActivationFunctionType
AX = mybir.AxisListType

P = 128
D = 1024
KD = D // P
META = 16
SEQ = 256
T1 = META + SEQ
HEADS = 8
FOX_HEADS = 16
FF_TILES = 22
HALF_FF = FF_TILES // 2
CONV_LEAD = 2
EPS = 1e-6
NEG = -1e30
SLOTS = 4
LEAD = 3
ITEM = 16 * P

PARAMS = [("gains", 8 * KD), ("kv_norm", KD), ("head_norm", KD), ("lb", 2 * KD), ("conv", 2 * 3 * 2 * FF_TILES),
          ("fg_b", 1), ("norm_mix", 2 * KD), ("norm_ffn", 2 * KD), ("final", KD), ("ada_b", 2 * 6 * KD),
          ("gdn_conv", 4 * 3 * HEADS), ("gdn_norm", 1), ("q_norm", 3), ("kv_norm2", 2), ("a_log", 1), ("dt_bias", 1)]
PCOL, _at = {}, 0
for _name, _n in PARAMS:
    PCOL[_name] = _at
    _at += _n
NPARAM = _at

CONSTS = [("ident", P), ("ones", P), ("causal_qk", P), ("causal_kq", P), ("chunk_kq", P), ("levels", 7 * P),
          ("rotate", P), ("reset_hgrn", T1), ("reset_gdn", SEQ), ("ones_row", T1), ("inv_freq", 1)]
CCOL, _at = {}, 0
for _name, _n in CONSTS:
    CCOL[_name] = _at
    _at += _n
NCONST = _at

STREAM = ([("a_in", 16, 16), ("a_out", 4, 16), ("up0", 22, 16), ("down0", 16, 11)]
          + [("kv", 8, 16), ("fg", 1, 8), ("b_q", 4, 16), ("b_out", 4, 16), ("up1", 22, 16), ("down1", 16, 11)]
          + [("gdn_qkv", 12, 16), ("gdn_gate", 4, 16), ("gdn_ab", 1, 8), ("gdn_out", 4, 16), ("gu0", 22, 16), ("dn0", 16, 11)]
          + [("mla_in", 3, 16), ("uq", 3, 12), ("ukv", 4, 8), ("mla_out", 4, 16), ("gu1", 22, 16), ("dn1", 16, 11)])
MOD_HOSTS, _at = {}, 0
for _name, _n, _every in (("a_in", 16, 2), ("a_out", 4, 1), ("down0", 16, 2), ("kv", 8, 1), ("b_q", 4, 1),
                          ("b_out", 4, 1), ("down1", 16, 2), ("gdn_gate", 4, 1)):
    MOD_HOSTS[_name] = (_at, _every)
    _at += _n // _every
MOD_ITEMS = 48
assert _at == MOD_ITEMS


class Signal:

    def __init__(self, ctx, nc, name):
        self.sem = ctx.enter_context(nc.semaphore(name))
        self.base = 0

    def at(self, n):
        return self.base + n

    def passed(self, n):
        self.base += n


def fused_model(nc, w, params_d, consts_d, hT_d, c_d, pos_d, out_d):
    with ExitStack() as ctx:
        def sbuf(c, name, shape, dt=F32):
            return c.enter_context(nc.sbuf_tensor(name, shape, dt))

        params = sbuf(ctx, "feature_params", [P, NPARAM])
        consts = sbuf(ctx, "constants", [P, NCONST])
        h = sbuf(ctx, "h", [P, KD, T1])
        rstd = sbuf(ctx, "rstd", [P, T1])
        std = sbuf(ctx, "std", [P, T1])
        work = sbuf(ctx, "work", [P, KD, T1])
        mod = sbuf(ctx, "mod", [P, 2, 6, KD])
        modf = mod[:, :, :, :].rearrange("p l s k -> p (l s k)")
        mod_sum = sbuf(ctx, "mod_sum", [P, 2, 2])
        c_row = sbuf(ctx, "c_row", [P, D])
        raw = sbuf(ctx, "raw", [P, SLOTS, ITEM])
        w_hi = sbuf(ctx, "w_hi", [P, SLOTS, ITEM], F32R)
        w_lo = sbuf(ctx, "w_lo", [P, SLOTS, ITEM], F32R)
        bank = [ctx.enter_context(nc.psum_tensor(f"bank{i}", [P, 512], F32)) for i in range(8)]

        sigs = {}

        def sig(name):
            if name not in sigs:
                sigs[name] = Signal(ctx, nc, name)
            return sigs[name]

        def par(name, i=0, n=1, p0=0, p1=P):
            if isinstance(i, int):
                return params[p0:p1, PCOL[name] + i:PCOL[name] + i + n]
            return params[p0:p1, bass.ds(i + PCOL[name], n)]

        def con(name, c0=0, n=None, p0=0, p1=P):
            n = dict(CONSTS)[name] - c0 if n is None else n
            return consts[p0:p1, CCOL[name] + c0:CCOL[name] + c0 + n]

        ident, ones = con("ident"), con("ones")

        raw_loaded = [ctx.enter_context(nc.semaphore(f"raw_loaded{s}")) for s in range(SLOTS)]
        hi_split = sig("hi_split")
        lo_split = sig("lo_split")
        item_done = sig("item_done")
        item_out = sig("item_out")
        starts, at = {}, 0
        for name, n, blocks in STREAM:
            starts[name] = (at, n, blocks)
            at += n
        ring_end = at

        mod_turns = [0, 0]

        def item_of(r):
            for name, (first, n, blocks) in starts.items():
                if first <= r < first + n:
                    return name, first, n, blocks

        def each(eng, lo, hi, body, head=2):
            i = lo
            while i < hi and (i % SLOTS or i - lo < head):
                body(i, i % SLOTS, i // SLOTS)
                i += 1
            turns = (hi - i) // SLOTS
            if turns >= 2:
                with eng.Fori(0, turns) as t:
                    for s in range(SLOTS):
                        body(t * SLOTS + (i + s), s, t + i // SLOTS)
                i += turns * SLOTS
            while i < hi:
                body(i, i % SLOTS, i // SLOTS)
                i += 1

        def load(sp, name, r, s):
            first, n, blocks = starts[name]
            if not isinstance(r, int) or r >= SLOTS:
                sp.wait_ge(lo_split.sem, r - (SLOTS - 1))
            sp.dma_start(raw[:, s, 0:blocks * P], w[name][r - first, :, :]).then_inc(raw_loaded[s], 16)

        mod_w = w["ada"]
        mod_loaded = [ctx.enter_context(nc.semaphore(f"mod_loaded{s}")) for s in range(2)]
        mod_used = sig("mod_used")
        mod_made = sig("mod_made")

        def mod_load(sp, room, a, s):
            sp.dma_start(room[:, s, :, :], mod_w[a, :, :].rearrange("p (t k) -> p t k", t=2)).then_inc(mod_loaded[s], 16)

        def mod_column(dve, room, a, s, turn):
            dve.wait_ge(mod_loaded[s], (turn + 1) * 16)
            for t in range(2):
                last = dve.tensor_tensor_reduce(out=room[:, s, t, :], in0=room[:, s, t, :], in1=c_row[:, :], scale=1.0,
                                                scalar=0.0, op0=ALU.mult, op1=ALU.add,
                                                accum_out=mod_sum[:, s, t:t + 1])
            last.then_inc(mod_used.sem, 1)
            dve.wait_ge(mod_used.sem, a + 1)
            at = a * 2
            d = modf[:, at:at + 2] if isinstance(at, int) else modf[:, bass.ds(at, 2)]
            dve.tensor_tensor(d, mod_sum[:, s, :], par("ada_b", at, 2), ALU.add)

        def split_hi(act, r, s, turn, blocks):
            act.wait_ge(raw_loaded[s], (turn + 1) * 16)
            if not isinstance(r, int) or r >= SLOTS:
                act.wait_ge(item_done.sem, r - (SLOTS - 1))
            act.activation(w_hi[:, s, 0:blocks * P], raw[:, s, 0:blocks * P], ACT.Copy).then_inc(hi_split.sem, 1)

        def split_lo(dve, r, s, turn, blocks):
            dve.wait_ge(hi_split.sem, r + 1)
            dve.tensor_tensor(w_lo[:, s, 0:blocks * P], raw[:, s, 0:blocks * P],
                              w_hi[:, s, 0:blocks * P].bitcast(F32), ALU.subtract).then_inc(lo_split.sem, 1)

        def split_ahead(eng, split, r, s, turn, last, blocks):
            if not isinstance(r, int):
                split(eng, r + LEAD, (s + LEAD) % SLOTS, turn + (s + LEAD) // SLOTS, blocks)
            elif r + LEAD < ring_end:
                split(eng, r + LEAD, (s + LEAD) % SLOTS, turn + (s + LEAD) // SLOTS, item_of(r + LEAD)[3])

        def steps(eng, name, step, head=2):
            first, n, blocks = starts[name]
            cut = max(first, first + n - LEAD)
            each(eng, first, cut, step, head)
            for r in range(cut, first + n):
                step(r, r % SLOTS, r // SLOTS)

        def product(name, tiles, k_tiles, x_hi, x_lo, cols, act_out=None, dve_out=None, pool_out=None, halves=False,
                    signals=(), dve_late=None, act_late=None, entry=None, sums=None, sqrt_next=False):
            first, n, blocks = starts[name]
            width = cols[1] - cols[0]

            def where(r, s, t):
                if halves:
                    return bank[((s - first) % SLOTS) // 2]
                return bank[4 * (s % 2) + t]

            mod_first, every = MOD_HOSTS.get(name, (0, 0))
            hosts = n // every if every else 0
            ahead = LEAD + SLOTS
            with ExitStack() as inner, nc.Block() as block:
                if hosts:
                    room = sbuf(inner, f"mod_w_{name}", [P, 2, 2, D])
                if sums:
                    act_out = branch_out(name, tiles, sums, sbuf(inner, f"branch_sq_{name}", [P, 4, T1]), halves)
                    sq = act_out.squares
                head = 4 if sums else 2

                def mod_at(s, turn):
                    slot = (s - first) % SLOTS // every % 2
                    i = turn * (SLOTS // every) + (s - first) // every
                    turns = turn * (SLOTS // every // 2) + (s - first - every * slot) // (2 * every)
                    return i + mod_first, slot, turns + mod_turns[slot]

                @block.sync
                def _(sp):
                    def step(r, s, turn):
                        if not isinstance(r, int):
                            load(sp, name, r + ahead, (s + ahead) % SLOTS)
                        elif r + ahead < ring_end:
                            load(sp, item_of(r + ahead)[0], r + ahead, (s + ahead) % SLOTS)
                        local = (s - first) % SLOTS
                        if hosts and local % every == 0:
                            a, slot, _ = mod_at(s, turn)
                            if not isinstance(a, int) or a + 2 < mod_first + hosts:
                                sp.wait_ge(mod_used.sem, a + 1)
                                mod_load(sp, room, a + 2, slot)
                    for i in range(min(2, hosts)):
                        mod_load(sp, room, mod_first + i, i)
                    if first == 0:
                        for r in range(SLOTS, ahead):
                            load(sp, name, r, r % SLOTS)
                    cut = max(first, first + n - ahead)
                    each(sp, first, cut, step)
                    for r in range(cut, first + n):
                        step(r, r % SLOTS, r // SLOTS)

                @block.scalar
                def _(act):
                    def step(r, s, turn):
                        early = not act_late or isinstance(r, int) and r == first + n - 1
                        if early:
                            split_ahead(act, split_hi, r, s, turn, first + n, blocks)
                        if act_out:
                            act_out(act, r - first, (s - first) % SLOTS, lambda t: where(r, s, t))
                        if not early:
                            split_ahead(act, split_hi, r, s, turn, first + n, blocks)
                        if act_late:
                            act_late(act, r - first, (s - first) % SLOTS, lambda t: where(r, s, t))
                    if entry:
                        entry.act(act)
                    if sqrt_next:
                        act.activation(std[:, 0:1], eps_col[:, 0:1], ACT.Sqrt)
                    steps(act, name, step, head)

                @block.vector
                def _(dve):
                    def step(r, s, turn):
                        early = not act_late or isinstance(r, int) and r == first + n - 1
                        if early:
                            split_ahead(dve, split_lo, r, s, turn, first + n, blocks)
                        local = (s - first) % SLOTS
                        if hosts and local % every == 0:
                            mod_column(dve, room, *mod_at(s, turn))
                        if dve_out:
                            dve_out(dve, r - first, (s - first) % SLOTS, lambda t: where(r, s, t))
                        if not early:
                            split_ahead(dve, split_lo, r, s, turn, first + n, blocks)
                        if dve_late:
                            dve_late(dve, r - first, (s - first) % SLOTS, lambda t: where(r, s, t))
                    if entry:
                        entry.dve(dve)
                    steps(dve, name, step)

                @block.gpsimd
                def _(pool):
                    if entry and entry.pool:
                        entry.pool(pool)
                    if pool_out:
                        each(pool, first, first + n,
                             lambda r, s, turn: pool_out(pool, r - first, (s - first) % SLOTS))

                @block.tensor
                def _(pe):
                    def step(r, s, turn):
                        i = r
                        pe.wait_ge(lo_split.sem, i + 1)
                        if not halves:
                            if not isinstance(i, int) or i >= 2:
                                pe.wait_ge(item_out.sem, i - 1)
                        elif (s - first) % 2 == 0:
                            pe.wait_ge(item_out.sem, i - 2)
                        k0 = HALF_FF * ((s - first) % 2) if halves else 0
                        for t in range(tiles):
                            o = where(r, s, t)[:, 0:width]
                            for k in range(k_tiles):
                                b = slice((t * k_tiles + k) * P, (t * k_tiles + k + 1) * P)
                                xk = k0 + k
                                begin = xk == 0
                                end = xk == (FF_TILES if halves else k_tiles) - 1
                                if entry and isinstance(r, int) and r == first and t == 0:
                                    pe.wait_ge(entry.split.sem, entry.split.at(k + 1))
                                pe.matmul(o, w_hi[:, s, b], x_hi[:, xk, cols[0]:cols[1]], start=begin, stop=False)
                                pe.matmul(o, w_hi[:, s, b], x_lo[:, xk, cols[0]:cols[1]], start=False, stop=False)
                                last = pe.matmul(o, w_lo[:, s, b], x_hi[:, xk, cols[0]:cols[1]], start=False,
                                                 stop=end)
                        last.then_inc(item_done.sem, 1)
                        local = (s - first) % SLOTS
                        j = r - first
                        if sums and halves and local % 2 == 0 and (not isinstance(r, int) or j >= 2):
                            at = turn * (SLOTS // 2) + (s - first - 2) // 2
                            add_up(at, (local // 2 + 1) % 2)
                        if sums and not halves and j >= 1:
                            for t in range(tiles):
                                add_up((j - 1) * tiles + t, (j - 1) % 2 * 2 + t)

                    def add_up(t, slot):
                        pe.wait_ge(branch_squared.sem, branch_squared.at(t + 1))
                        pe.matmul(bank[7][:, 0:width], ones, sq[:, slot, 0:width], start=isinstance(t, int) and t == 0,
                                  stop=isinstance(t, int) and t == KD - 1).then_inc(branch_summed.sem, 1)
                    if entry:
                        entry.pe(pe)
                    each(pe, first, first + n, step, head)
                    if sums:
                        for t in range(KD - (1 if halves else tiles), KD):
                            add_up(t, 1 if halves else (n - 1) % 2 * 2 + t % 2)
            for i in range(2):
                mod_turns[i] += (hosts + 1 - i) // 2
            if sums:
                branch_squared.passed(KD)
                branch_summed.passed(KD)
            if entry:
                entry.passed()
            for name_, count in signals:
                sig(name_).passed(count)

        branch_squared, branch_summed = sig("branch_squared"), sig("branch_summed")

        def branch_out(name, tiles, cols, squares, halves):
            width = cols[1] - cols[0]

            def out(act, j, s, where):
                if halves and s % 2 == 0:
                    return
                item_ready(act, name, j)
                far = not isinstance(j, int) or j >= 4 or (not halves and j >= 2)
                if far:
                    back = (j - 1) // 2 - 1 if halves else (j - 1) * tiles
                    act.wait_ge(branch_summed.sem, branch_summed.at(back))
                for t in range(tiles):
                    at = (j - 1) // 2 if halves else j * tiles + t
                    d = work[:, at, cols[0]:cols[1]] if isinstance(at, int) else work[:, bass.ds(at, 1), cols[0]:cols[1]]
                    act.activation(d, where(t)[:, 0:width], ACT.Copy)
                    slot = s // 2 if halves else j % 2 * 2 + t
                    last = act.activation(squares[:, slot, 0:width], where(t)[:, 0:width], ACT.Square)
                    last.then_inc(branch_squared.sem, 1)
                act.wait_ge(branch_squared.sem, branch_squared.at((j + 1) // 2 if halves else (j + 1) * tiles))
                act.sem_inc(item_out.sem, 2 if halves else 1)
            out.squares = squares
            return out

        def item_ready(eng, name, j):
            eng.wait_ge(item_done.sem, j + (starts[name][0] + 1))

        def copy_out(name, tiles, dst, tile0, width, func=ACT.Copy, scale=1.0):
            def out(act, j, s, where):
                item_ready(act, name, j)
                for t in range(tiles):
                    at = j * tiles + (tile0 + t)
                    d = dst[:, at, 0:width] if isinstance(at, int) else dst[:, bass.ds(at, 1), 0:width]
                    last = act.activation(d, where(t)[:, 0:width], func, scale=scale)
                last.then_inc(item_out.sem, 1)
            return out

        class NormEntry:

            def __init__(self, src, n, cols, gain, x_hi, x_lo, shift=None, residual=None, stats=True, count=D,
                         act_first=None, dve_first=None, act_then=None, dve_then=None):
                names = ("std_made", "rstd_made", "weighed", "h_added", "squared", "summed", "x_made", "x_high",
                         "x_split")
                std_made, rstd_made, weighed, h_added, squared, summed, x_made, x_high, x_split = map(sig, names)
                c0, c1 = cols
                self.split = x_split
                self.made = x_made
                normed = residual is not None and residual[1]
                self.pool = None
                roots = int(normed) + int(stats)
                self.counts = ((std_made, roots), (rstd_made, roots), (weighed, n * normed),
                               (h_added, n if residual else 0), (squared, n * stats), (summed, int(stats)),
                               (x_made, n if gain else 0), (x_high, n if x_hi is not None else 0),
                               (x_split, n if x_hi is not None else 0))

                def act(act):
                    if normed:
                        act.activation(std[:, c0:c1], bank[7][:, 0:c1 - c0], ACT.Sqrt, scale=1.0 / D,
                                       bias=eps_col[:, 0:1]).then_inc(std_made.sem, 1)
                    if stats:
                        for k in range(n):
                            if residual:
                                act.wait_ge(h_added.sem, h_added.at(k + 1))
                            act.activation(work[:, k, c0:c1], src(k), ACT.Square).then_inc(squared.sem, 1)
                        if act_first:
                            act_first(act)
                        act.wait_ge(summed.sem, summed.at(1))
                        act.activation(std[:, c0:c1], bank[6][:, 0:c1 - c0], ACT.Sqrt, scale=1.0 / count,
                                       bias=eps_col[:, 0:1]).then_inc(std_made.sem, 1)
                    if x_hi is not None:
                        for k in range(n):
                            if gain:
                                act.wait_ge(x_made.sem, x_made.at(k + 1))
                            x = work[:, k, c0:c1] if gain else src(k)
                            if shift:
                                ins = act.activation(x_hi[:, k, c0:c1], x, ACT.Identity, bias=shift(k))
                            else:
                                ins = act.activation(x_hi[:, k, c0:c1], x, ACT.Copy)
                            ins.then_inc(x_high.sem, 1)
                    if act_then:
                        act_then(act)

                def dve(dve):
                    roots = [0]

                    def invert():
                        roots[0] += 1
                        dve.wait_ge(std_made.sem, std_made.at(roots[0]))
                        dve.reciprocal(rstd[:, c0:c1], std[:, c0:c1]).then_inc(rstd_made.sem, 1)
                        dve.wait_ge(rstd_made.sem, rstd_made.at(roots[0]))

                    def add(k):
                        dve.wait_ge(weighed.sem, weighed.at(k + 1))
                        dve.tensor_tensor(h[:, k, c0:c1], h[:, k, c0:c1], work[:, k, c0:c1],
                                          ALU.add).then_inc(h_added.sem, 1)

                    def low(k):
                        dve.wait_ge(x_high.sem, x_high.at(k + 1))
                        x = work[:, k, c0:c1] if gain else src(k)
                        hi = x_hi[:, k, c0:c1].bitcast(F32)
                        if shift:
                            ins = dve.scalar_tensor_tensor(x_lo[:, k, c0:c1], x, shift(k), hi, ALU.add, ALU.subtract)
                        else:
                            ins = dve.tensor_tensor(x_lo[:, k, c0:c1], x, hi, ALU.subtract)
                        ins.then_inc(x_split.sem, 1)
                    if normed:
                        invert()
                        for k in range(n):
                            dve.scalar_tensor_tensor(work[:, k, c0:c1], work[:, k, c0:c1], residual[0](k),
                                                     rstd[:, c0:c1], ALU.mult, ALU.mult).then_inc(weighed.sem, 1)
                            if k:
                                add(k - 1)
                        add(n - 1)
                    elif residual:
                        for k in range(n):
                            dve.scalar_tensor_tensor(h[:, k, c0:c1], work[:, k, c0:c1], residual[0](k),
                                                     h[:, k, c0:c1], ALU.mult, ALU.add).then_inc(h_added.sem, 1)
                    if dve_first:
                        dve_first(dve)
                    if stats:
                        if residual:
                            dve.wait_ge(h_added.sem, h_added.at(n))
                        invert()
                    for k in range(n):
                        if gain:
                            dve.scalar_tensor_tensor(work[:, k, c0:c1], src(k), gain(k), rstd[:, c0:c1],
                                                     ALU.mult, ALU.mult).then_inc(x_made.sem, 1)
                        if k and x_hi is not None:
                            low(k - 1)
                    if x_hi is not None:
                        low(n - 1)
                    if dve_then:
                        dve_then(dve)

                def pe(pe):
                    if stats:
                        for k in range(n):
                            pe.wait_ge(squared.sem, squared.at(k + 1))
                            last = pe.matmul(bank[6][:, 0:c1 - c0], ones, work[:, k, c0:c1], start=k == 0,
                                             stop=k == n - 1)
                        last.then_inc(summed.sem, 1)
                self.act, self.dve, self.pe = act, dve, pe

            def passed(self):
                for s_, n_ in self.counts:
                    s_.passed(n_)

        class HeadNormEntry:

            def __init__(self, o, n, width, gain, gate, x_hi, x_lo, head_sq):
                names = ("head_squared", "head_summed", "head_logged", "head_rstd", "head_gated", "head_normed", "x_high",
                         "x_split")
                squared, summed, logged, ready, gated, normed, high, x_split = map(sig, names)
                self.split = x_split
                self.counts = [(s_, n) for s_ in (squared, summed, logged, ready, gated, normed, high, x_split)]

                def act(act):
                    def high_part(k):
                        act.wait_ge(normed.sem, normed.at(k + 1))
                        act.activation(x_hi[:, k, 0:width], work[:, k, 0:width], ACT.Copy).then_inc(high.sem, 1)
                    for k in range(n):
                        act.activation(head_sq[:, k, :], o[:, k, :], ACT.Square).then_inc(squared.sem, 1)
                    for k in range(n):
                        act.wait_ge(summed.sem, summed.at(k + 1))
                        act.activation(head_sq[:, k, :], bank[k][:, 0:width], ACT.Ln, scale=1.0 / P,
                                       bias=eps_col[:, 0:1]).then_inc(logged.sem, 1)
                    for k in range(n):
                        act.wait_ge(logged.sem, logged.at(k + 1))
                        act.activation(head_sq[:, k, :], head_sq[:, k, :], ACT.Exp, scale=-0.5).then_inc(ready.sem, 1)
                        if k >= 2:
                            high_part(k - 2)
                    high_part(n - 2)
                    high_part(n - 1)

                def pool(pool):
                    for k in range(n):
                        pool.tensor_tensor(work[:, k, 0:width], o[:, k, :], gate(k), ALU.mult).then_inc(gated.sem, 1)

                def pe(pe):
                    for k in range(n):
                        pe.wait_ge(squared.sem, squared.at(k + 1))
                        pe.matmul(bank[k][:, 0:width], ones, head_sq[:, k, :], start=True,
                                  stop=True).then_inc(summed.sem, 1)

                def dve(dve):
                    def low(k):
                        dve.wait_ge(high.sem, high.at(k + 1))
                        dve.tensor_tensor(x_lo[:, k, 0:width], work[:, k, 0:width], x_hi[:, k, 0:width].bitcast(F32),
                                          ALU.subtract).then_inc(x_split.sem, 1)

                    def norm(k):
                        dve.wait_ge(ready.sem, ready.at(k + 1))
                        dve.wait_ge(gated.sem, gated.at(k + 1))
                        dve.scalar_tensor_tensor(work[:, k, 0:width], work[:, k, 0:width], gain(k), head_sq[:, k, :],
                                                 ALU.mult, ALU.mult).then_inc(normed.sem, 1)
                    for k in range(n):
                        norm(k)
                        if k >= 2:
                            low(k - 2)
                    low(n - 2)
                    low(n - 1)
                self.act, self.dve, self.pe, self.pool = act, dve, pe, pool

            def passed(self):
                for s_, n_ in self.counts:
                    s_.passed(n_)

        eps_col = sbuf(ctx, "eps_col", [P, 1])

        h_in, params_in, consts_in, c_in = sig("h_in"), sig("params_in"), sig("consts_in"), sig("c_in")
        c_ready = sig("c_ready")
        with nc.Block() as block:
            @block.sync
            def _(sp):
                sp.dma_start(h[:, :, :], hT_d).then_inc(h_in.sem, 16)
                sp.dma_start(params[:, :], params_d).then_inc(params_in.sem, 16)
                sp.dma_start(consts[:, :], consts_d).then_inc(consts_in.sem, 16)
                for r in range(LEAD):
                    load(sp, "a_in", r, r % SLOTS)
                sp.dma_start(c_row[:, :], c_d).then_inc(c_in.sem, 16)
                load(sp, "a_in", LEAD, LEAD)

            @block.vector
            def _(dve):
                dve.memset(eps_col[:, :], EPS)

            @block.scalar
            def _(act):
                act.wait_ge(h_in.sem, 16)

            @block.tensor
            def _(pe):
                pe.wait_ge(consts_in.sem, 16)

        def modulation_scales():
            with nc.Block() as block:
                @block.vector
                def _(dve):
                    for layer in range(2):
                        for part, gains in ((1, "norm_mix"), (4, "norm_ffn")):
                            dve.scalar_tensor_tensor(mod[:, layer, part, :], mod[:, layer, part, :], 1.0,
                                                     par(gains, layer * KD, KD), ALU.add, ALU.mult)

        gain1 = lambda layer, i: (lambda k: par("gains", (4 * layer + i) * KD + k))

        def up_product(layer, x_hi, x_lo, a_hi, a_lo, cols, up, conv, phase, entry):
            lead = 0 if cols[0] == 0 else CONV_LEAD * conv
            width_in = cols[1] - cols[0]
            width = width_in - lead
            gate = sbuf(phase, f"gate_{up}", [P, 2, width])
            value = sbuf(phase, f"value_{up}", [P, 2, width])
            act_s = sbuf(phase, f"act_{up}", [P, 2, width])
            tapped, conved, silued, multiplied, high, halved = (sig("tapped"), sig("conved"), sig("silued"),
                                                                sig("multiplied"), sig("a_high"), sig("a_split"))
            first, n, _ = starts[up]
            taps = 4 if conv else 0

            def act_out(act, j, s, where):
                item_ready(act, up, j)
                if not conv:
                    return
                if not isinstance(j, int) or j >= 2:
                    act.wait_ge(multiplied.sem, multiplied.at(j - 1))
                for t, dst in ((0, gate), (1, value)):
                    act.activation(dst[:, s % 2, :], where(t)[:, lead:width_in], ACT.Copy,
                                   scale=par("conv", j + ((layer * 3 + 2) * 2 + t) * FF_TILES)).then_inc(tapped.sem, 1)

            def dve_out(dve, j, s, where):
                if not conv:
                    return
                for tap in (1, 0):
                    back = 2 - tap
                    skip = max(0, back - lead)
                    for t, dst in ((0, gate), (1, value)):
                        if tap == 1:
                            dve.wait_ge(tapped.sem, tapped.at(j * 2 + (t + 1)))
                        else:
                            dve.wait_ge(conved.sem, conved.at(j * 4 + (t + 1)))
                        d = dst[:, s % 2, skip:width]
                        last = dve.scalar_tensor_tensor(
                            d, where(t)[:, lead + skip - back:width_in - back],
                            par("conv", j + ((layer * 3 + tap) * 2 + t) * FF_TILES), d, ALU.mult, ALU.add)
                        last.then_inc(conved.sem, 1)

            def act_late(act, j, s, where):
                if conv:
                    act.wait_ge(conved.sem, conved.at(j * 4 + 3))
                if not isinstance(j, int) or j >= 2:
                    act.wait_ge(multiplied.sem, multiplied.at(j - 1))
                src = gate[:, s % 2, :] if conv else where(0)[:, 0:width]
                act.activation(act_s[:, s % 2, :], src, ACT.Silu).then_inc(silued.sem, 1)

            def dve_late(dve, j, s, where):
                dve.wait_ge(silued.sem, silued.at(j + 1))
                if conv:
                    dve.wait_ge(conved.sem, conved.at(j * 4 + 4))
                if not isinstance(j, int) or j >= 2:
                    dve.wait_ge(halved.sem, halved.at(j - 1))
                src = value[:, s % 2, :] if conv else where(1)[:, 0:width]
                dve.tensor_tensor(prod[:, s % 2, :], act_s[:, s % 2, :], src, ALU.mult).then_inc(multiplied.sem, 1)

            def pool_out(pool, j, s):
                pool.wait_ge(multiplied.sem, multiplied.at(j + 1))
                hi = a_hi[:, j, :] if isinstance(j, int) else a_hi[:, bass.ds(j, 1), :]
                lo = a_lo[:, j, :] if isinstance(j, int) else a_lo[:, bass.ds(j, 1), :]
                pool.tensor_copy(hi, prod[:, s % 2, :]).then_inc(high.sem, 1)
                pool.wait_ge(high.sem, high.at(j + 1))
                pool.tensor_tensor(lo, prod[:, s % 2, :], hi.bitcast(F32), ALU.subtract).then_inc(halved.sem, 1)

            prod = sbuf(phase, f"prod_{up}", [P, 2, width])

            if conv:
                def dve_conv(dve, j, s, where):
                    dve_out(dve, j, s, where)
                    dve.wait_ge(conved.sem, conved.at(j * 4 + 4))
                    dve.sem_inc(item_out.sem, 1)
                product(up, 2, KD, x_hi, x_lo, cols, act_out=act_out, dve_out=dve_conv, pool_out=pool_out,
                        act_late=act_late, dve_late=dve_late, entry=entry,
                        signals=(("tapped", 2 * n), ("conved", 4 * n), ("silued", n), ("multiplied", n),
                                 ("a_high", n), ("a_split", n)))
            else:
                def dve_plain(dve, j, s, where):
                    dve_late(dve, j, s, where)
                    dve.wait_ge(multiplied.sem, multiplied.at(j + 1))
                    dve.sem_inc(item_out.sem, 1)
                product(up, 2, KD, x_hi, x_lo, cols, act_out=lambda a, j, s, wh: (act_out(a, j, s, wh),
                                                                                act_late(a, j, s, wh)),
                        dve_out=dve_plain, pool_out=pool_out, entry=entry,
                        signals=(("silued", n), ("multiplied", n), ("a_high", n), ("a_split", n)))

        def down_product(down, a_hi, a_lo, out, sums):
            def act_out(act, j, s, where):
                if s % 2 == 1:
                    item_ready(act, down, j)
                    at = (j - 1) // 2
                    d = work[:, at, out[0]:out[1]] if isinstance(at, int) else work[:, bass.ds(at, 1), out[0]:out[1]]
                    act.activation(d, where(0)[:, 0:out[1] - out[0]], ACT.Copy).then_inc(item_out.sem, 2)
            product(down, 1, HALF_FF, a_hi, a_lo, (0, out[1] - out[0]), act_out=None if sums else act_out, halves=True,
                    sums=sums and out, sqrt_next=True)

        with ExitStack() as outer:
            qfig = sbuf(outer, "qfig", [P, 4 * KD, T1])
            with ExitStack() as phase:
                x_hi, x_lo = sbuf(phase, "x_hi_a", [P, KD, T1], F32R), sbuf(phase, "x_lo_a", [P, KD, T1], F32R)

                def first_high(act):
                    split_hi(act, 0, 0, 0, starts["a_in"][2])

                def high_then(act):
                    for r in range(1, LEAD):
                        split_hi(act, r, r, 0, starts["a_in"][2])
                    act.wait_ge(c_in.sem, 16)
                    act.activation(c_row[:, :], c_row[:, :], ACT.Silu).then_inc(c_ready.sem, 1)

                def first_low(dve):
                    dve.wait_ge(params_in.sem, 16)
                    split_lo(dve, 0, 0, 0, starts["a_in"][2])

                def low_then(dve):
                    for r in range(1, LEAD):
                        split_lo(dve, r, r, 0, starts["a_in"][2])
                    dve.wait_ge(c_ready.sem, 1)
                entry = NormEntry(lambda k: h[:, k, :], KD, (0, T1), gain1(0, 0), x_hi, x_lo, act_first=first_high,
                                  dve_first=first_low, act_then=high_then, dve_then=low_then)

                def a_in_out(act, j, s, where):
                    item_ready(act, "a_in", j)
                    for t in range(2):
                        at = j * 2 + t
                        d = qfig[:, at, :] if isinstance(at, int) else qfig[:, bass.ds(at, 1), :]
                        last = act.activation(d, where(t)[:, 0:T1], ACT.Copy)
                    last.then_inc(item_out.sem, 1)
                product("a_in", 2, KD, x_hi, x_lo, (0, T1), act_out=a_in_out, entry=entry)

            q, f, v, g = (qfig[:, i * KD:(i + 1) * KD, :] for i in range(4))
            hgrn2(nc, sbuf, sig, bank, q, f, v, g, work, par, con, ident)
            with ExitStack() as phase:
                x_hi, x_lo = sbuf(phase, "x_hi_b", [P, KD, T1], F32R), sbuf(phase, "x_lo_b", [P, KD, T1], F32R)
                entry = HeadNormEntry(v, HEADS, T1, lambda k: par("head_norm", k), lambda k: g[:, k, :], x_hi, x_lo, q)
                product("a_out", 2, KD, x_hi, x_lo, (0, T1), entry=entry, sums=(0, T1), sqrt_next=True)

        def ffn_layer(layer, cols, gain, up, down, residual, conv, shift=None):
            width = cols[1] - cols[0] - (CONV_LEAD if conv and cols[0] else 0)
            out = (cols[1] - width, cols[1])
            with ExitStack() as phase:
                a_hi = sbuf(phase, f"a_hi_{up}", [P, FF_TILES, width], F32R)
                a_lo = sbuf(phase, f"a_lo_{up}", [P, FF_TILES, width], F32R)
                with ExitStack() as inner:
                    x_hi = sbuf(inner, f"x_hi_{up}", [P, KD, T1], F32R)
                    x_lo = sbuf(inner, f"x_lo_{up}", [P, KD, T1], F32R)
                    entry = NormEntry(lambda k: h[:, k, cols[0]:cols[1]], KD, cols, gain, x_hi, x_lo, shift=shift,
                                      residual=residual)
                    up_product(layer, x_hi, x_lo, a_hi, a_lo, cols, up, conv, inner, entry)
                down_product(down, a_hi, a_lo, out, sums=bool(conv))

        ffn_layer(0, (0, T1), gain1(0, 2), "up0", "down0", (gain1(0, 1), True), 1)

        late = (META - CONV_LEAD, T1)
        real = (META, T1)
        with ExitStack() as outer:
            kv = sbuf(outer, "kv", [P, 2 * KD, T1])
            qf = sbuf(outer, "q_fox", [P, KD, T1])
            zf = sbuf(outer, "zf", [P, T1])
            with ExitStack() as phase:
                x_hi, x_lo = sbuf(phase, "x_hi_c", [P, KD, T1], F32R), sbuf(phase, "x_lo_c", [P, KD, T1], F32R)
                entry = NormEntry(lambda k: h[:, k, :], KD, (0, T1), lambda k: par("kv_norm", k), x_hi, x_lo,
                                  residual=(gain1(0, 3), True))
                product("kv", 2, KD, x_hi, x_lo, (0, T1), act_out=copy_out("kv", 2, kv, 0, T1), entry=entry)

                def fg_out(act, j, s, where):
                    item_ready(act, "fg", j)
                    act.activation(zf[0:FOX_HEADS, :], where(0)[0:FOX_HEADS, 0:T1], ACT.Identity,
                                   bias=par("fg_b", p1=FOX_HEADS)).then_inc(item_out.sem, 1)
                product("fg", 1, KD, x_hi, x_lo, (0, T1), act_out=fg_out)
                entry = NormEntry(lambda k: h[:, k, :], KD, (0, T1), gain1(1, 0), x_hi, x_lo, stats=False)
                product("b_q", 2, KD, x_hi, x_lo, (0, T1), act_out=copy_out("b_q", 2, qf, 0, T1, scale=0.125), entry=entry)
            with ExitStack() as phase:
                v_tok = sbuf(phase, "v_tok", [P, 3, D])
                c_tok = sbuf(phase, "c_tok", [P, 3, FOX_HEADS])
                neg_c = sbuf(phase, "neg_c", [FOX_HEADS, T1])
                fox_gates(nc, sbuf, sig, bank, zf, neg_c, c_tok, con, ident)
                chunks = [(0, META), (META, P), (META + P, P)]
                to_token_major(nc, sig, bank, lambda t: kv[:, KD + t, :], KD, chunks, v_tok, ident)

                def logits(pe, h_, out, q0, qn, kn):
                    p0 = 64 * (h_ % 2)
                    pe.matmul(out, qf[p0:p0 + 64, h_ // 2, q0:q0 + qn], kv[p0:p0 + 64, h_ // 2, 0:kn],
                              start=True, stop=False)
                    return pe.matmul(out, con("ident", h_, 1, 0, FOX_HEADS).broadcast_to([FOX_HEADS, qn]),
                                     neg_c[:, 0:kn], start=False, stop=True)
                attention(nc, sbuf, sig, bank, "fox", FOX_HEADS, 64, chunks, logits, v_tok, qf, con, ident,
                          row_add=lambda c, h_, n: c_tok[0:n, c, h_:h_ + 1])
            with ExitStack() as phase:
                x_hi, x_lo = sbuf(phase, "x_hi_d", [P, KD, T1], F32R), sbuf(phase, "x_lo_d", [P, KD, T1], F32R)
                entry = NormEntry(lambda k: qf[:, k, late[0]:late[1]], KD, late, None, x_hi, x_lo, stats=False)
                product("b_out", 2, KD, x_hi, x_lo, late, entry=entry, sums=late, sqrt_next=True)
        ffn_layer(1, late, gain1(1, 2), "up1", "down1", (gain1(1, 1), True), 1)
        modulation_scales()

        modcol = lambda layer, part: (lambda k: mod[:, layer, part, k:k + 1])
        with ExitStack() as outer:
            qkvg = sbuf(outer, "qkvg", [P, 4 * HEADS, SEQ])
            ab = sbuf(outer, "ab", [P, SEQ])
            with ExitStack() as phase:
                x_hi, x_lo = sbuf(phase, "x_hi_e", [P, KD, T1], F32R), sbuf(phase, "x_lo_e", [P, KD, T1], F32R)
                u = sbuf(phase, "u_gdn", [P, 4, SEQ])
                entry = NormEntry(lambda k: h[:, k, META:T1], KD, real, modcol(0, 1), x_hi, x_lo,
                                  shift=modcol(0, 0), residual=(gain1(1, 3), True))
                gdn_in_product(sig, starts, product, item_ready, item_out, x_hi, x_lo, real, qkvg, u, par, entry)

                def ab_out(act, j, s, where):
                    item_ready(act, "gdn_ab", j)
                    act.activation(ab[:, :], where(0)[:, 0:SEQ], ACT.Copy).then_inc(item_out.sem, 1)
                product("gdn_ab", 1, KD, x_hi, x_lo, real, act_out=ab_out)
            delta_rule(nc, sbuf, sig, bank, qkvg, ab, work, par, con, ident, ones, eps_col)
            o = qkvg[:, 0:HEADS, :]
            with ExitStack() as phase:
                x_hi, x_lo = sbuf(phase, "x_hi_f", [P, KD, T1], F32R), sbuf(phase, "x_lo_f", [P, KD, T1], F32R)
                head_sq = sbuf(phase, "head_sq_f", [P, HEADS, SEQ])
                entry = HeadNormEntry(o, HEADS, SEQ, lambda k: par("gdn_norm"), lambda k: qkvg[:, 3 * HEADS + k, :],
                                      x_hi, x_lo, head_sq)
                product("gdn_out", 2, KD, x_hi, x_lo, (0, SEQ), act_out=copy_out("gdn_out", 2, work[:, :, META:T1], 0, SEQ),
                        entry=entry, sqrt_next=True)
        ffn_layer(0, real, modcol(0, 4), "gu0", "dn0", (modcol(0, 2), False), 0, shift=modcol(0, 3))

        with ExitStack() as outer:
            k_nope = sbuf(outer, "k_nope", [P, 2 * HEADS, SEQ])
            q_mla = sbuf(outer, "q_mla", [P, HEADS + HEADS // 2, SEQ])
            latent = sbuf(outer, "latent", [P, 6, SEQ])
            sin_cos = sbuf(outer, "sin_cos", [P, 2, SEQ])
            rope_angles(nc, sbuf, sig, sin_cos, pos_d, con)
            with ExitStack() as phase:
                x_hi, x_lo = sbuf(phase, "x_hi_g", [P, KD, T1], F32R), sbuf(phase, "x_lo_g", [P, KD, T1], F32R)
                entry = NormEntry(lambda k: h[:, k, META:T1], KD, real, modcol(1, 1), x_hi, x_lo,
                                  shift=modcol(1, 0), residual=(modcol(0, 5), False))
                product("mla_in", 2, KD, x_hi, x_lo, real, act_out=copy_out("mla_in", 2, latent, 0, SEQ), entry=entry,
                        sqrt_next=True)
                whole = (0, SEQ)
                entry = NormEntry(lambda k: latent[:, k, :], 3, whole, lambda k: par("q_norm", k), x_hi, x_lo, count=3 * P)
                product("uq", 4, 3, x_hi, x_lo, whole, act_out=copy_out("uq", 4, q_mla, 0, SEQ,
                                                                        scale=float(192 ** -0.5)), entry=entry)
                entry = NormEntry(lambda k: latent[:, 3 + k, :], 2, whole, lambda k: par("kv_norm2", k), x_hi, x_lo,
                                  count=2 * P)
                product("ukv", 4, 2, x_hi, x_lo, whole, act_out=copy_out("ukv", 4, k_nope, 0, SEQ), entry=entry)
            q_rope = q_mla[:, HEADS:HEADS + HEADS // 2, :]
            k_rope = latent[:, 5:6, :]
            rotate(nc, sbuf, sig, bank, [(q_rope, 4), (k_rope, 1)], sin_cos, con)
            o = q_mla[:, 0:HEADS, :]
            with ExitStack() as phase:
                v_tok = sbuf(phase, "v_tok2", [P, 2, D])
                chunks = [(0, P), (P, P)]
                to_token_major(nc, sig, bank, lambda t: k_nope[:, HEADS + t, :], HEADS, chunks, v_tok, ident)

                def logits(pe, h_, out, q0, qn, kn):
                    p0 = 64 * (h_ % 2)
                    pe.matmul(out, q_mla[:, h_, q0:q0 + qn], k_nope[:, h_, 0:kn], start=True, stop=False)
                    return pe.matmul(out, q_rope[p0:p0 + 64, h_ // 2, q0:q0 + qn], k_rope[p0:p0 + 64, 0, 0:kn],
                                     start=False, stop=True)
                attention(nc, sbuf, sig, bank, "mla", HEADS, P, chunks, logits, v_tok, o, con, ident)
            with ExitStack() as phase:
                x_hi, x_lo = sbuf(phase, "x_hi_i", [P, KD, T1], F32R), sbuf(phase, "x_lo_i", [P, KD, T1], F32R)
                entry = NormEntry(lambda k: o[:, k, :], KD, (0, SEQ), None, x_hi, x_lo, stats=False)
                product("mla_out", 2, KD, x_hi, x_lo, (0, SEQ), act_out=copy_out("mla_out", 2, work[:, :, META:T1], 0, SEQ),
                        entry=entry, sqrt_next=True)
        ffn_layer(1, real, modcol(1, 4), "gu1", "dn1", (modcol(1, 2), False), 0, shift=modcol(1, 3))

        entry = NormEntry(lambda k: h[:, k, META:T1], KD, real, lambda k: par("final", k), None, None,
                          residual=(modcol(1, 5), False))
        stored = sig("stored")
        with nc.Block() as block:
            @block.scalar
            def _(act):
                entry.act(act)

            @block.vector
            def _(dve):
                entry.dve(dve)

            @block.tensor
            def _(pe):
                entry.pe(pe)

            @block.sync
            def _(sp):
                for k in range(KD):
                    sp.wait_ge(entry.made.sem, entry.made.at(k + 1))
                    sp.dma_start(out_d[:, k, :], work[:, k, META:T1]).then_inc(stored.sem, 16)
                sp.wait_ge(stored.sem, KD * 16)


def hgrn2(nc, sbuf, sig, bank, q, f, v, g, k, par, con, ident):
    real = (META, T1)
    tiles = [(0, META), (META, P), (META + P, P)]
    n_chunks = SEQ // 64
    with ExitStack() as scope:
        b = sbuf(scope, "log_decay", [P, HEADS, T1])
        e = sbuf(scope, "decay", [P, HEADS, T1])
        k_in = sbuf(scope, "k_in", [P, HEADS, T1])
        lb = sbuf(scope, "lower_bound", [P, 6, KD])
        lb_max, lb_exp, lb_done = sig("lb_max"), sig("lb_exp"), sig("lb_done")
        sigmoided, silued = sig("f_sigmoided"), sig("g_silued")
        f_made, k_made, logged, summed = sig("f_made"), sig("k_made"), sig("f_logged"), sig("b_summed")
        exped, q_in, k_in_made, diffed = sig("b_exped"), sig("q_in"), sig("k_in_made"), sig("b_diffed")
        diff_exped = sig("diff_exped")
        reset = con("reset_hgrn")
        v_tok = sbuf(scope, "v_tok_a", [P, 2, 3, P])
        k_tok = sbuf(scope, "k_tok_a", [P, 2, 3, P])
        attn = sbuf(scope, "attn_a", [P, 2, 3, P])
        state = sbuf(scope, "state_a", [P, 2, n_chunks, P])
        turned, copied, masked = sig("turned"), sig("tok_copied"), sig("attn_masked")
        ds_done, stated, o_done, o_out = sig("ds_done"), sig("stated"), sig("o_done"), sig("o_out")

        def added_to(y, c):
            return bank[y][:, 3 * P:4 * P] if c == 2 else bank[6][:, c * P:(c + 1) * P]

        k_out_made = sig("k_out_made")
        behind = 4
        with nc.Block() as block:
            @block.scalar
            def _(act):
                def take_out(i):
                    if i >= 2:
                        act.wait_ge(o_done.sem, o_done.at(i - 1))
                        act.activation(v[:, i - 2, :], bank[7][:, 0:T1], ACT.Copy).then_inc(o_out.sem, 1)
                    if i < HEADS:
                        y = i % 2
                        act.wait_ge(turned.sem, turned.at(i + 1))
                        for src, dst in ((bank[2 + y], v_tok), (bank[4 + y], k_tok)):
                            act.activation(dst[0:META, y, 0, :], src[0:META, 0:P], ACT.Copy)
                            last = act.activation(dst[:, y, 1:3, :],
                                                  src[:, P:3 * P].rearrange("p (x c) -> p x c", x=2), ACT.Copy)
                        last.then_inc(copied.sem, 1)

                act.wait_ge(lb_max.sem, lb_max.at(3))
                act.activation(lb[:, 1:3, :], lb[:, 1:3, :], ACT.Exp).then_inc(lb_exp.sem, 1)
                for i in range(HEADS):
                    act.activation(f[:, i, :], f[:, i, :], ACT.Sigmoid).then_inc(sigmoided.sem, 1)
                for i in range(HEADS):
                    act.wait_ge(k_made.sem, k_made.at(i + 1))
                    act.activation(f[:, i, :], f[:, i, :], ACT.Ln).then_inc(logged.sem, 1)
                for i in range(HEADS + behind + 2):
                    if i < HEADS:
                        act.wait_ge(summed.sem, summed.at(i + 1))
                        act.activation(e[:, i, :], b[:, i, :], ACT.Exp).then_inc(exped.sem, 1)
                        act.activation(k_in[:, i, :], b[:, i, :], ACT.Exp, scale=-1.0).then_inc(exped.sem, 1)
                    if 0 <= i - 2 < HEADS:
                        h = i - 2
                        act.wait_ge(diffed.sem, diffed.at(2 * h + 2))
                        act.activation(f[:, h, :], f[:, h, :], ACT.Exp).then_inc(diff_exped.sem, 1)
                    if i >= behind:
                        take_out(i - behind)
                    if i >= HEADS + 2:
                        pair = slice((i - HEADS - 2) * 2, (i - HEADS - 1) * 2)
                        act.activation(g[:, pair, :], g[:, pair, :], ACT.Silu).then_inc(silued.sem, 1)

            @block.vector
            def _(dve):
                def mask_and_state(i):
                    if i < HEADS:
                        y = i % 2
                        dve.wait_ge(turned.sem, turned.at(i + 1))
                        if i >= 2:
                            dve.wait_ge(o_done.sem, o_done.at(i - 1))
                        dve.tensor_tensor(attn[0:META, y, 0, 0:META], bank[y][0:META, 0:META],
                                          con("chunk_kq", 0, META, 0, META), ALU.mult)
                        dve.tensor_tensor(attn[:, y, 1:3, :], bank[y][:, P:3 * P].rearrange("p (x c) -> p x c", x=2),
                                          con("chunk_kq").unsqueeze(1).broadcast_to([P, 2, P]),
                                          ALU.mult).then_inc(masked.sem, 1)
                    if i >= 1:
                        h, y = i - 1, (i - 1) % 2
                        dve.wait_ge(ds_done.sem, ds_done.at(h + 1))
                        dve.tensor_copy(state[:, y, 0, :], added_to(y, 0)).then_inc(stated.sem, 1)
                        for c in range(n_chunks - 1):
                            t = META + 64 * c + 63
                            dve.wait_ge(stated.sem, stated.at(n_chunks * h + c + 1))
                            dve.scalar_tensor_tensor(state[:, y, c + 1, :], state[:, y, c, :], e[:, h, t:t + 1],
                                                     added_to(y, c + 1), ALU.mult,
                                                     ALU.add).then_inc(stated.sem, 1)

                l0, l1 = par("lb", 0, KD), par("lb", KD, KD)
                dve.tensor_tensor(lb[:, 0, :], l0, l1, ALU.max).then_inc(lb_max.sem, 1)
                dve.wait_ge(lb_max.sem, lb_max.at(1))
                dve.tensor_tensor(lb[:, 1, :], l0, lb[:, 0, :], ALU.subtract).then_inc(lb_max.sem, 1)
                dve.tensor_tensor(lb[:, 2, :], l1, lb[:, 0, :], ALU.subtract).then_inc(lb_max.sem, 1)
                dve.wait_ge(lb_exp.sem, lb_exp.at(1))
                dve.tensor_tensor(lb[:, 3, :], lb[:, 1, :], lb[:, 2, :], ALU.add).then_inc(lb_done.sem, 1)
                dve.wait_ge(lb_done.sem, lb_done.at(1))
                dve.reciprocal(lb[:, 3, :], lb[:, 3, :]).then_inc(lb_done.sem, 1)
                dve.wait_ge(lb_done.sem, lb_done.at(2))
                dve.tensor_tensor(lb[:, 4, :], lb[:, 1, :], lb[:, 3, :], ALU.mult).then_inc(lb_done.sem, 1)
                dve.wait_ge(lb_done.sem, lb_done.at(3))
                dve.tensor_scalar(lb[:, 5, :], lb[:, 4, :], -1.0, 1.0, ALU.mult, ALU.add).then_inc(lb_done.sem, 1)
                dve.wait_ge(lb_done.sem, lb_done.at(4))
                for i in range(HEADS):
                    dve.wait_ge(sigmoided.sem, sigmoided.at(i + 1))
                    dve.tensor_scalar(f[:, i, :], f[:, i, :], lb[:, 5, i:i + 1], lb[:, 4, i:i + 1], ALU.mult,
                                      ALU.add).then_inc(f_made.sem, 1)
                    dve.wait_ge(f_made.sem, f_made.at(i + 1))
                    dve.tensor_scalar(k[:, i, :], f[:, i, :], -1.0, 1.0, ALU.mult, ALU.add).then_inc(k_made.sem, 1)
                for i in range(1, HEADS + behind + 2):
                    if 0 <= i - 1 < HEADS:
                        h = i - 1
                        dve.wait_ge(logged.sem, logged.at(h + 1))
                        dve.tensor_tensor_scan(b[:, h, :], reset, f[:, h, :], 0.0, ALU.mult,
                                               ALU.add).then_inc(summed.sem, 1)
                    if 0 <= i - 2 < HEADS:
                        h = i - 2
                        dve.wait_ge(summed.sem, summed.at(h + 1))
                        dve.wait_ge(exped.sem, exped.at(2 * h + 2))
                        dve.tensor_tensor(q[:, h, :], q[:, h, :], e[:, h, :], ALU.mult).then_inc(q_in.sem, 1)
                        dve.tensor_tensor(k_in[:, h, :], k_in[:, h, :], k[:, h, :], ALU.mult).then_inc(k_in_made.sem, 1)
                        dve.tensor_tensor(f[:, h, 0:META], b[:, h, META - 1:META].broadcast_to([P, META]),
                                          b[:, h, 0:META], ALU.subtract).then_inc(diffed.sem, 1)
                        chunked = b[:, h, META:T1].rearrange("p (c t) -> p c t", t=64)
                        dve.tensor_tensor(f[:, h, META:T1].rearrange("p (c t) -> p c t", t=64),
                                          chunked[:, :, 63:64].broadcast_to([P, n_chunks, 64]), chunked,
                                          ALU.subtract).then_inc(diffed.sem, 1)
                    if 0 <= i - 4 < HEADS:
                        h = i - 4
                        dve.wait_ge(diff_exped.sem, diff_exped.at(h + 1))
                        dve.tensor_tensor(f[:, h, :], f[:, h, :], k[:, h, :], ALU.mult).then_inc(k_out_made.sem, 1)
                    if i > behind:
                        mask_and_state(i - behind - 1)

            @block.tensor
            def _(pe):
                for i in range(HEADS + 2):
                    if i >= 2:
                        h, y = i - 2, i % 2
                        pe.wait_ge(masked.sem, masked.at(h + 1))
                        pe.wait_ge(stated.sem, stated.at(n_chunks * (h + 1)))
                        if h >= 1:
                            pe.wait_ge(o_out.sem, o_out.at(h))
                        for x, (t0, n) in enumerate(tiles):
                            pe.matmul(bank[7][:, t0:t0 + n], v_tok[0:n, y, x, :], attn[0:n, y, x, 0:n],
                                      start=x == 0, stop=False, skip_group_check=True)
                        for c in range(n_chunks):
                            t = slice(META + 64 * c, META + 64 * c + 64)
                            last = pe.matmul(bank[7][:, t], state[:, y, c, :], q[:, h, t], start=False,
                                             stop=c == n_chunks - 1, skip_group_check=True)
                        last.then_inc(o_done.sem, 1)
                    if i < HEADS:
                        y = i % 2
                        pe.wait_ge(q_in.sem, q_in.at(i + 1))
                        pe.wait_ge(k_in_made.sem, k_in_made.at(i + 1))
                        pe.wait_ge(k_out_made.sem, k_out_made.at(i + 1))
                        if i >= 2:
                            pe.wait_ge(copied.sem, copied.at(i - 1))
                            pe.wait_ge(masked.sem, masked.at(i - 1))
                            pe.wait_ge(stated.sem, stated.at(n_chunks * (i - 1)))
                        for x, (t0, n) in enumerate(tiles):
                            pe.transpose(bank[2 + y][0:n, x * P:(x + 1) * P], v[:, i, t0:t0 + n], ident)
                            pe.transpose(bank[4 + y][0:n, x * P:(x + 1) * P], f[:, i, t0:t0 + n], ident)
                        for x, (t0, n) in enumerate(tiles):
                            last = pe.matmul(bank[y][0:n, x * P:x * P + n], k_in[:, i, t0:t0 + n], q[:, i, t0:t0 + n],
                                             start=True, stop=True)
                        last.then_inc(turned.sem, 1)
                    if 1 <= i <= HEADS:
                        h, y = i - 1, (i - 1) % 2
                        pe.wait_ge(copied.sem, copied.at(h + 1))
                        if h >= 1:
                            pe.wait_ge(stated.sem, stated.at(n_chunks * h))
                        pe.wait_ge(masked.sem, masked.at(h + 1))
                        pe.matmul(added_to(y, 0), k_tok[0:META, y, 0, :], v_tok[0:META, y, 0, :], start=True, stop=True)
                        for c in range(n_chunks - 1):
                            r = slice(64 * (c % 2), 64 * (c % 2) + 64)
                            last = pe.matmul(added_to(y, c + 1), k_tok[r, y, 1 + c // 2, :],
                                             v_tok[r, y, 1 + c // 2, :], start=True, stop=True)
                        last.then_inc(ds_done.sem, 1)
        for s, n in ((lb_max, 3), (lb_exp, 1), (lb_done, 4), (sigmoided, HEADS), (silued, behind), (f_made, HEADS),
                     (k_made, HEADS), (logged, HEADS), (summed, HEADS), (exped, 2 * HEADS), (q_in, HEADS),
                     (k_in_made, HEADS), (diffed, 2 * HEADS), (diff_exped, HEADS), (k_out_made, HEADS)):
            s.passed(n)
        for s, n in ((turned, HEADS), (copied, HEADS), (masked, HEADS), (ds_done, HEADS),
                     (stated, n_chunks * HEADS), (o_done, HEADS), (o_out, HEADS)):
            s.passed(n)


def fox_gates(nc, sbuf, sig, bank, zf, neg_c, c_tok, con, ident):
    n = FOX_HEADS
    a_step, c_step, c_turned = sig("fg_act"), sig("fg_dve"), sig("c_turned")
    with ExitStack() as scope:
        t = sbuf(scope, "fg_room", [n, 3, T1])
        z = zf[0:n, :]
        with nc.Block() as block:
            @block.scalar
            def _(act):
                act.activation(t[:, 0, :], z, ACT.Abs).then_inc(a_step.sem, 1)
                act.wait_ge(a_step.sem, a_step.at(1))
                act.activation(t[:, 0, :], t[:, 0, :], ACT.Exp, scale=-1.0).then_inc(a_step.sem, 1)
                act.wait_ge(a_step.sem, a_step.at(2))
                act.activation(t[:, 0, :], t[:, 0, :], ACT.Ln, bias=1.0).then_inc(a_step.sem, 1)

            @block.vector
            def _(dve):
                dve.wait_ge(a_step.sem, a_step.at(3))
                dve.scalar_tensor_tensor(t[:, 1, :], z, 0.0, t[:, 0, :], ALU.min, ALU.subtract).then_inc(c_step.sem, 1)
                dve.wait_ge(c_step.sem, c_step.at(1))
                dve.tensor_tensor_scan(t[:, 2, :], con("ones_row", p1=n), t[:, 1, :], 0.0, ALU.mult,
                                       ALU.add).then_inc(c_step.sem, 1)
                dve.wait_ge(c_step.sem, c_step.at(2))
                dve.tensor_scalar(neg_c[:, :], t[:, 2, :], -1.0, None, ALU.mult)
                dve.wait_ge(c_turned.sem, c_turned.at(1))
                dve.tensor_copy(c_tok[0:META, 0, :], bank[0][0:META, 0:n])
                dve.tensor_copy(c_tok[:, 1:3, :], bank[0][:, n:3 * n].rearrange("p (x c) -> p x c", x=2))

            @block.tensor
            def _(pe):
                pe.wait_ge(c_step.sem, c_step.at(2))
                for x, (t0, m) in enumerate(((0, META), (META, P), (META + P, P))):
                    last = pe.transpose(bank[0][0:m, x * n:(x + 1) * n], t[:, 2, t0:t0 + m], ident[0:n, 0:n])
                last.then_inc(c_turned.sem, 1)
        a_step.passed(3)
        c_step.passed(2)
        c_turned.passed(1)


def to_token_major(nc, sig, bank, src, n_tiles, chunks, dst, ident):
    turned, copied = sig("tile_turned"), sig("tile_copied")
    with nc.Block() as block:
        @block.tensor
        def _(pe):
            for t in range(n_tiles):
                if t >= 4:
                    pe.wait_ge(copied.sem, copied.at(t - 3))
                for x, (t0, n) in enumerate(chunks):
                    last = pe.transpose(bank[t % 4][0:n, x * P:(x + 1) * P], src(t)[:, t0:t0 + n], ident)
                last.then_inc(turned.sem, 1)

        @block.scalar
        def _(act):
            for t in range(n_tiles):
                act.wait_ge(turned.sem, turned.at(t + 1))
                x = 0
                if chunks[0][1] < P:
                    n = chunks[0][1]
                    act.activation(dst[0:n, 0, t * P:(t + 1) * P], bank[t % 4][0:n, 0:P], ACT.Copy)
                    x = 1
                act.activation(dst[:, x:len(chunks), t * P:(t + 1) * P],
                               bank[t % 4][:, x * P:len(chunks) * P].rearrange("p (x c) -> p x c", c=P),
                               ACT.Copy).then_inc(copied.sem, 1)
    turned.passed(n_tiles)
    copied.passed(n_tiles)


def attention(nc, sbuf, sig, bank, name, n_heads, dv, chunks, logits, v_tok, out, con, ident, row_add=None):
    width = chunks[-1][0] + chunks[-1][1]
    nt = len(chunks)
    offs = [sum(q0 + qn for q0, qn in chunks[:x]) for x in range(nt)]
    cols = offs[-1] + width
    full = [y for y in range(nt) if chunks[y][1] == P]
    per = P // dv
    pt_off, at = {}, 0
    for y in full:
        pt_off[y] = at
        at += width - chunks[y][0]
    pt_cols = at
    small = [y for y in range(nt) if y not in full]
    for y in small:
        pt_off[y] = 0
    scored, maxed, exped, scaled = sig("scored"), sig("maxed"), sig("p_exped"), sig("p_scaled")
    added, inverted = sig("mask_added"), sig("sum_inverted")
    p_turned, pt_copied, pv_done, pv_out = sig("p_turned"), sig("pt_copied"), sig("pv_done"), sig("pv_out")
    with ExitStack() as scope:
        p = sbuf(scope, f"probs_{name}", [P, 3, cols])
        pt = sbuf(scope, f"probs_turned_{name}", [P, 2, pt_cols])
        pt_small = sbuf(scope, f"probs_turned_meta_{name}", [META, 2, width])
        neg_max = sbuf(scope, f"neg_max_{name}", [P, 3, nt])
        row_sum = sbuf(scope, f"row_sum_{name}", [P, 3, nt])
        n_add = nt + (sum(q0 > 0 for q0, _ in chunks) if row_add else 0)

        def pt_of(y, b):
            q0, n = chunks[y]
            if y in small:
                return pt_small[0:n, b, 0:width - q0]
            return pt[:, b, pt_off[y]:pt_off[y] + width - q0]

        with nc.Block() as block:
            @block.tensor
            def _(pe):
                for i in range(n_heads + 3):
                    if i < n_heads:
                        if i >= 2:
                            pe.wait_ge(exped.sem, exped.at(nt * (i - 1)))
                        for x, (q0, qn) in enumerate(chunks):
                            last = logits(pe, i, bank[i % 2][0:qn, offs[x]:offs[x] + q0 + qn], q0, qn, q0 + qn)
                        last.then_inc(scored.sem, 1)
                    if 2 <= i <= n_heads + 1:
                        h, b = i - 2, i % 2
                        pe.wait_ge(scaled.sem, scaled.at(nt * (h + 1)))
                        if h >= 2:
                            pe.wait_ge(pt_copied.sem, pt_copied.at(h - 1))
                        for x, (q0, qn) in enumerate(chunks):
                            for y in range(x + 1):
                                k0, kn = chunks[y]
                                at = pt_off[y] + q0 - k0
                                last = pe.transpose(bank[(4 if y in small else 2) + b][0:kn, at:at + qn],
                                                    p[0:qn, h % 3, offs[x] + k0:offs[x] + k0 + kn], ident[0:qn, 0:qn])
                        last.then_inc(p_turned.sem, 1)
                    if i >= 3:
                        h, b = i - 3, (i - 3) % 2
                        pe.wait_ge(pt_copied.sem, pt_copied.at(h + 1))
                        t, p0 = h // per, dv * (h % per)
                        if t >= 2 and h % per == 0:
                            pe.wait_ge(pv_out.sem, pv_out.at(t - 1))
                        for y, (k0, kn) in enumerate(chunks):
                            last = pe.matmul(bank[6 + t % 2][p0:p0 + dv, k0:width], v_tok[0:kn, y, h * dv:(h + 1) * dv],
                                             pt_of(y, b), start=y == 0, stop=y == nt - 1)
                        last.then_inc(pv_done.sem, 1)

            @block.vector
            def _(dve):
                for i in range(n_heads + 1):
                    if i < n_heads:
                        b = i % 2
                        dve.wait_ge(scored.sem, scored.at(i + 1))
                        n = n_add * i
                        for x, (q0, qn) in enumerate(chunks):
                            s = bank[b][0:qn, offs[x]:offs[x] + q0 + qn]
                            add = row_add(x, i, qn) if row_add else 0.0
                            dve.scalar_tensor_tensor(s[:, q0:q0 + qn], s[:, q0:q0 + qn], add,
                                                     con("causal_qk", 0, qn, 0, qn), ALU.add,
                                                     ALU.add).then_inc(added.sem, 1)
                            n += 1
                            if row_add and q0:
                                dve.tensor_scalar(s[:, 0:q0], s[:, 0:q0], add, None, ALU.add).then_inc(added.sem, 1)
                                n += 1
                        dve.wait_ge(added.sem, added.at(n))
                        for x, (q0, qn) in enumerate(chunks):
                            dve.tensor_reduce(neg_max[0:qn, i % 3, x:x + 1], bank[b][0:qn, offs[x]:offs[x] + q0 + qn],
                                              AX.X, ALU.max, negate=True).then_inc(maxed.sem, 1)
                    if i >= 1:
                        h, b = i - 1, (i - 1) % 2
                        dve.wait_ge(exped.sem, exped.at(nt * (h + 1)))
                        for x, (q0, qn) in enumerate(chunks):
                            dve.reciprocal(row_sum[0:qn, h % 3, x:x + 1],
                                           row_sum[0:qn, h % 3, x:x + 1]).then_inc(inverted.sem, 1)
                        for x, (q0, qn) in enumerate(chunks):
                            dve.wait_ge(inverted.sem, inverted.at(nt * h + x + 1))
                            s = p[0:qn, h % 3, offs[x]:offs[x] + q0 + qn]
                            dve.tensor_scalar(s, s, row_sum[0:qn, h % 3, x:x + 1], None,
                                              ALU.mult).then_inc(scaled.sem, 1)

            @block.scalar
            def _(act):
                for i in range(n_heads + 3):
                    if i < n_heads:
                        b = i % 2
                        if i >= 3:
                            act.wait_ge(p_turned.sem, p_turned.at(i - 2))
                        act.wait_ge(maxed.sem, maxed.at(nt * (i + 1)))
                        for x, (q0, qn) in enumerate(chunks):
                            act.activation(p[0:qn, i % 3, offs[x]:offs[x] + q0 + qn],
                                           bank[b][0:qn, offs[x]:offs[x] + q0 + qn], ACT.Exp,
                                           bias=neg_max[0:qn, i % 3, x:x + 1],
                                           accum_out=row_sum[0:qn, i % 3, x:x + 1]).then_inc(exped.sem, 1)
                    if 2 <= i <= n_heads + 1:
                        h, b = i - 2, i % 2
                        act.wait_ge(p_turned.sem, p_turned.at(h + 1))
                        if h >= 2:
                            act.wait_ge(pv_done.sem, pv_done.at(h - 1))
                        if small:
                            act.activation(pt_of(0, b), bank[4 + b][0:META, 0:width], ACT.Copy)
                        act.activation(pt[:, b, :], bank[2 + b][:, 0:pt_cols], ACT.Copy).then_inc(pt_copied.sem, 1)
                    if i >= 3 and (i - 3) % per == per - 1:
                        t = (i - 3) // per
                        act.wait_ge(pv_done.sem, pv_done.at(i - 2))
                        act.activation(out[:, t, 0:width], bank[6 + t % 2][:, 0:width], ACT.Copy).then_inc(pv_out.sem, 1)
        for s, n in ((scored, n_heads), (maxed, nt * n_heads), (exped, nt * n_heads), (scaled, nt * n_heads),
                     (added, n_add * n_heads), (inverted, nt * n_heads), (p_turned, n_heads),
                     (pt_copied, n_heads), (pv_done, n_heads), (pv_out, n_heads // per)):
            s.passed(n)


def gdn_in_product(sig, starts, product, item_ready, item_out, x_hi, x_lo, real, qkvg, u, par, entry):
    tapped, conved, silued = sig("tapped"), sig("conved"), sig("silued")
    n = starts["gdn_qkv"][1]

    def act_out(act, j, s, where):
        item_ready(act, "gdn_qkv", j)
        if not isinstance(j, int) or j >= 2:
            act.wait_ge(silued.sem, silued.at(j * 2 - 2))
        for t in range(2):
            act.activation(u[:, 2 * (s % 2) + t, :], where(t)[:, 0:SEQ], ACT.Copy,
                           scale=par("gdn_conv", j * 8 + (t * 4 + 3))).then_inc(tapped.sem, 1)

    def dve_out(dve, j, s, where):
        for tap in (2, 1, 0):
            back = 3 - tap
            for t in range(2):
                if tap == 2:
                    dve.wait_ge(tapped.sem, tapped.at(j * 2 + (t + 1)))
                else:
                    dve.wait_ge(conved.sem, conved.at(j * 6 + (2 * (1 - tap) + t + 1)))
                d = u[:, 2 * (s % 2) + t, back:SEQ]
                dve.scalar_tensor_tensor(d, where(t)[:, 0:SEQ - back], par("gdn_conv", j * 8 + (t * 4 + tap)), d,
                                         ALU.mult, ALU.add).then_inc(conved.sem, 1)
        dve.wait_ge(conved.sem, conved.at(j * 6 + 6))
        dve.sem_inc(item_out.sem, 1)

    def act_late(act, j, s, where):
        for t in range(2):
            act.wait_ge(conved.sem, conved.at(j * 6 + (5 + t)))
            at = j * 2 + t
            d = qkvg[:, at, :] if isinstance(at, int) else qkvg[:, bass.ds(at, 1), :]
            act.activation(d, u[:, 2 * (s % 2) + t, :], ACT.Silu).then_inc(silued.sem, 1)
    product("gdn_qkv", 2, KD, x_hi, x_lo, real, act_out=act_out, dve_out=dve_out, act_late=act_late, entry=entry,
            signals=(("tapped", 2 * n), ("conved", 6 * n), ("silued", 2 * n)))

    def gate_out(act, j, s, where):
        item_ready(act, "gdn_gate", j)
        for t in range(2):
            at = j * 2 + (t + 3 * HEADS)
            d = qkvg[:, at, :] if isinstance(at, int) else qkvg[:, bass.ds(at, 1), :]
            last = act.activation(d, where(t)[:, 0:SEQ], ACT.Silu)
        last.then_inc(item_out.sem, 1)
    product("gdn_gate", 2, KD, x_hi, x_lo, real, act_out=gate_out)


def delta_rule(nc, sbuf, sig, bank, qkvg, ab, work, par, con, ident, ones, eps_col):
    H, C = HEADS, P
    q, k, v = qkvg[:, 0:H, :], qkvg[:, H:2 * H, :], qkvg[:, 2 * H:3 * H, :]
    with ExitStack() as scope:
        rows = sbuf(scope, "gate_rows", [P, SEQ])
        tok = sbuf(scope, "gate_tok", [P, 2, P])
        both = sbuf(scope, "coupling_inverse", [P, 2, 2 * H, C])
        LT, TT = both[:, 0, :, :], both[:, 1, :, :]
        kbe = work[:, :, 0:P]
        kdec = work[:, :, P:2 * P]
        G, B, BE, DE = 0, 32, 64, 96
        with ExitStack() as inner:
            t = sbuf(inner, "gate_room", [H, 6, SEQ])
            neg_a = sbuf(inner, "neg_a", [H, 1])
            sq = both[:, :, :, :].rearrange("p a (h x) c -> p a h (x c)", x=2)
            a_step, d_step, z_step = sig("gdn_act"), sig("gdn_dve"), sig("gdn_zero")
            rows_ready, rows_turned = sig("rows_ready"), sig("rows_turned")
            squared, summed, logged, ready = sig("qk_squared"), sig("qk_summed"), sig("qk_logged"), sig("qk_rstd")
            with nc.Block() as block:
                @block.gpsimd
                def _(pool):
                    pool.memset(rows[:, :], 0.0).then_inc(z_step.sem, 1)

                @block.scalar
                def _(act):
                    for a, x in enumerate((q, k)):
                        act.activation(sq[:, a, :, :], x, ACT.Square).then_inc(squared.sem, 1)
                    act.wait_ge(z_step.sem, z_step.at(1))
                    act.activation(rows[B:B + H, :], ab[32:32 + H, :], ACT.Sigmoid).then_inc(a_step.sem, 1)
                    act.activation(t[:, 5, :], ab[32:32 + H, :], ACT.Sigmoid).then_inc(a_step.sem, 1)
                    act.activation(neg_a[:, :], par("a_log", p1=H), ACT.Exp).then_inc(a_step.sem, 1)
                    act.wait_ge(d_step.sem, d_step.at(1))
                    act.activation(t[:, 1, :], t[:, 0, :], ACT.Abs).then_inc(a_step.sem, 1)
                    act.wait_ge(a_step.sem, a_step.at(4))
                    act.activation(t[:, 1, :], t[:, 1, :], ACT.Exp, scale=-1.0).then_inc(a_step.sem, 1)
                    act.wait_ge(a_step.sem, a_step.at(5))
                    act.activation(t[:, 1, :], t[:, 1, :], ACT.Ln, bias=1.0).then_inc(a_step.sem, 1)
                    for h in range(H):
                        act.wait_ge(summed.sem, summed.at(h + 1))
                        o = bank[h][:, 0:2 * SEQ].rearrange("p (a t) -> p a t", a=2)
                        act.activation(sq[:, :, h, :], o, ACT.Ln, bias=eps_col[:, 0:1]).then_inc(logged.sem, 1)
                    for h in range(H):
                        act.wait_ge(logged.sem, logged.at(h + 1))
                        act.activation(sq[:, :, h, :], sq[:, :, h, :], ACT.Exp, scale=-0.5).then_inc(ready.sem, 1)
                    act.wait_ge(d_step.sem, d_step.at(5))
                    act.activation(t[:, 3, :], rows[G:G + H, :], ACT.Exp).then_inc(a_step.sem, 1)
                    act.wait_ge(d_step.sem, d_step.at(6))
                    act.activation(rows[DE:DE + H, :], t[:, 4, :], ACT.Exp).then_inc(a_step.sem, 1)

                @block.vector
                def _(dve):
                    dve.tensor_scalar(t[:, 0, :], ab[0:H, :], par("dt_bias", p1=H), None, ALU.add).then_inc(d_step.sem, 1)
                    dve.wait_ge(a_step.sem, a_step.at(6))
                    dve.wait_ge(d_step.sem, d_step.at(1))
                    dve.scalar_tensor_tensor(t[:, 2, :], t[:, 0, :], 0.0, t[:, 1, :], ALU.max,
                                             ALU.add).then_inc(d_step.sem, 1)
                    dve.tensor_scalar(neg_a[:, :], neg_a[:, :], -1.0, None, ALU.mult).then_inc(d_step.sem, 1)
                    dve.wait_ge(d_step.sem, d_step.at(3))
                    dve.tensor_scalar(t[:, 2, :], t[:, 2, :], neg_a[:, 0:1], None, ALU.mult).then_inc(d_step.sem, 1)
                    dve.wait_ge(d_step.sem, d_step.at(4))
                    dve.wait_ge(z_step.sem, z_step.at(1))
                    dve.tensor_tensor_scan(rows[G:G + H, :], con("reset_gdn", p1=H), t[:, 2, :], 0.0, ALU.mult,
                                           ALU.add).then_inc(d_step.sem, 1)
                    dve.wait_ge(d_step.sem, d_step.at(5))
                    g2 = rows[G:G + H, :].rearrange("p (c t) -> p c t", c=2)
                    dve.tensor_tensor(t[:, 4, :].rearrange("p (c t) -> p c t", c=2),
                                      g2[:, :, C - 1:C].broadcast_to([H, 2, C]), g2,
                                      ALU.subtract).then_inc(d_step.sem, 1)
                    for h in range(H):
                        dve.wait_ge(ready.sem, ready.at(h + 1))
                        dve.scalar_tensor_tensor(q[:, h, :], q[:, h, :], float(P ** -0.5), sq[:, 0, h, :], ALU.mult,
                                                 ALU.mult)
                        dve.tensor_tensor(k[:, h, :], k[:, h, :], sq[:, 1, h, :], ALU.mult)
                    dve.wait_ge(a_step.sem, a_step.at(8))
                    dve.tensor_tensor(rows[BE:BE + H, :], t[:, 3, :], t[:, 5, :], ALU.mult).then_inc(rows_ready.sem, 1)
                    dve.wait_ge(rows_turned.sem, rows_turned.at(1))
                    dve.tensor_copy(tok[:, :, :], bank[6][:, 0:2 * P].rearrange("p (x c) -> p x c", x=2))

                @block.tensor
                def _(pe):
                    pe.wait_ge(squared.sem, squared.at(2))
                    for h in range(H):
                        for a in range(2):
                            last = pe.matmul(bank[h][:, a * SEQ:(a + 1) * SEQ], ones, sq[:, a, h, :], start=True,
                                             stop=True)
                        last.then_inc(summed.sem, 1)
                    pe.wait_ge(logged.sem, logged.at(H))
                    pe.wait_ge(rows_ready.sem, rows_ready.at(1))
                    for x in range(2):
                        last = pe.transpose(bank[6][:, x * P:(x + 1) * P], rows[:, x * C:(x + 1) * C], ident)
                    last.then_inc(rows_turned.sem, 1)
            for s, n in ((a_step, 8), (d_step, 6), (z_step, 1), (rows_ready, 1), (rows_turned, 1), (squared, 2),
                         (summed, H), (logged, H), (ready, H)):
                s.passed(n)

        with ExitStack() as inner:
            kb = sbuf(inner, "k_beta", [P, 2, SEQ])
            decay = sbuf(inner, "pair_decay", [P, 2, 2, C])
            eg = sbuf(inner, "q_decay", [P, 2, C])
            spread, turned = sig("spread"), sig("turned")
            kb_made, arg_made, decayed = sig("kb_made"), sig("decay_arg"), sig("pair_decayed")
            paired, kdec_made, coupled = sig("paired"), sig("kdec_made"), sig("coupled")
            taken = sig("tok_taken")
            with nc.Block() as block:
                @block.tensor
                def _(pe):
                    for i in range(H + 1):
                        if i < H:
                            y = i % 2
                            if i >= 2:
                                pe.wait_ge(arg_made.sem, arg_made.at(2 * (i - 1)))
                                pe.wait_ge(decayed.sem, decayed.at(2 * (i - 1)))
                                pe.wait_ge(taken.sem, taken.at(3 * (i - 1)))
                                pe.wait_ge(kdec_made.sem, kdec_made.at(i - 1))
                            pe.matmul(bank[y][:, 0:SEQ], con("ident", G + i, 1).broadcast_to([P, P]),
                                      rows[:, :], start=True, stop=True)
                            pe.matmul(bank[y][:, SEQ:2 * SEQ], con("ident", B + i, 1).broadcast_to([P, P]),
                                      rows[:, :], start=True, stop=True).then_inc(spread.sem, 1)
                            for n, src in enumerate((k, v)):
                                for x in range(2):
                                    last = pe.transpose(bank[2 + y][:, (2 * n + x) * P:(2 * n + x + 1) * P],
                                                        src[:, i, x * C:(x + 1) * C], ident)
                            last.then_inc(turned.sem, 1)
                        if i >= 1:
                            h, y = i - 1, (i - 1) % 2
                            pe.wait_ge(kb_made.sem, kb_made.at(h + 1))
                            if h >= 2:
                                pe.wait_ge(coupled.sem, coupled.at(3 * (h - 1)))
                            for n, src in enumerate((kb[:, y, :], q[:, h, :])):
                                for x in range(2):
                                    last = pe.matmul(bank[4 + y][:, (2 * n + x) * P:(2 * n + x + 1) * P],
                                                     k[:, h, x * C:(x + 1) * C], src[:, x * C:(x + 1) * C],
                                                     start=True, stop=True)
                            last.then_inc(paired.sem, 1)

                @block.vector
                def _(dve):
                    for i in range(H + 1):
                        if i < H:
                            y = i % 2
                            dve.wait_ge(spread.sem, spread.at(i + 1))
                            if i >= 2:
                                dve.wait_ge(paired.sem, paired.at(i - 1))
                                dve.wait_ge(coupled.sem, coupled.at(3 * (i - 1)))
                            dve.tensor_tensor(kb[:, y, :], k[:, i, :], bank[y][:, SEQ:2 * SEQ],
                                              ALU.mult).then_inc(kb_made.sem, 1)
                            for x in range(2):
                                dve.scalar_tensor_tensor(decay[:, y, x, :], bank[y][:, x * C:(x + 1) * C],
                                                         tok[:, x, G + i:G + i + 1], con("causal_kq"),
                                                         ALU.subtract, ALU.add).then_inc(arg_made.sem, 1)
                            dve.wait_ge(turned.sem, turned.at(i + 1))
                            dve.tensor_scalar(kdec[:, i, :], bank[2 + y][:, 0:P], tok[:, 0, DE + i:DE + i + 1], None,
                                              ALU.mult).then_inc(kdec_made.sem, 1)
                        if i >= 1:
                            h, y = i - 1, (i - 1) % 2
                            dve.wait_ge(paired.sem, paired.at(h + 1))
                            dve.wait_ge(decayed.sem, decayed.at(2 * h + 2))
                            pair = bank[4 + y][:, 0:4 * P].rearrange("p (a x c) -> p a x c", a=2, x=2)
                            dve.tensor_tensor(LT[:, 2 * h:2 * h + 2, :], pair[:, 0, :, :], decay[:, y, :, :],
                                              ALU.mult).then_inc(coupled.sem, 1)
                            dve.tensor_tensor(k[:, h, :].rearrange("p (x c) -> p x c", x=2), pair[:, 1, :, :],
                                              decay[:, y, :, :], ALU.mult).then_inc(coupled.sem, 1)
                            dve.tensor_tensor(q[:, h, C:2 * C], q[:, h, C:2 * C], eg[:, y, :],
                                              ALU.mult).then_inc(coupled.sem, 1)

                @block.scalar
                def _(act):
                    for i in range(H):
                        y = i % 2
                        act.wait_ge(arg_made.sem, arg_made.at(2 * i + 2))
                        if i >= 2:
                            act.wait_ge(coupled.sem, coupled.at(3 * (i - 1)))
                        act.activation(decay[:, y, :, :], decay[:, y, :, :], ACT.Exp).then_inc(decayed.sem, 1)
                        act.activation(eg[:, y, :], bank[y][:, C:2 * C], ACT.Exp).then_inc(decayed.sem, 1)
                        act.wait_ge(kdec_made.sem, kdec_made.at(i + 1))
                        act.activation(kbe[:, i, :], bank[2 + y][:, P:2 * P], ACT.Copy,
                                       scale=tok[:, 1, BE + i:BE + i + 1]).then_inc(taken.sem, 1)
                        for x in range(2):
                            act.activation(v[:, i, x * C:(x + 1) * C], bank[2 + y][:, (2 + x) * P:(3 + x) * P], ACT.Copy,
                                           scale=tok[:, x, B + i:B + i + 1]).then_inc(taken.sem, 1)
            for s, n in ((spread, H), (turned, H), (kb_made, H), (arg_made, 2 * H), (decayed, 2 * H), (paired, H),
                         (kdec_made, H), (coupled, 3 * H), (taken, 3 * H)):
                s.passed(n)

        with ExitStack() as inner:
            T = sbuf(inner, "inverse", [P, 2 * H, C])
            Lo = sbuf(inner, "coupling_level", [P, 2 * H, C])
            LoT = sbuf(inner, "lo_t", [P, 2 * H, C // 2])
            masked, lo_t, lo_t_out = sig("level_masked"), sig("lo_t_done"), sig("lo_t_out")
            delta, updated, t_turned, tt_out = sig("delta_done"), sig("t_updated"), sig("t_turned"), sig("tt_out")
            groups, levels = 4, 7
            with nc.Block() as block:
                @block.gpsimd
                def _(pool):
                    for l in range(levels):
                        for g in range(groups):
                            if l == 1:
                                pool.wait_ge(updated.sem, updated.at(g + 1))
                            elif l:
                                pool.wait_ge(lo_t.sem, lo_t.at((l - 2) * groups + g + 1))
                            u = slice(4 * g, 4 * g + 4)
                            pool.tensor_tensor(Lo[:, u, :], LT[:, u, :],
                                               con("levels", l * P, P).unsqueeze(1).broadcast_to([P, 4, P]),
                                               ALU.mult).then_inc(masked.sem, 1)

                @block.vector
                def _(dve):
                    for g in range(groups):
                        u = slice(4 * g, 4 * g + 4)
                        dve.wait_ge(masked.sem, masked.at(g + 1))
                        dve.tensor_tensor(TT[:, u, :], ident.unsqueeze(1).broadcast_to([P, 4, P]), Lo[:, u, :],
                                          ALU.subtract).then_inc(updated.sem, 1)
                    for l in range(1, levels):
                        s = 1 << l
                        for g in range(groups):
                            dve.wait_ge(delta.sem, delta.at((l - 1) * groups + g + 1))
                            left = T[:, 4 * g:4 * g + 4, :].rearrange("p u (b two s) -> p (u b) two s", two=2, s=s)
                            dve.tensor_tensor(left[:, :, 0, :], left[:, :, 0, :],
                                              bank[4 + g][:, 0:2 * P].rearrange("p (b s) -> p b s", s=s),
                                              ALU.subtract).then_inc(updated.sem, 1)

                @block.tensor
                def _(pe):
                    for g in range(groups):
                        pe.wait_ge(updated.sem, updated.at(g + 1))
                        for u in range(4):
                            last = pe.transpose(bank[g][:, u * P:(u + 1) * P], TT[:, 4 * g + u, :], ident)
                        last.then_inc(t_turned.sem, 1)
                    for l in range(1, levels):
                        s = 1 << l
                        for g in range(groups):
                            pe.wait_ge(masked.sem, masked.at(l * groups + g + 1))
                            pe.wait_ge(tt_out.sem, tt_out.at((l - 1) * groups + g + 1))
                            for u in range(4):
                                left = T[:, 4 * g + u, :].rearrange("p (b two s) -> p b two s", two=2, s=s)[:, :, 0, :]
                                last = pe.matmul(bank[g][:, u * 64:(u + 1) * 64], Lo[:, 4 * g + u, :], left,
                                                 start=True, stop=True)
                            last.then_inc(lo_t.sem, 1)
                        for g in range(groups):
                            pe.wait_ge(lo_t_out.sem, lo_t_out.at((l - 1) * groups + g + 1))
                            pe.wait_ge(updated.sem, updated.at((l - 1) * groups + g + 1))
                            for u in range(4):
                                last = pe.matmul(bank[4 + g][:, u * 64:(u + 1) * 64], TT[:, 4 * g + u, :],
                                                 LoT[:, 4 * g + u, :], start=True, stop=True)
                            last.then_inc(delta.sem, 1)
                        for g in range(groups):
                            pe.wait_ge(updated.sem, updated.at(l * groups + g + 1))
                            for u in range(4):
                                last = pe.transpose(bank[g][:, u * P:(u + 1) * P], T[:, 4 * g + u, :], ident)
                            last.then_inc(t_turned.sem, 1)

                @block.scalar
                def _(act):
                    for g in range(groups):
                        act.wait_ge(t_turned.sem, t_turned.at(g + 1))
                        act.activation(T[:, 4 * g:4 * g + 4, :], bank[g][:, 0:4 * P].rearrange("p (u c) -> p u c", u=4),
                                       ACT.Copy).then_inc(tt_out.sem, 1)
                    for l in range(1, levels):
                        for g in range(groups):
                            act.wait_ge(lo_t.sem, lo_t.at((l - 1) * groups + g + 1))
                            act.activation(LoT[:, 4 * g:4 * g + 4, :],
                                           bank[g][:, 0:2 * P].rearrange("p (u c) -> p u c", u=4),
                                           ACT.Copy).then_inc(lo_t_out.sem, 1)
                        for g in range(groups):
                            act.wait_ge(t_turned.sem, t_turned.at(l * groups + g + 1))
                            act.activation(TT[:, 4 * g:4 * g + 4, :],
                                           bank[g][:, 0:4 * P].rearrange("p (u c) -> p u c", u=4),
                                           ACT.Copy).then_inc(tt_out.sem, 1)
            for s in (masked, updated, t_turned, tt_out):
                s.passed(levels * groups)
            for s in (lo_t, lo_t_out, delta):
                s.passed((levels - 1) * groups)

        with ExitStack() as inner:
            vn0, vn1, S1, wT = (sbuf(inner, n, [P, H, P]) for n in ("v_new0", "v_new1", "state1", "neg_w_T"))
            r1, r1_out, r2, r2_out, r3, r3_out, r4, r4_out = (
                sig(n) for n in ("u0_w1", "u0_w1_out", "state_done", "state_out", "v1_done", "v1_out", "o_done", "o_out"))
            with nc.Block() as block:
                @block.tensor
                def _(pe):
                    for i in range(H + 3):
                        if i < H:
                            y = i % 2
                            if i >= 2:
                                pe.wait_ge(r1_out.sem, r1_out.at(2 * (i - 1)))
                            pe.matmul(bank[y][:, 0:P], TT[:, 2 * i, :], v[:, i, 0:C], start=True, stop=True)
                            pe.matmul(bank[y][:, P:2 * P], kbe[:, i, :], TT[:, 2 * i + 1, :], start=True,
                                      stop=True).then_inc(r1.sem, 1)
                        if 1 <= i <= H:
                            h, y = i - 1, (i - 1) % 2
                            pe.wait_ge(r1_out.sem, r1_out.at(2 * h + 2))
                            if h >= 2:
                                pe.wait_ge(r2_out.sem, r2_out.at(h - 1))
                            pe.matmul(bank[2 + y][:, 0:P], kdec[:, h, :], vn0[:, h, :], start=True,
                                      stop=True).then_inc(r2.sem, 1)
                        if 2 <= i <= H + 1:
                            h, y = i - 2, i % 2
                            pe.wait_ge(r2_out.sem, r2_out.at(h + 1))
                            if h >= 2:
                                pe.wait_ge(r3_out.sem, r3_out.at(h - 1))
                            pe.matmul(bank[4 + y][:, 0:P], TT[:, 2 * h + 1, :], v[:, h, C:2 * C], start=True, stop=False)
                            pe.matmul(bank[4 + y][:, 0:P], wT[:, h, :], S1[:, h, :], start=False,
                                      stop=True).then_inc(r3.sem, 1)
                        if i >= 3:
                            h, y = i - 3, (i - 3) % 2
                            pe.wait_ge(r3_out.sem, r3_out.at(h + 1))
                            if h >= 2:
                                pe.wait_ge(r4_out.sem, r4_out.at(h - 1))
                            pe.matmul(bank[6 + y][:, 0:C], vn0[:, h, :], k[:, h, 0:C], start=True, stop=True)
                            pe.matmul(bank[6 + y][:, C:2 * C], S1[:, h, :], q[:, h, C:2 * C], start=True, stop=False)
                            pe.matmul(bank[6 + y][:, C:2 * C], vn1[:, h, :], k[:, h, C:2 * C], start=False,
                                      stop=True).then_inc(r4.sem, 1)

                @block.scalar
                def _(act):
                    for i in range(H + 3):
                        if i < H:
                            act.wait_ge(r1.sem, r1.at(i + 1))
                            act.activation(vn0[:, i, :], bank[i % 2][:, 0:P], ACT.Copy).then_inc(r1_out.sem, 1)
                            act.activation(wT[:, i, :], bank[i % 2][:, P:2 * P], ACT.Copy,
                                           scale=-1.0).then_inc(r1_out.sem, 1)
                        if 1 <= i <= H:
                            act.wait_ge(r2.sem, r2.at(i))
                            act.activation(S1[:, i - 1, :], bank[2 + (i - 1) % 2][:, 0:P],
                                           ACT.Copy).then_inc(r2_out.sem, 1)

                @block.vector
                def _(dve):
                    for i in range(2, H + 3):
                        if i <= H + 1:
                            h = i - 2
                            dve.wait_ge(r3.sem, r3.at(h + 1))
                            dve.tensor_copy(vn1[:, h, :], bank[4 + h % 2][:, 0:P]).then_inc(r3_out.sem, 1)
                        if i >= 3:
                            h = i - 3
                            dve.wait_ge(r4.sem, r4.at(h + 1))
                            dve.tensor_copy(q[:, h, :], bank[6 + h % 2][:, 0:2 * C]).then_inc(r4_out.sem, 1)
            for s, n in ((r1, H), (r1_out, 2 * H), (r2, H), (r2_out, H), (r3, H), (r3_out, H), (r4, H), (r4_out, H)):
                s.passed(n)


def rope_angles(nc, sbuf, sig, sin_cos, pos_d, con):
    import math
    pos_in, step = sig("pos_in"), sig("angle_step")
    two_pi_hi = 6.28125
    two_pi_lo = 2 * math.pi - two_pi_hi
    rounder = 1.5 * 2.0 ** 23
    top = 3.1415925
    with ExitStack() as scope:
        pos = sbuf(scope, "positions", [P, SEQ], mybir.dt.int32)
        a = sbuf(scope, "angles", [P, 4, SEQ])
        with nc.Block() as block:
            @block.sync
            def _(sp):
                sp.dma_start(pos[:, :], pos_d).then_inc(pos_in.sem, 16)

            @block.vector
            def _(dve):
                count = [0]

                def then(ins):
                    count[0] += 1
                    ins.then_inc(step.sem, 1)
                    dve.wait_ge(step.sem, step.at(count[0]))
                dve.wait_ge(pos_in.sem, pos_in.at(16))
                ang, turns, s, c = (a[:, i, :] for i in range(4))
                then(dve.tensor_copy(ang, pos[:, :]))
                then(dve.tensor_scalar(ang, ang, con("inv_freq"), None, ALU.mult))
                then(dve.tensor_scalar(turns, ang, 1 / (2 * math.pi), rounder, ALU.mult, ALU.add))
                then(dve.tensor_scalar(turns, turns, rounder, None, ALU.subtract))
                then(dve.scalar_tensor_tensor(ang, turns, -two_pi_hi, ang, ALU.mult, ALU.add))
                then(dve.scalar_tensor_tensor(ang, turns, -two_pi_lo, ang, ALU.mult, ALU.add))
                then(dve.tensor_scalar(s, ang, top, -top, ALU.min, ALU.max))
                then(dve.tensor_scalar(c, ang, math.pi / 2, None, ALU.add))
                then(dve.tensor_scalar(turns, c, top, -2 * math.pi, ALU.is_gt, ALU.mult))
                then(dve.tensor_tensor(c, c, turns, ALU.add))
                then(dve.tensor_scalar(c, c, top, -top, ALU.min, ALU.max))

            @block.scalar
            def _(act):
                act.wait_ge(step.sem, step.at(11))
                act.activation(sin_cos[:, 0, :], a[:, 2, :], ACT.Sin)
                act.activation(sin_cos[:, 1, :], a[:, 3, :], ACT.Sin)
        pos_in.passed(16)
        step.passed(11)


def rotate(nc, sbuf, sig, bank, parts, sin_cos, con):
    rotated, sined, cosined, summed = sig("rotated"), sig("sined"), sig("cosined"), sig("rope_summed")
    tiles = [(part, t) for part, n in parts for t in range(n)]
    with ExitStack() as scope:
        other = sbuf(scope, "rope_other", [P, len(tiles), SEQ])
        with nc.Block() as block:
            @block.tensor
            def _(pe):
                for i, (x, t) in enumerate(tiles):
                    pe.matmul(bank[i][:, 0:SEQ], con("rotate"), x[:, t, :], start=True, stop=True).then_inc(rotated.sem, 1)

            @block.vector
            def _(dve):
                for i, (x, t) in enumerate(tiles):
                    dve.wait_ge(rotated.sem, rotated.at(i + 1))
                    dve.tensor_tensor(other[:, i, :], bank[i][:, 0:SEQ], sin_cos[:, 0, :], ALU.mult).then_inc(sined.sem, 1)
                    dve.tensor_tensor(x[:, t, :], x[:, t, :], sin_cos[:, 1, :], ALU.mult).then_inc(cosined.sem, 1)
                    dve.wait_ge(sined.sem, sined.at(i + 1))
                    dve.wait_ge(cosined.sem, cosined.at(i + 1))
                    dve.tensor_tensor(x[:, t, :], x[:, t, :], other[:, i, :], ALU.add).then_inc(summed.sem, 1)
    for s in (rotated, sined, cosined, summed):
        s.passed(len(tiles))


def _blocks(w, k_tiles, tiles):
    import numpy as np
    k, n = w.shape
    full = np.zeros((k_tiles * P, -(-n // P) * P), np.float32)
    full[:k, :n] = w
    b = full.reshape(k_tiles, P, -1, P).transpose(2, 0, 1, 3)
    items = b.reshape(-1, tiles, k_tiles, P, P).transpose(0, 3, 1, 2, 4)
    return np.ascontiguousarray(items).reshape(items.shape[0], P, tiles * k_tiles * P)


def _halves(w):
    import numpy as np
    k, n = w.shape
    full = np.zeros((FF_TILES * P, n), np.float32)
    full[:k] = w
    b = full.reshape(2, HALF_FF, P, n // P, P).transpose(3, 0, 2, 1, 4)
    return np.ascontiguousarray(b).reshape(-1, P, HALF_FF * P)


def _pairs(a, b):
    import numpy as np
    n = FF_TILES * P
    fa, fb = np.zeros((D, n), np.float32), np.zeros((D, n), np.float32)
    fa[:, :a.shape[1]], fb[:, :b.shape[1]] = a, b
    both = np.stack([fa.reshape(D, FF_TILES, P), fb.reshape(D, FF_TILES, P)], axis=2)
    return _blocks(both.reshape(D, 2 * n), KD, 2)


def _cols(v):
    return v.reshape(-1, P).T


def _layout(x):
    import numpy as np
    d_ff = x["ffn_w_down"].shape[1]
    w = {}
    ada = np.concatenate([x["ada_w_2"][0], x["ada_w_2"][1]], axis=1)
    w["ada"] = np.ascontiguousarray(ada.T.reshape(MOD_ITEMS, 2, P, D).transpose(0, 2, 1, 3)).reshape(MOD_ITEMS, P, 2 * D)
    w["a_in"] = _blocks(x["a_w_in"][0], KD, 2)
    w["a_out"] = _blocks(x["a_w_out"][0], KD, 2)
    for l in range(2):
        w[f"up{l}"] = _pairs(x["ffn_w_up"][l][:, :d_ff], x["ffn_w_up"][l][:, d_ff:])
        w[f"down{l}"] = _halves(x["ffn_w_down"][l])
        w[f"gu{l}"] = _pairs(x["ffn_w_gate_2"][l], x["ffn_w_up_2"][l])
        w[f"dn{l}"] = _halves(x["ffn_w_down_2"][l])
    w["kv"] = _blocks(x["kv_w"][:, :2 * D], KD, 2)
    w["fg"] = _blocks(x["kv_w"][:, 2 * D:], KD, 1)
    w["b_q"] = _blocks(x["b_w_q"][0], KD, 2)
    w["b_out"] = _blocks(x["b_w_out"][0], KD, 2)
    gw = x["gdn_w_in_2"][0]
    w["gdn_qkv"] = _blocks(gw[:, :3 * D], KD, 2)
    w["gdn_gate"] = _blocks(gw[:, 3 * D:4 * D], KD, 2)
    ab = np.zeros((D, P), np.float32)
    ab[:, 0:HEADS], ab[:, 32:32 + HEADS] = gw[:, 4 * D:4 * D + HEADS], gw[:, 4 * D + HEADS:]
    w["gdn_ab"] = _blocks(ab, KD, 1)
    w["gdn_out"] = _blocks(x["gdn_w_out_2"][0], KD, 2)
    mi = x["mla_w_in_2"][0]
    w["mla_in"] = _blocks(np.concatenate([mi, mi[:, 640:704]], axis=1), KD, 2)
    uq = x["mla_w_uq_2"][0].reshape(384, HEADS, 192)
    w["uq"] = _blocks(np.concatenate([uq[:, :, :128].reshape(384, -1), uq[:, :, 128:].reshape(384, -1)], axis=1), 3, 4)
    ukv = x["mla_w_ukv_2"][0].reshape(256, HEADS, 256)
    w["ukv"] = _blocks(np.concatenate([ukv[:, :, :128].reshape(256, -1), ukv[:, :, 128:].reshape(256, -1)], axis=1), 2, 4)
    w["mla_out"] = _blocks(x["mla_w_out_2"][0], KD, 2)

    params = np.zeros((P, NPARAM), np.float32)

    def put(name, v, at=0):
        params[:v.shape[0], PCOL[name] + at:PCOL[name] + at + v.shape[1]] = v
    for l in range(2):
        for i in range(4):
            put("gains", _cols(x["norm_gains"][l, i]), (4 * l + i) * KD)
        for t in range(3):
            for half in range(2):
                v = np.zeros(FF_TILES * P, np.float32)
                v[:d_ff] = x["ffn_conv"][l, t, half * d_ff:(half + 1) * d_ff]
                put("conv", _cols(v), ((l * 3 + t) * 2 + half) * FF_TILES)
        put("norm_mix", _cols(x["norm_mix_g_2"][l]), l * KD)
        put("norm_ffn", _cols(x["norm_ffn_g_2"][l]), l * KD)
        put("ada_b", _cols(x["ada_b_2"][l]), l * 6 * KD)
        put("lb", _cols(x["a_lb_logits"][l]), l * KD)
    put("kv_norm", _cols(x["kv_norm"]))
    put("head_norm", _cols(x["a_head_norm"][0]))
    put("fg_b", x["fg_b"].reshape(-1, 1))
    put("final", _cols(x["final_norm_g_2"]))
    put("gdn_conv", x["gdn_conv_w_2"][0].reshape(3 * HEADS, P, 4).transpose(1, 0, 2).reshape(P, -1))
    put("gdn_norm", _cols(x["gdn_norm_g_2"][0]))
    put("q_norm", _cols(x["mla_q_norm_g_2"][0]))
    put("kv_norm2", _cols(x["mla_kv_norm_g_2"][0]))
    put("a_log", x["gdn_a_log_2"][0].reshape(-1, 1))
    put("dt_bias", x["gdn_dt_bias_2"][0].reshape(-1, 1))

    tokens = np.concatenate([x["meta_tokens"], x["x"][0]], axis=0)
    hT = np.ascontiguousarray(tokens.T.reshape(KD, P, T1).transpose(1, 0, 2))
    pos = np.ascontiguousarray(np.broadcast_to(x["positions_2"].astype(np.int32), (P, SEQ)))
    c = np.ascontiguousarray(np.broadcast_to(x["c_2"], (P, D)))
    return w, params, hT, c, pos


def _constants():
    import numpy as np
    c = np.zeros((P, NCONST), np.float32)

    def put(name, v):
        c[:, CCOL[name]:CCOL[name] + dict(CONSTS)[name]] = v
    row, col = np.arange(P)[:, None], np.arange(P)[None, :]
    put("ident", np.eye(P))
    put("ones", 1.0)
    put("causal_qk", np.where(col <= row, 0.0, NEG))
    put("causal_kq", np.where(row <= col, 0.0, NEG))
    put("chunk_kq", (row <= col) & (row // 64 == col // 64))
    levels = [(row // (2 * s) == col // (2 * s)) & (row % (2 * s) < s) & (col % (2 * s) >= s)
              for s in (1, 2, 4, 8, 16, 32, 64)]
    put("levels", np.concatenate(levels, axis=1))
    put("rotate", np.where((col % 64 < 32) & (row == col + 32), -1.0, np.where((col % 64 >= 32) & (row == col - 32), 1.0, 0.0)))
    t = np.arange(T1)
    put("reset_hgrn", np.broadcast_to((t != 0) & ((t < META) | ((t - META) % 64 != 0)), (P, T1)))
    t = np.arange(SEQ)
    put("reset_gdn", np.broadcast_to(t % P != 0, (P, SEQ)))
    put("ones_row", 1.0)
    exponent = (np.arange(P) % 32 * 2).astype(np.float64) / 64
    put("inv_freq", (10000.0 ** -exponent)[:, None])
    return c


def kernel(**inputs):
    import numpy as _np
    import concourse.bacc as _bacc
    from concourse.bass_utils import run_bass_kernel_spmd as _run

    nc = _bacc.Bacc("TRN2", target_bir_lowering=False, num_devices=1)
    w, params, hT, c, pos = _layout({k: _np.asarray(v) for k, v in inputs.items()})
    arrays = {f"w_{name}": a for name, a in w.items()}
    arrays |= {"params": params, "consts": _constants(), "hT": hT, "c": c, "pos": pos}
    aps = {n: nc.dram_tensor(n, a.shape, mybir.dt.from_np(a.dtype), kind="ExternalInput").ap()
           for n, a in arrays.items()}
    out = nc.dram_tensor("out", (P, KD, SEQ), F32, kind="ExternalOutput").ap()
    fused_model(nc, {name: aps[f"w_{name}"] for name in w}, aps["params"], aps["consts"], aps["hT"], aps["c"], aps["pos"], out)
    r = _run(nc, [arrays], core_ids=[0])
    got = r.results[0]["out"]
    return _np.ascontiguousarray(got.transpose(2, 1, 0).reshape(1, SEQ, D))
```
